# Optimizing a Trainium2 kernel written in Bass

```python
import math
import jax, jax.numpy as jnp
from jax import lax
import numpy as np

D_MODEL = 1024
BATCH = 1
SEQ = 512
DEPTH = 2

GRID_W = 64
GLA_HEADS = 4
GLA_DK = 64
GLA_DV = 128
GLA_RANK = 16
GLA_TAU = 16.0
GLA_CHUNK = 64
NA_HEADS = 8
NA_DH = 64
WIN_H = 8
WIN_W = 16
Q_BLOCK_W = 16
K_BLOCK_W = 32
N_EXPERTS = 32
N_GROUPS = 4
EXPERTS_PER_GROUP = N_EXPERTS // N_GROUPS
TOP_K = 2
D_EXPERT = 512
MOE_BLOCK = 128
GLA_QK_W = GLA_HEADS * GLA_DK
GLA_V_W = GLA_HEADS * GLA_DV
NA_W = NA_HEADS * NA_DH
MIX_W = GLA_V_W + NA_W
IN_W = 2 * GLA_QK_W + 2 * GLA_V_W + 2 * GLA_RANK + 3 * NA_W
EPS = 1e-6
NEG = -1e30

kernel_name = "hybrid_gla_natten_grouped_moe_encoder"

def _split_points():
    widths = [GLA_QK_W, GLA_QK_W, GLA_V_W, GLA_V_W, GLA_RANK, GLA_RANK, NA_W, NA_W, NA_W]
    pts, acc = [], 0
    for w in widths[:-1]:
        acc += w
        pts.append(acc)
    return pts

def rms_norm(x, g):
    xf = x.astype(jnp.float32)
    y = xf * lax.rsqrt(jnp.mean(xf * xf, axis=-1, keepdims=True) + EPS)
    return (y * g.astype(jnp.float32)).astype(x.dtype)

def _heads(t, n):
    b, s, _ = t.shape
    return t.reshape(b, s, n, -1).transpose(0, 2, 1, 3)

def gla_scan(q, k, v, log_a, strict):
    B, H, T, dk = q.shape
    dv = v.shape[-1]
    C = GLA_CHUNK
    nc = T // C

    def chunks(t):
        return jnp.moveaxis(t.reshape(B, H, nc, C, t.shape[-1]), 2, 0)

    qc, kc, vc, ac = chunks(q), chunks(k), chunks(v), chunks(log_a)
    bc = jnp.cumsum(ac, axis=-2)
    mask = jnp.tril(jnp.ones((C, C), dtype=bool), -1 if strict else 0)

    def step(S, inp):
        q_, k_, v_, b_ = inp
        diff = b_[:, :, :, None, :] - b_[:, :, None, :, :]
        decay = jnp.exp(jnp.where(mask[:, :, None], diff, -jnp.inf))
        scores = jnp.sum(q_[:, :, :, None, :] * k_[:, :, None, :, :] * decay, axis=-1)
        o = (jnp.einsum('bhij,bhje->bhie', scores, v_)
             + jnp.einsum('bhid,bhde->bhie', q_ * jnp.exp(b_), S))
        b_last = b_[:, :, -1:, :]
        S_new = (jnp.exp(b_last[:, :, 0, :])[..., None] * S
                 + jnp.einsum('bhjd,bhje->bhde', k_ * jnp.exp(b_last - b_), v_))
        return S_new, o

    S0 = jnp.zeros((B, H, dk, dv), jnp.float32)
    _, o = lax.scan(step, S0, (qc, kc, vc, bc))
    return jnp.moveaxis(o, 0, 2).reshape(B, H, T, dv)

def _na_indices(rows):
    kh = min(WIN_H, rows)
    r = np.arange(rows)
    row_start = np.clip(r - kh // 2, 0, rows - kh)
    key_rows = row_start[:, None] + np.arange(kh)
    n_cb = GRID_W // Q_BLOCK_W
    q_cols = np.arange(n_cb)[:, None] * Q_BLOCK_W + np.arange(Q_BLOCK_W)
    col_start = np.clip(q_cols - WIN_W // 2, 0, GRID_W - WIN_W)
    blk_start = np.clip(np.arange(n_cb) * Q_BLOCK_W - WIN_W // 2, 0, GRID_W - K_BLOCK_W)
    key_cols = blk_start[:, None] + np.arange(K_BLOCK_W)
    col_ok = ((key_cols[:, None, :] >= col_start[:, :, None])
              & (key_cols[:, None, :] < col_start[:, :, None] + WIN_W))
    L = kh * K_BLOCK_W
    tok = (key_rows[:, None, :, None] * GRID_W + key_cols[None, :, None, :]).reshape(rows, n_cb, L)
    mask = np.broadcast_to(col_ok[:, :, None, :], (n_cb, Q_BLOCK_W, kh, K_BLOCK_W)).reshape(n_cb, Q_BLOCK_W, L)
    rel_r = key_rows - r[:, None] + WIN_H - 1
    rel_c = np.clip(key_cols[:, None, :] - q_cols[:, :, None] + WIN_W - 1, 0, 2 * WIN_W - 2)
    full = (rows, n_cb, Q_BLOCK_W, kh, K_BLOCK_W)
    ri = np.broadcast_to(rel_r[:, None, None, :, None], full).reshape(rows, n_cb, Q_BLOCK_W, L)
    ci = np.broadcast_to(rel_c[None, :, :, None, :], full).reshape(rows, n_cb, Q_BLOCK_W, L)
    return tok, mask, ri, ci

def neighborhood_attention(q, k, v, rpb):
    B, H, T, dh = q.shape
    rows = T // GRID_W
    tok, mask, ri, ci = _na_indices(rows)
    n_cb = GRID_W // Q_BLOCK_W
    qb = q.reshape(B, H, rows, n_cb, Q_BLOCK_W, dh)
    kg = k[:, :, tok]
    vg = v[:, :, tok]
    s = jnp.einsum('bhrnqd,bhrnkd->bhrnqk', qb, kg).astype(jnp.float32) * (dh ** -0.5)
    bias = rpb.astype(jnp.float32)[:, ri, ci]
    s = jnp.where(mask[None, None, None], s + bias[None], NEG)
    p = jax.nn.softmax(s, axis=-1)
    o = jnp.einsum('bhrnqk,bhrnkd->bhrnqd', p.astype(v.dtype), vg)
    return o.reshape(B, H, T, dh)

def mixer(h, w_in, gate_w, gate_b, gla_norm, q_norm, k_norm, rpb, w_out):
    B, T, _ = h.shape
    f32 = jnp.float32
    proj = h @ w_in
    qg, kg, vg, gg, lf, lb, qn, kn, vn = jnp.split(proj, _split_points(), axis=-1)
    q = _heads(qg, GLA_HEADS).astype(f32) * (GLA_DK ** -0.5)
    k = _heads(kg, GLA_HEADS).astype(f32)
    v = _heads(vg, GLA_HEADS).astype(f32)
    la_f = _heads(jax.nn.log_sigmoid((lf @ gate_w[0] + gate_b[0]).astype(f32)) / GLA_TAU, GLA_HEADS)
    la_b = _heads(jax.nn.log_sigmoid((lb @ gate_w[1] + gate_b[1]).astype(f32)) / GLA_TAU, GLA_HEADS)
    o_f = gla_scan(q, k, v, la_f, False)
    flip = lambda t: jnp.flip(t, axis=2)
    o_b = flip(gla_scan(flip(q), flip(k), flip(v), flip(la_b), True))
    o_gla = rms_norm(o_f + o_b, gla_norm)
    o_gla = o_gla.transpose(0, 2, 1, 3).reshape(B, T, GLA_V_W) * jax.nn.silu(gg.astype(f32))
    qh = rms_norm(_heads(qn, NA_HEADS), q_norm)
    kh = rms_norm(_heads(kn, NA_HEADS), k_norm)
    vh = _heads(vn, NA_HEADS)
    o_na = neighborhood_attention(qh, kh, vh, rpb).transpose(0, 2, 1, 3).reshape(B, T, NA_W)
    cat = jnp.concatenate([o_gla.astype(h.dtype), o_na.astype(h.dtype)], axis=-1)
    return cat @ w_out

def grouped_moe(h, router_w, router_b, w1, w3, w2):
    N, D = h.shape
    f32 = jnp.float32
    scores = jax.nn.sigmoid(h.astype(f32) @ router_w.astype(f32))
    sel = scores + router_b.astype(f32)
    grp = sel.reshape(N, N_GROUPS, EXPERTS_PER_GROUP)
    group_score = lax.top_k(grp, TOP_K)[0].sum(-1)
    best = jnp.argmax(group_score, axis=-1)
    in_grp = jnp.take_along_axis(grp, best[:, None, None], axis=1)[:, 0]
    _, local = lax.top_k(in_grp, TOP_K)
    eidx = best[:, None] * EXPERTS_PER_GROUP + local
    gw = jnp.take_along_axis(scores, eidx, axis=1)
    gw = gw / jnp.sum(gw, axis=-1, keepdims=True)
    M = N * TOP_K
    flat_e = eidx.reshape(-1)
    flat_tok = jnp.repeat(jnp.arange(N, dtype=jnp.int32), TOP_K)
    order = jnp.argsort(flat_e)
    sorted_e = flat_e[order]
    sorted_tok = flat_tok[order]
    sorted_w = gw.reshape(-1)[order]
    counts = jnp.bincount(flat_e, length=N_EXPERTS)
    padded = (counts + MOE_BLOCK - 1) // MOE_BLOCK * MOE_BLOCK
    pad_end = jnp.cumsum(padded)
    pad_start = pad_end - padded
    start = jnp.cumsum(counts) - counts
    dest = pad_start[sorted_e] + (jnp.arange(M) - start[sorted_e])
    P = (-(-M // MOE_BLOCK) + N_EXPERTS) * MOE_BLOCK
    NB = P // MOE_BLOCK
    buf_tok = jnp.full((P,), N, jnp.int32).at[dest].set(sorted_tok)
    h_pad = jnp.concatenate([h, jnp.zeros((1, D), h.dtype)], axis=0)
    xb = h_pad[buf_tok].reshape(NB, MOE_BLOCK, D)
    blk_e = jnp.minimum(jnp.searchsorted(pad_end, jnp.arange(NB) * MOE_BLOCK, side='right'), N_EXPERTS - 1)

    def expert_block(args):
        xblk, e = args
        return (jax.nn.silu(xblk @ w1[e]) * (xblk @ w3[e])) @ w2[e]

    y = lax.map(expert_block, (xb, blk_e)).reshape(P, D)
    y_assign = y[dest].astype(f32) * sorted_w[:, None]
    out = jax.ops.segment_sum(y_assign, sorted_tok, num_segments=N)
    return out.astype(h.dtype)

def setup_inputs(seed: int = 0) -> dict:
    key = jax.random.key(seed)
    ks = jax.random.split(key, 20)
    nrm = lambda k, s: jax.random.normal(k, s, jnp.float32)
    D = D_MODEL
    return {
        "x": nrm(ks[0], (BATCH, SEQ, D)),
        "c": nrm(ks[1], (BATCH, D)),
        "w_ada": nrm(ks[2], (DEPTH, D, 6 * D)) * (0.5 * D ** -0.5),
        "b_ada": nrm(ks[3], (DEPTH, 6 * D)) * 0.02,
        "attn_norm": 1.0 + 0.05 * nrm(ks[4], (DEPTH, D)),
        "ffn_norm": 1.0 + 0.05 * nrm(ks[5], (DEPTH, D)),
        "w_in": nrm(ks[6], (DEPTH, D, IN_W)) * D ** -0.5,
        "gla_gate_w": nrm(ks[7], (DEPTH, 2, GLA_RANK, GLA_QK_W)) * GLA_RANK ** -0.5,
        "gla_gate_b": 0.1 * nrm(ks[8], (DEPTH, 2, GLA_QK_W)),
        "gla_out_norm": 1.0 + 0.05 * nrm(ks[9], (DEPTH, GLA_DV)),
        "na_q_norm": 1.0 + 0.05 * nrm(ks[10], (DEPTH, NA_DH)),
        "na_k_norm": 1.0 + 0.05 * nrm(ks[11], (DEPTH, NA_DH)),
        "na_rpb": 0.02 * nrm(ks[12], (DEPTH, NA_HEADS, 2 * WIN_H - 1, 2 * WIN_W - 1)),
        "w_out": nrm(ks[13], (DEPTH, MIX_W, D)) * MIX_W ** -0.5,
        "router_w": nrm(ks[14], (D, N_EXPERTS)) * D ** -0.5,
        "router_b": 0.01 * nrm(ks[15], (N_EXPERTS,)),
        "w1": nrm(ks[16], (DEPTH, N_EXPERTS, D, D_EXPERT)) * D ** -0.5,
        "w3": nrm(ks[17], (DEPTH, N_EXPERTS, D, D_EXPERT)) * D ** -0.5,
        "w2": nrm(ks[18], (DEPTH, N_EXPERTS, D_EXPERT, D)) * D_EXPERT ** -0.5,
    }

def reference(x, c, w_ada, b_ada, attn_norm, ffn_norm, w_in, gla_gate_w, gla_gate_b,
              gla_out_norm, na_q_norm, na_k_norm, na_rpb, w_out, router_w, router_b,
              w1, w3, w2):
    B, T, D = x.shape
    c_act = jax.nn.silu(c)
    for l in range(DEPTH):
        mod = c_act @ w_ada[l] + b_ada[l]
        sh1, sc1, g1, sh2, sc2, g2 = jnp.split(mod, 6, axis=-1)
        h = rms_norm(x, attn_norm[l]) * (1.0 + sc1[:, None]) + sh1[:, None]
        x = x + g1[:, None] * mixer(h, w_in[l], gla_gate_w[l], gla_gate_b[l], gla_out_norm[l],
                                    na_q_norm[l], na_k_norm[l], na_rpb[l], w_out[l])
        h = rms_norm(x, ffn_norm[l]) * (1.0 + sc2[:, None]) + sh2[:, None]
        y = grouped_moe(h.reshape(B * T, D), router_w, router_b, w1[l], w3[l], w2[l])
        x = x + g2[:, None] * y.reshape(B, T, D)
    return x


_drawn_inputs = setup_inputs


def setup_inputs(seed=0):
    import zlib

    import numpy as np

    out = dict(_drawn_inputs(seed))
    spreads = {}
    factors = {'na_q_norm': 8.0, 'na_k_norm': 4.388, 'na_rpb': 8.0}
    for name, (base, spread) in spreads.items():
        noise = np.random.default_rng([zlib.crc32(name.encode()), seed]).standard_normal(out[name].shape)
        drawn = base * np.exp(spread * noise) if base else spread * noise
        out[name] = __import__('jax').numpy.asarray(drawn.astype(out[name].dtype))
    for name, factor in factors.items():
        out[name] = (out[name] * factor).astype(out[name].dtype)
    return out
```

```python
from contextlib import ExitStack

import concourse.bass as bass
from concourse import mybir

F32 = mybir.dt.float32
I32 = mybir.dt.int32
ALU = mybir.AluOpType
ACT = mybir.ActivationFunctionType
AX = mybir.AxisListType.X

P = 128
T = 512
D = 1024
L = 2
KD = D // P
TT = T // P
ROWS, COLS = 8, 64
NE, NG, EG = 32, 4, 8
DE = 512
SLOTS = 64
MAXOV = 2 * T // SLOTS
NBLK = NE + MAXOV
EPS = 1e-6
NEG = -1e30
TAU_INV = 1.0 / 16.0
C_QK, C_V, C_G, C_LF, C_QN, C_KN, C_VN = 0, 512, 1024, 1536, 1568, 2080, 2592
IN_W = 3104
RPB_W = 15 * 31
RPB_PAD = 16
KEY_AT = [0, 1, 3, 4]
RPB_OFF = [0, -8, -8, -16]
MASK_OF = [0, 1, 1, 2]
LEVELS = [6, 5, 4, 3, 2, 1, 0]
RING = 6
NPAR = 19
ADA_PIECES = 24
WIN_PIECES = 12
DVE_STEPS, ACT_STEPS, POOL_STEPS = 257, 18, 0



class Signal:

    def __init__(self, nc, ctx, name, per, first=0):
        self.s = ctx.enter_context(nc.semaphore(name))
        self.per, self.first = per, first

    def at(self, l, n):
        return l * self.per + self.first + n


def tile_plan():
    t = [(("x", 1, tt, h), "ad"[h]) for tt in range(TT) for h in range(2)]
    t += [(("q", d), "a") for d in range(2)] + [(("ada", 0), "d"), (("ada", 0, 1), "d")]
    t += [(("k", d), "a") for d in range(2)] + [(("lf",), "a"), (("ada", 1), "d")]
    t += [(("v", 0, c), "a") for c in range(TT)] + [(("ada", 2), "d")]
    t += [(("v", 1, c), "a") for c in range(TT)] + [(("ada", 3), "d"), (("ada", 3, 1), "d")]
    t += [(("g", h), "d") for h in range(4)]
    t += [(("z", c), "d") for c in range(TT)]
    t += [(("b", r, d), "a") for r in range(2) for d in range(2)]
    for c in range(TT):
        t += [(("kx", c), "a"), (("kt", c), "d")]
    t += [(("U", 0, c), "d") for c in (0, 1, 2)] + [(("U", 1, c), "d") for c in (3, 2, 1)]
    t += [(("P", 7, c), "a") for c in range(TT)]
    fill = [[("kn", 0)], [("kms", 0), ("kn", 1)], [("kms", 1), ("kn", 2)], [("kms", 2), ("kn", 3)],
            [("kms", 3), ("vf", 0)], [("vf", 1), ("vt", 0, 0), ("vt", 0, 1)],
            [("vf", 2), ("vt", 1, 0), ("vt", 1, 1), ("vf", 3), ("vt", 2, 0), ("vt", 2, 1), ("vt", 3, 0), ("vt", 3, 1)]]
    who = {"kn": "d", "kms": "a", "vf": "a", "vt": "a"}
    for n, lev in enumerate(LEVELS):
        t += [(("P", lev, c), "d") for c in range(TT)]
        t += [(k, who[k[0]]) for k in fill[n]]
    for pre in ("qn", "o"):
        ms = pre[0] + "ms"
        t += [((pre, 0), "d"), ((pre, 1), "d"), ((ms, 0), "a")]
        t += [(("ada", 4), "d")] if pre == "qn" else []
        t += [((pre, 2), "d"), ((ms, 1), "a"), ((pre, 3), "d"), ((ms, 2), "a"), ((ms, 3), "a")]
        t += [(("ada", 5), "d")] if pre == "qn" else []
    for h in range(9):
        if h < 8:
            t += [(("S", h, i), "d") for i in range(2)]
        if 1 <= h < 9:
            t += [(("PT", h - 1, i), "a") for i in range(2)]
    t += [(("y", m, tt), "d") for m in range(4) for tt in range(TT)]
    t += [(("x", 2, tt, h), "ad"[h]) for tt in range(TT) for h in range(2)]
    t += [(("logits",), "d"), (("rank",), "d"), (("over",), "d"), (("slot",), "d")]
    return t


def build(nc, A):
    plan = tile_plan()
    index = {key: n for n, (key, _) in enumerate(plan)}
    taken, seen = {}, {"a": 0, "d": 0}
    mean_of = {"kn": "kms", "qn": "qms", "o": "oms"}
    order = sorted(plan, key=lambda e: index[(mean_of[e[0][0]], e[0][1])] + 0.5 if e[0][0] in mean_of else index[e[0]])
    for key, who in order:
        seen[who] += 1
        taken[key] = (who, seen[who])

    with ExitStack() as ctx:
        def sb(name, shape, dt=F32):
            return ctx.enter_context(nc.sbuf_tensor(name, shape, dt))

        def sig(name, per, first=0):
            return Signal(nc, ctx, name, per, first)

        ring = sb("ring", [P, 6, 4096])
        x_sb = sb("x_sb", [P, TT, D])
        hT = sb("hT", [P, KD, T])
        pool_a = sb("pool_a", [P, 6656])
        pool_b = sb("pool_b", [P, 5632])
        pool_c = sb("pool_c", [P, 2048])
        g1_bc = sb("g1_bc", [P, D])
        g2_bc = sb("g2_bc", [P, D])
        acc = sb("acc", [P, D])
        brow = sb("brow", [P, 2, 256])
        ident = sb("ident", [P, P])
        ones = sb("ones", [P, P])
        mean64 = sb("mean64", [P, P])
        upto = sb("upto", [P, P])
        since = sb("since", [P, P])
        after = sb("after", [P, P])
        before = sb("before", [P, P])
        lvl = sb("lvl", [P, 7, P], mybir.dt.uint8)
        par_all = sb("par_all", [P, L, NPAR])
        par = sb("par", [P, NPAR])
        anorm0 = sb("anorm0", [P, KD])
        c_sb = sb("c_sb", [P, KD])
        A1, B1 = sb("A1", [P, KD]), sb("B1", [P, KD])
        A2, B2 = sb("A2", [P, KD]), sb("B2", [P, KD])
        eps_c = sb("eps_c", [P, 1])
        gatew = sb("gatew", [33, 512])
        rw_sb = sb("rw_sb", [P, KD, NE])
        rb_sb = sb("rb_sb", [P, NE])
        ssq = sb("ssq", [P, 8])
        rstd = sb("rstd", [P, 8])
        mx = sb("mx", [P, 2, 4])
        nmx = sb("nmx", [P, 2, 4])
        sm = sb("sm", [P, 2, 4])
        rsm = sb("rsm", [P, 2, 4])
        dec = sb("dec", [P, 2, 8])
        gwt = sb("gwt", [P, 2, TT])
        row_of = sb("row_of", [P, 2, TT], I32)
        slot_tok = sb("slot_tok", [SLOTS, NBLK], I32)
        tok_now = sb("tok_now", [SLOTS, 2], I32)
        ov_exp = sb("ov_exp", [P, MAXOV], I32)
        wneg = sb("wneg", [P, 3, 32])
        ov_pair = sb("ov_pair", [P, 2], I32)
        ov_f = sb("ov_f", [P, 1])
        one_c = sb("one_c", [P, 1])
        pad0 = sb("pad0", [L, RPB_PAD])
        ctmp = sb("ctmp", [P, KD])
        qscale = sb("qscale", [P, 1])
        lo = sb("lo", [P, 4])
        tok8 = sb("tok8", [P, 8])

        flat = ring[:, :, :].rearrange("p s n -> p (s n)")
        win_w = [flat[:, i * 2048:(i + 1) * 2048].rearrange("p (k n) -> p k n", k=KD) for i in range(2)]
        ada_w = [flat[:, 4096 + i * 2048:4096 + (i + 1) * 2048].rearrange("p (k n) -> p k n", k=KD) for i in range(2)]
        Z = 8192

        def z(n):
            nonlocal Z
            Z += n
            return flat[:, Z - n:Z]
        eq, ek2, qz_l, kz_l = z(1024), z(1024), z(2048), z(1024)
        wlf = ek2[:, 0:256].rearrange("p (k n) -> p k n", k=KD)
        qnz = flat[:, 8192:8192 + 4096].rearrange("p (d r t) -> p d r t", d=4, r=2)
        la = z(2048).rearrange("p (c n) -> p c n", c=TT)
        amat = la.rearrange("p c n -> p (c n)").rearrange("p (c h i) -> p c h i", c=TT, h=4)
        ekx = z(1024).rearrange("p (u n) -> p u n", u=2)
        bT = z(2048).rearrange("p (r n) -> p r n", r=2)
        khat = z(2048).rearrange("p (c n) -> p c n", c=TT)
        gtab = flat[:, Z - 4096:Z - 4096 + 8 * 265].rearrange("p (h m) -> p h m", h=8)
        bm = flat[:, Z - 4096 + 2120:Z - 4096 + 2120 + 1536].rearrange("p (u s n) -> p u s n", u=2, s=3)
        v_tm = z(2048).rearrange("p (c n) -> p c n", c=TT)
        sg = z(2048).rearrange("p (h n) -> p h n", h=4)
        assert Z == 6 * 4096
        cat = hT
        qz = pool_a[:, 0:2048].rearrange("p (r n) -> p r n", r=2)
        kT = pool_a[:, 2048:3072]
        qd = pool_a[:, 3072:5120].rearrange("p (r n) -> p r n", r=2)
        st = pool_a[:, 5120:6656].rearrange("p (r c n) -> p r c n", r=2, c=3)
        S_sb = pool_a[:, 0:2048].rearrange("p (u c n) -> p u c n", u=2, c=4)
        P_sb = pool_a[:, 2048:4096].rearrange("p (u c n) -> p u c n", u=2, c=4)
        PT_sb = pool_a[:, 4096:6144].rearrange("p (u c n) -> p u c n", u=2, c=4)
        xg = pool_a[0:SLOTS, 0:2048].rearrange("p (u n) -> p u n", u=2)
        hgT = pool_a[:, 2048:3072].rearrange("p (u k s) -> p u k s", u=2, k=KD)
        sil = pool_a[:, 3072:4096].rearrange("p (u n) -> p u n", u=2)
        gTs = pool_a[:, 4096:4608].rearrange("p (u n) -> p u n", u=2)
        y_sb = pool_a[:, 4608:5632].rearrange("p (u n) -> p u n", u=2)
        kn = pool_b[:, 0:2048].rearrange("p (d t) -> p d t", d=4)
        vn = pool_b[:, 2048:5632].rearrange("p (n f) -> p n f", n=7)
        sq = pool_c[:, 0:1024].rearrange("p (u n) -> p u n", u=2)
        rt = pool_c[:, 1024:2048].rearrange("p (u n) -> p u n", u=2)
        lfx = pool_c[0:33, 0:512]
        xn = pool_c[:, :].rearrange("p (u n) -> p u n", u=2)
        yg = hT[:, :, :].rearrange("p k t -> p (k t)").rearrange("p (u j n) -> p u j n", u=2, j=2)
        w13 = [[ring[:, 3 * u + i, :].rearrange("p (k n) -> p k n", k=KD) for i in range(2)] for u in range(2)]
        w2s = [ring[:, 3 * u + 2, :].rearrange("p (h q n) -> p h q n", h=2, q=2) for u in range(2)]

        def rt_at(a, n, dt=F32):
            v = pool_b[:, a:a + n]
            return v if dt == F32 else v.bitcast(dt)
        R = {name: rt_at(i * 128, 128) for i, name in enumerate(
            ("score", "sel", "oh1", "oh2", "tmp", "sel2", "first", "lin", "pick1", "pick2", "mask",
             "rank", "dst", "ge", "t2", "t3"))}
        small = [rt_at(2048 + i * 32, 32) for i in range(24)]
        oslot = rt_at(2816, 8 * 64).rearrange("p (j n) -> p j n", j=8)
        oblk = rt_at(3328, 8 * NBLK).rearrange("p (j n) -> p j n", j=8)
        wide = rt_at(3712, MAXOV * NE).rearrange("p (b e) -> p b e", b=MAXOV)
        iota8 = sb("iota8", [P, NE])
        iota4 = sb("iota4", [P, NG])
        iota_e = sb("iota_e", [P, NE])
        iota_s = sb("iota_s", [P, 64])
        io_p, io_f, xor, xsh = (pool_c[:, i * P:(i + 1) * P].bitcast(I32) for i in range(4))
        xfl = pool_c[:, 512:640]
        io_8, io_t, io_e = (pool_c[:, a:b].bitcast(I32) for a, b in ((640, 648), (648, 656), (656, 688)))

        bank = [ctx.enter_context(nc.psum_tensor(f"bank{i}", [P, 512], F32)) for i in range(8)]

        rpb_pad = nc.dram_tensor("rpb_padded", [L, 8 * RPB_W + 2 * RPB_PAD], F32).ap()
        xn_dram = nc.dram_tensor("xn_rows", [T, D], F32).ap()
        y_dram = nc.dram_tensor("y_rows", [NBLK * SLOTS, D], F32).ap()

        tile_ready = sig("tile_ready", len(plan))
        act_took = sig("act_took", seen["a"])
        dve_took = sig("dve_took", seen["d"])
        dve_step = sig("dve_step", DVE_STEPS)
        act_step = sig("act_step", ACT_STEPS)
        pool_step = sig("pool_step", POOL_STEPS)
        consts_p, consts_v = sig("consts_p", 0), sig("consts_v", 0)
        zeros_done, pads_done, rpb_copied = sig("zeros_done", 0), sig("pads_done", 0), sig("rpb_copied", 0)
        x_in, par_in = sig("x_in", 0), sig("par_in", 0)
        c_act = sig("c_act", 0)
        x_new = sig("x_new", TT, TT)
        mod0 = sig("mod0", 0)
        mod_ready = sig("mod_ready", 0)
        win_in = [sig(f"win_in{i}", 16 * WIN_PIECES // 2) for i in range(2)]
        lf_in, gatew_in, gtab_in = sig("lf_in", 16), sig("gatew_in", 48), sig("gtab_in", 16 * 8)
        ada_in = [sig(f"ada_in{i}", 16 * ADA_PIECES, 32 * 4) for i in range(2)]
        ada_used = sig("ada_used", ADA_PIECES, 8)
        wo_in = [sig(f"wo_in{i}", 32) for i in range(2)]
        rstd_done = sig("rstd_done", 2)
        xn_done = sig("xn_done", 8)
        xn_stored = [sig(f"xn_stored{i}", 32) for i in range(2)]
        zeroed_q = sig("zeroed_q", 1)
        zeroed_n = sig("zeroed_n", 1)
        ln_done, gexp_done = sig("ln_done", 4), sig("gexp_done", 4)
        sg_done = sig("sg_done", 1)
        la_done = sig("la_done", 4)
        dec_done = sig("dec_done", 1)
        ekx_done, khat_done = sig("ekx_done", 4), sig("khat_done", 4)
        st_done = sig("st_done", 1)
        diff_q, diff_k = sig("diff_q", 7), sig("diff_k", 7)
        exp_q, exp_k = sig("exp_q", 7), sig("exp_k", 7)
        lev_q, lev_k = sig("lev_q", 7), sig("lev_k", 7)
        sq_done, rt_done = sig("sq_done", 12), sig("rt_done", 12)
        cat_g = sig("cat_g", 1)
        bm_done = sig("bm_done", 8)
        smax_done, sexp_done = sig("smax_done", 8), sig("sexp_done", 8)
        prob_done = sig("prob_done", 8)
        on_done = sig("on_done", 4)
        cat_n = sig("cat_n", 4)
        x_mid = sig("x_mid", TT)
        mask_done, over_in, slot1h = sig("mask_done", 1), sig("over_in", 1), sig("slot1h", 1)
        routed = sig("routed", 1)
        blk = {n: sig(n, 0) for n in ("xg_T", "hg_done", "up_ready", "up_exp", "g_done", "gT_ready",
                                      "gTs_done", "y_ready", "y_evac", "y_saved")}
        dve_blk = sig("dve_blk", 0)
        w_blk = [[sig(f"{n}_in{u}", 0) for n in ("w1", "w3", "w2")] for u in range(2)]
        gathered = [sig(f"gathered{u}", 0) for u in range(2)]
        tok_set = sig("tok_set", 0)
        y_stored = [sig(f"y_stored{u}", 0) for u in range(2)]
        yrows_in = [sig(f"yrows_in{u}", 64) for u in range(2)]
        out_done = sig("out_done", 0)
        y_zeros, y_zeroed = sig("y_zeros", 0), sig("y_zeroed", 0)
        cstep, pstep = sig("cstep", 0), sig("pstep", 0)
        route_exp = sig("route_exp", 1)

        def wait(eng, s, l, n):
            assert s.first + n > 0
            eng.wait_ge(s.s, s.at(l, n))

        def ready(eng, l, key):
            wait(eng, tile_ready, l, index[key] + 1)
            return bank[index[key] % RING]

        passed = {id(e): sig(n, 0) for e, n in ((nc.sync, "passed_sp"), (nc.tensor, "passed_pe"),
                                                (nc.scalar, "passed_act"), (nc.vector, "passed_dve"),
                                                (nc.gpsimd, "passed_pool"))}
        block = ctx.enter_context(nc.Block())


        def pass_on(eng):
            eng.sem_inc(passed[id(eng)].s, 1)

        def wait_blk(eng, name, G, n):
            eng.wait_ge(blk[name].s, G + (2 + n))

        def free_bank(pe, l, key):
            n = index[key]
            if n >= RING:
                who, count = taken[plan[n - RING][0]]
                wait(pe, act_took if who == "a" else dve_took, l, count)
            return bank[n % RING]

        def reg_counts(eng):
            pass_on(eng)
            return (eng.value_load(ov_pair[0:1, 0:1], min_val=0, max_val=L * MAXOV),
                    eng.value_load(ov_pair[0:1, 1:2], min_val=0, max_val=MAXOV))

        def ap_of(v, off, dims):
            return bass.AP(tensor=v.tensor, offset=v.offset + off, ap=[v.ap[0]] + dims)

        def rep(v, n):
            return bass.AP(tensor=v.tensor, offset=v.offset, ap=list(v.ap) + [[0, n]])

        def again(v, n):
            return bass.AP(tensor=v.tensor, offset=v.offset, ap=[v.ap[0], [0, n]] + list(v.ap[1:]))

        ada_cols = [2048 + 256 * m for m in range(16)] + [256 * m for m in range(8)]
        win_cols = [0, 256, C_V, C_V + 256, C_G, C_G + 256, C_KN, C_KN + 256, C_VN, C_VN + 256, C_QN, C_QN + 256]
        last_of_piece = [("q", 1), ("k", 1), ("v", 0, 3), ("v", 1, 3), ("g", 1), ("g", 3), ("kn", 1), ("kn", 3),
                         ("vf", 1), ("vf", 3), ("qn", 1), ("qn", 3)]
        w_ada_v = A["w_ada"].rearrange("l (p k) n -> l p k n", k=KD)
        w_in_v = A["w_in"].rearrange("l (p k) n -> l p k n", k=KD)
        w_out_v = A["w_out"].rearrange("l (k p) n -> l p k n", p=P)
        w1_v = A["w1"].rearrange("l e (p k) n -> (l e) p (k n)", k=KD)
        w3_v = A["w3"].rearrange("l e (p k) n -> (l e) p (k n)", k=KD)
        w2_v = A["w2"].rearrange("l e (h p q) n -> (l e) p h (q n)", h=2, q=2)
        y_blk = y_dram.rearrange("(b s) (h n) -> b h s n", s=SLOTS, h=2)

        @block.sync
        def _(sp):
            def ada_piece(slot, layer, col):
                sp.dma_start(ada_w[slot], w_ada_v[layer][:, :, col:col + 256]).then_inc(ada_in[slot].s, 16)
                sp.dma_start(brow[0:1, slot, :], A["b_ada"].rearrange("l (a n) -> l a n", a=1)[layer][:, col:col + 256]
                             ).then_inc(ada_in[slot].s, 16)

            def load_w1(u, e):
                sp.dma_start(ring[:, 3 * u, :], w1_v[e]).then_inc(w_blk[u][0].s, 16)

            def load_w3(u, e):
                sp.dma_start(ring[:, 3 * u + 1, :], w3_v[e]).then_inc(w_blk[u][1].s, 16)

            def load_w2(u, e):
                sp.dma_start(ring[:, 3 * u + 2, :].rearrange("p (h n) -> p h n", h=2), w2_v[e]
                             ).then_inc(w_blk[u][2].s, 16)

            sp.dma_start(c_sb[:, :], A["c"][0].rearrange("(p k) -> p k", k=KD)).then_inc(par_in.s, 16)
            sp.dma_start(x_sb[:, :, :], A["x"][0].rearrange("(t p) d -> p t d", p=P)).then_inc(x_in.s, 16)
            sp.wait_ge(consts_v.s, 1)
            for m in range(8):
                if m >= 2:
                    sp.wait_ge(ada_used.s, m - 1)
                ada_piece(m % 2, 0, 256 * m)

            sp.wait_ge(y_zeros.s, 1)
            sp.dma_start(y_dram[NE * SLOTS:].rearrange("(p a) d -> p a d", p=P),
                         again(pool_b[:, 0:D], MAXOV * SLOTS // P)).then_inc(y_zeroed.s, 16)

            with sp.Fori(0, L) as l:
                def win_piece(m):
                    if m >= 2:
                        wait(sp, tile_ready, l, index[last_of_piece[m - 2]] + 1)
                    sp.dma_start(win_w[m % 2], w_in_v[l][:, :, win_cols[m]:win_cols[m] + 256]
                                 ).then_inc(win_in[m % 2].s, 16)

                def ada(m):
                    wait(sp, ada_used, l, m - 1)
                    pass_on(sp)
                    ada_piece(m % 2, l if m < 16 else (1 - l), ada_cols[m])

                sp.wait_ge(x_new.s, l * TT + TT)
                win_piece(0)
                sp.dma_start(wlf[:, :, :], w_in_v[l][:, :, C_LF:C_LF + 32]).then_inc(lf_in.s, 16)
                win_piece(1)
                for m in range(4):
                    ada(m)
                win_piece(2)
                for m in range(4, 8):
                    ada(m)
                win_piece(3)
                for m in range(8, 12):
                    ada(m)
                win_piece(4)
                for m in range(12, 16):
                    ada(m)
                for m in range(5, 10):
                    win_piece(m)
                ada(16), ada(17)
                win_piece(10), win_piece(11)
                for m in range(18, 24):
                    ada(m)
                wait(sp, tile_ready, l, index[("qn", 3)] + 1)
                load_w1(0, l * NE)

                def wo_piece(m):
                    sp.dma_start(ada_w[m % 2], w_out_v[l][:, :, m * 256:(m + 1) * 256]).then_inc(wo_in[m % 2].s, 16)
                for m in range(2):
                    wait(sp, ada_used, l, ADA_PIECES - 1 + m)
                    wo_piece(m)
                wait(sp, cat_n, l, 4)
                load_w2(0, l * NE)
                load_w1(1, l * NE + 1), load_w3(1, l * NE + 1), load_w2(1, l * NE + 1)
                for m in range(2, 4):
                    wait(sp, tile_ready, l, index[("y", m - 2, TT - 1)] + 1)
                    wo_piece(m)
                wait(sp, tile_ready, l, index[("y", 3, TT - 1)] + 1)
                load_w3(0, l * NE)
                wait(sp, routed, l, 1)
                ov0, nov = reg_counts(sp)
                with sp.Fori(1, NE // 2) as i:
                    for u in range(2):
                        G = l * NE + ov0 + i * 2 + u
                        e = l * NE + i * 2 + u
                        wait_blk(sp, "up_ready", G, -1)
                        load_w1(u, e)
                        load_w3(u, e)
                        wait_blk(sp, "y_ready", G, -1)
                        load_w2(u, e)
                with sp.If(nov > 0):
                    with sp.Fori(0, nov) as j:
                        G = l * NE + NE + ov0 + j
                        e = sp.value_load(ov_exp[0:1, bass.ds(j, 1)], min_val=0, max_val=NE - 1)
                        wait_blk(sp, "up_ready", G, 0)
                        load_w1(0, l * NE + e)
                        load_w3(0, l * NE + e)
                        wait_blk(sp, "y_ready", G, 0)
                        load_w2(0, l * NE + e)
            sp.wait_ge(x_new.s, L * TT + TT)
            sp.dma_start(A["out"][0].rearrange("(t p) d -> p t d", p=P), x_sb[:, :, :]).then_inc(out_done.s, 16)
            sp.wait_ge(out_done.s, 16)

        @block.tensor
        def _(pe):
            def mm(out, lhsT, rhs, start, stop):
                return nc.tensor.matmul(out, lhsT, rhs, start=start, stop=stop, skip_group_check=True)

            def sum_chunk(out, cols):
                for k in range(KD):
                    last = mm(out[:, k:k + 1], acc[:, :].rearrange("p (n k) -> p k n", k=KD)[:, k, :],
                              ones[:, 0:1], True, True)
                return last

            pe.wait_ge(consts_p.s, 1)
            pe.wait_ge(consts_v.s, 2)
            for n in ("xg_T", "up_ready", "gT_ready", "y_ready"):
                pe.sem_inc(blk[n].s, 2)
            for n in range(2):
                pe.wait_ge(ada_used.s, 4 * (n + 1))
                sum_chunk(bank[7][:, n * 8:n * 8 + 8], n).then_inc(mod0.s, 1)

            with pe.Fori(0, L) as l:
                def norm_transposes(which):
                    for tt in range(TT):
                        wait(pe, xn_done, l, 4 * (which - 1) + tt + 1)
                        for h in range(2):
                            out = free_bank(pe, l, ("x", which, tt, h))
                            for k in range(4):
                                src = xn[:, tt % 2, :].rearrange("p (n k) -> p k n", k=KD)[:, 4 * h + k, :]
                                last = nc.tensor.transpose(out[:, k * P:(k + 1) * P], src, ident[:, :])
                            last.then_inc(tile_ready.s, 1)

                def hT_ready(which):
                    wait(pe, act_took, l, taken[("x", which, TT - 1, 0)][1])
                    wait(pe, dve_took, l, taken[("x", which, TT - 1, 1)][1])

                def piece(m):
                    wait(pe, win_in[m % 2], l, 16 * (m // 2 + 1))
                    return win_w[m % 2]

                def feature_tile(key, w, col):
                    out = free_bank(pe, l, key)
                    for k in range(KD):
                        last = mm(out[:, :], w[:, k, col:col + P], hT[:, k, :], k == 0, k == KD - 1)
                    last.then_inc(tile_ready.s, 1)

                def token_tile(key, w, tokens):
                    out = free_bank(pe, l, key)
                    for k in range(KD):
                        last = mm(out[:, 0:256], tokens(k), w[:, k, :], k == 0, k == KD - 1)
                    last.then_inc(tile_ready.s, 1)

                def ada_tile(n):
                    out = free_bank(pe, l, ("ada", n))
                    wait(pe, ada_used, l, 4 * (n + 1))
                    if n in (0, 3):
                        mm(out[:, :], ones[:, :], acc[:, 0:512], True, True).then_inc(tile_ready.s, 1)
                        out = free_bank(pe, l, ("ada", n, 1))
                        mm(out[:, :], ones[:, :], acc[:, 512:1024], True, True).then_inc(tile_ready.s, 1)
                    else:
                        sum_chunk(out, n).then_inc(tile_ready.s, 1)

                norm_transposes(1)
                hT_ready(1)
                w = piece(0)
                for d in range(2):
                    feature_tile(("q", d), w, d * P)
                ada_tile(0)
                w = piece(1)
                for d in range(2):
                    feature_tile(("k", d), w, d * P)
                out = free_bank(pe, l, ("lf",))
                wait(pe, lf_in, l, 16)
                for k in range(KD):
                    last = mm(out[0:32, :], wlf[:, k, :], hT[:, k, :], k == 0, k == KD - 1)
                last.then_inc(tile_ready.s, 1)
                ada_tile(1)
                for m in range(2):
                    w = piece(2 + m)
                    for c in range(TT):
                        token_tile(("v", m, c), w, lambda k: hT[:, k, c * P:(c + 1) * P])
                    ada_tile(2 + m)
                for h in range(4):
                    feature_tile(("g", h), piece(4 + h // 2), (h % 2) * P)

                wait(pe, act_took, l, taken[("lf",)][1])
                wait(pe, gatew_in, l, 48)
                for c in range(TT):
                    out = free_bank(pe, l, ("z", c))
                    mm(out[:, :], lfx[:, c * P:(c + 1) * P], gatew[:, :], True, True).then_inc(tile_ready.s, 1)
                wait(pe, la_done, l, 4)
                for r in range(2):
                    for d in range(2):
                        out = free_bank(pe, l, ("b", r, d))
                        for c in range(TT):
                            f = r * 256 + d * P
                            last = mm(out[:, c * P:(c + 1) * P], la[:, c, f:f + P], (upto, since)[r][:, :], True, True)
                        last.then_inc(tile_ready.s, 1)
                for c in range(TT):
                    out = free_bank(pe, l, ("kx", c))
                    mm(out[:, 0:256], after[:, :], la[:, c, 0:256], True, True)
                    mm(out[:, 256:512], before[:, :], la[:, c, 256:512], True, True).then_inc(tile_ready.s, 1)
                    out = free_bank(pe, l, ("kt", c))
                    for d in range(2):
                        last = nc.tensor.transpose(out[:, d * P:(d + 1) * P],
                                                   kT[:, d * T + c * P:d * T + (c + 1) * P], ident[:, :])
                    last.then_inc(tile_ready.s, 1)
                for r, c in [(0, 0), (0, 1), (0, 2), (1, 3), (1, 2), (1, 1)]:
                    out = free_bank(pe, l, ("U", r, c))
                    wait(pe, khat_done, l, c + 1)
                    for h in range(4):
                        half = 64 * (h % 2)
                        last = mm(out[half:half + 64, (h // 2) * P:(h // 2 + 1) * P],
                                  khat[:, c, r * 256 + h * 64:r * 256 + h * 64 + 64],
                                  v_tm[:, c, h * P:(h + 1) * P], True, True)
                    last.then_inc(tile_ready.s, 1)

                def level_tiles(lev, kv, qv):
                    for c in range(TT):
                        out = free_bank(pe, l, ("P", lev, c))
                        for d in range(2):
                            at = d * T + c * P
                            last = mm(out[:, d * 256:(d + 1) * 256], kv[:, at:at + P], qv[:, :, at:at + P], True, True)
                        last.then_inc(tile_ready.s, 1)

                def mean_tile(key, n, weights):
                    out = free_bank(pe, l, key)
                    wait(pe, sq_done, l, n + 1)
                    mm(out[:, :], weights[:, :], sq[:, n % 2, :], True, True).then_inc(tile_ready.s, 1)

                wait(pe, zeroed_q, l, 1)
                level_tiles(7, kT, qz)
                done = index[("P", 7, TT - 1)] + 1
                for n, lev in enumerate(LEVELS):
                    wait(pe, lev_q, l, n + 1)
                    wait(pe, lev_k, l, n + 1)
                    level_tiles(lev, kz_l, qz_l.rearrange("p (r n) -> p r n", r=2))
                    done = index[("P", lev, TT - 1)] + 1
                    while done < len(plan) and plan[done][0][0] in ("kn", "kms", "vf", "vt"):
                        key = plan[done][0]
                        if key[0] == "kn":
                            feature_tile(key, piece(6 + key[1] // 2), (key[1] % 2) * P)
                        elif key[0] == "kms":
                            mean_tile(key, key[1], mean64)
                        elif key[0] == "vf":
                            feature_tile(key, piece(8 + key[1] // 2), (key[1] % 2) * P)
                        else:
                            out = free_bank(pe, l, key)
                            wait(pe, act_took, l, taken[("vf", key[1])][1])
                            for n7 in range(4 * key[2], min(4 * key[2] + 4, 7)):
                                last = nc.tensor.transpose(out[:, (n7 % 4) * P:(n7 % 4 + 1) * P],
                                                           ekx[:, key[1] % 2, n7 * 64:n7 * 64 + P], ident[:, :])
                            last.then_inc(tile_ready.s, 1)
                        done += 1
                for i, ms in ((0, None), (1, 0), (2, 1), (3, 2), (None, 3)):
                    if i is not None:
                        feature_tile(("qn", i), piece(10 + i // 2), (i % 2) * P)
                    if ms is not None:
                        mean_tile(("qms", ms), 4 + ms, mean64)
                    if i == 1:
                        ada_tile(4)
                ada_tile(5)

                wait(pe, dve_took, l, taken[("P", 0, TT - 1)][1])
                wait(pe, st_done, l, 1)
                for i, ms in ((0, None), (1, 0), (2, 1), (3, 2), (None, 3)):
                    if i is not None:
                        out = free_bank(pe, l, ("o", i))
                        half, d = 64 * (i % 2), i // 2
                        for c in range(TT):
                            o = out[:, c * P:(c + 1) * P]
                            at = d * T + c * P
                            last = mm(o, v_tm[:, c, i * P:(i + 1) * P], amat[:, c, i, :], True, False)
                            for r in range(2):
                                if (c > 0, c < TT - 1)[r]:
                                    last = mm(o, st[half:half + 64, r, c - 1 + r, d * P:(d + 1) * P],
                                              qd[half:half + 64, r, at:at + P], False, r == 1 or c == TT - 1)
                        last.then_inc(tile_ready.s, 1)
                    if ms is not None:
                        mean_tile(("oms", ms), 8 + ms, ones)

                for h in range(10):
                    if h < 8:
                        d, r = h // 2, h % 2
                        if r == 0:
                            wait(pe, dve_took, l, taken[("qn", d)][1])
                        for i in range(2):
                            out = free_bank(pe, l, ("S", h, i))
                            for cb in (2 * i, 2 * i + 1):
                                q0 = T - P * (cb + 1)
                                last = mm(out[:, (cb % 2) * 256:(cb % 2 + 1) * 256], qnz[:, d, r, q0:q0 + P],
                                          kn[:, d, KEY_AT[cb] * 64:KEY_AT[cb] * 64 + 256], True, True)
                            last.then_inc(tile_ready.s, 1)
                    if 1 <= h < 9:
                        g = h - 1
                        wait(pe, prob_done, l, g + 1)
                        for i in range(2):
                            out = free_bank(pe, l, ("PT", g, i))
                            for cb in (2 * i, 2 * i + 1):
                                for half in range(2):
                                    last = nc.tensor.transpose(
                                        out[:, (cb % 2) * 256 + half * P:(cb % 2) * 256 + (half + 1) * P],
                                        P_sb[:, g % 2, cb, half * P:(half + 1) * P], ident[:, :])
                            last.then_inc(tile_ready.s, 1)
                    if h >= 2:
                        g = h - 2
                        d, r = g // 2, g % 2
                        wait(pe, act_took, l, taken[("PT", g, 1)][1])
                        if r == 0 and d >= 2:
                            wait(pe, cat_n, l, d - 1)
                        for cb in range(4):
                            q0 = T - P * (cb + 1)
                            for half in range(2):
                                last = mm(bank[6 + d % 2][64 * r:64 * r + 64, q0:q0 + P],
                                          vn[:, KEY_AT[cb] + 2 * half, g * 64:(g + 1) * 64],
                                          PT_sb[:, g % 2, cb, half * P:(half + 1) * P], half == 0, half == 1)
                        if r == 1:
                            last.then_inc(on_done.s, 1)

                wait(pe, cat_g, l, 1)
                wait(pe, cat_n, l, 4)
                for m in range(4):
                    wait(pe, wo_in[m % 2], l, 16 * (m // 2 + 1))
                    for tt in range(TT):
                        token_tile(("y", m, tt), ada_w[m % 2], lambda k: cat[:, k, tt * P:(tt + 1) * P])
                norm_transposes(2)
                hT_ready(2)
                out = free_bank(pe, l, ("logits",))
                for tt in range(TT):
                    for k in range(KD):
                        last = mm(out[:, tt * NE:(tt + 1) * NE], hT[:, k, tt * P:(tt + 1) * P], rw_sb[:, k, :],
                                  k == 0, k == KD - 1)
                last.then_inc(tile_ready.s, 1)

                out = free_bank(pe, l, ("rank",))
                wait(pe, mask_done, l, 1)
                mask = R["mask"]
                for tt in range(TT):
                    o = out[:, tt * NE:(tt + 1) * NE]
                    mm(o, before[:, :], mask[:, tt * NE:(tt + 1) * NE], True, tt == 0)
                    for t2 in range(tt):
                        mm(o, ones[:, :], mask[:, t2 * NE:(t2 + 1) * NE], False, t2 == tt - 1)
                for tt in range(TT):
                    mm(out[:, 128:128 + NE], ones[:, :], mask[:, tt * NE:(tt + 1) * NE], tt == 0, tt == TT - 1)
                for tt in range(TT):
                    last = mm(out[0:NE, 160:161], mask[:, tt * NE:(tt + 1) * NE], ones[:, 0:1], tt == 0, tt == TT - 1)
                last.then_inc(tile_ready.s, 1)
                out = free_bank(pe, l, ("over",))
                wait(pe, over_in, l, 1)
                nov = R["t3"][0:NE, :]
                mm(out[:, 0:NE], nov, before[0:NE, 0:NE], True, True)
                mm(out[:, NE:NE + 1], nov, ones[0:NE, 0:1], True, True).then_inc(tile_ready.s, 1)
                out = free_bank(pe, l, ("slot",))
                wait(pe, slot1h, l, 1)
                for j in range(8):
                    last = mm(out[0:SLOTS, 0:NBLK], oslot[:, j, :], oblk[:, j, :], j == 0, j == 7)
                last.then_inc(tile_ready.s, 1)

                wait(pe, routed, l, 1)
                ov0, nov = reg_counts(pe)

                def expert_block(u, G, uses, back):
                    pe.wait_ge(gathered[u].s, uses * 16 + 16)
                    wait_blk(pe, "hg_done", G, 1 - back)
                    pass_on(pe)
                    for k in range(KD):
                        src = xg[:, u, :].rearrange("p (n k) -> p k n", k=KD)[:, k, :]
                        last = nc.tensor.transpose(bank[u][:, k * SLOTS:(k + 1) * SLOTS], src,
                                                   ident[0:SLOTS, 0:SLOTS])
                    last.then_inc(blk["xg_T"].s, 1)
                    wait_blk(pe, "hg_done", G, 1)
                    wait_blk(pe, "g_done", G, 1 - back)
                    for mat in range(2):
                        pe.wait_ge(w_blk[u][mat].s, uses * 16 + 16)
                        for k in range(KD):
                            for half in range(2):
                                last = mm(bank[2 + u][64 * half:64 * half + 64, mat * 256:(mat + 1) * 256],
                                          hgT[:, u, k, :], w13[u][mat][:, k, half * 256:(half + 1) * 256],
                                          k == 0, k == KD - 1)
                    last.then_inc(blk["up_ready"].s, 1)
                    wait_blk(pe, "g_done", G, 1)
                    wait_blk(pe, "gTs_done", G, 1 - back)
                    for q in range(2):
                        src = sil[:, u, 256:512].rearrange("p (n q) -> p q n", q=2)[:, q, :]
                        last = nc.tensor.transpose(bank[4 + u][:, q * P:(q + 1) * P], src, ident[:, :])
                    last.then_inc(blk["gT_ready"].s, 1)
                    wait_blk(pe, "gTs_done", G, 1)
                    wait_blk(pe, "y_evac", G, 1 - back)
                    pe.wait_ge(w_blk[u][2].s, uses * 16 + 16)
                    for n in range(4):
                        hh, q = n // 2, n % 2
                        for nh in range(2):
                            last = mm(bank[6 + u][64 * nh:64 * nh + 64, :],
                                      gTs[:, u, q * P + hh * 64:q * P + hh * 64 + 64],
                                      w2s[u][:, hh, q, nh * 512:(nh + 1) * 512], n == 0, n == 3)
                    last.then_inc(blk["y_ready"].s, 1)

                with pe.Fori(0, NE // 2) as i:
                    expert_block(0, l * NE + ov0 + i * 2, l * (NE // 2) + ov0 + i, 2)
                    expert_block(1, l * NE + ov0 + i * 2 + 1, l * (NE // 2) + i, 2)
                with pe.If(nov > 0):
                    with pe.Fori(0, nov) as j:
                        expert_block(0, l * NE + NE + ov0 + j, l * (NE // 2) + NE // 2 + ov0 + j, 1)

        @block.scalar
        def _(act):
            steps = [0]

            def link(l, ins):
                steps[0] += 1
                ins.then_inc(act_step.s, 1)
                wait(act, act_step, l, steps[0])

            F = nc.scalar.activation
            nc.scalar.preload_act_table_set("natural_log_exp_and_others")
            act.wait_ge(consts_p.s, 1)
            for n in ("gTs_done", "y_evac", "up_exp"):
                act.sem_inc(blk[n].s, 2)
            for l0 in range(L):
                def vec(v, n):
                    return v.rearrange("(p k) -> p k", k=n)
                act.dma_start(par_all[:, l0, 0:8], vec(A["ffn_norm"][l0], KD)).then_inc(par_in.s, 16)
                act.dma_start(par_all[:, l0, 8:16], vec(A["attn_norm"][1 - l0], KD)).then_inc(par_in.s, 16)
                act.dma_start(par_all[:, l0, 16:17], vec(A["gla_out_norm"][l0], 1)).then_inc(par_in.s, 16)
                for half in range(2):
                    rows = slice(64 * half, 64 * half + 64)
                    act.dma_start(par_all[rows, l0, 17:18], vec(A["na_q_norm"][l0], 1)).then_inc(par_in.s, 16)
                    act.dma_start(par_all[rows, l0, 18:19], vec(A["na_k_norm"][l0], 1)).then_inc(par_in.s, 16)
            act.dma_start(anorm0[:, :], A["attn_norm"][0].rearrange("(p k) -> p k", k=KD)).then_inc(par_in.s, 16)
            act.dma_start(rw_sb[:, :, :], A["router_w"].rearrange("(p k) n -> p k n", k=KD)).then_inc(par_in.s, 16)
            act.dma_start(rb_sb[:, :], bass.AP(tensor=A["router_b"].tensor, offset=0, ap=[[0, P], [1, NE]])
                          ).then_inc(par_in.s, 16)
            act.dma_start(rpb_pad[:, RPB_PAD:RPB_PAD + 8 * RPB_W], A["na_rpb"].rearrange("l h a b -> l (h a b)")
                          ).then_inc(rpb_copied.s, 16)
            act.wait_ge(consts_v.s, 2)
            act.dma_start(rpb_pad[:, 0:RPB_PAD], pad0[:, :]).then_inc(rpb_copied.s, 16)
            act.dma_start(rpb_pad[:, RPB_PAD + 8 * RPB_W:], pad0[:, :]).then_inc(rpb_copied.s, 16)
            act.wait_ge(rpb_copied.s, 48)
            act.wait_ge(par_in.s, 16 * 18)
            F(ctmp[:, :], c_sb[:, :], ACT.Exp, scale=-1.0).then_inc(c_act.s, 1)

            with act.Fori(0, L) as l:
                steps[0] = 0

                def gates_load():
                    act.dma_start(gatew[0:16, 0:256], A["gla_gate_w"].rearrange("l r a n -> (l r) a n")[l * 2]
                                  ).then_inc(gatew_in.s, 16)
                    act.dma_start(gatew[16:32, 256:512], A["gla_gate_w"].rearrange("l r a n -> (l r) a n")[l * 2 + 1]
                                  ).then_inc(gatew_in.s, 16)
                    act.dma_start(gatew[32:33, :], A["gla_gate_b"].rearrange("l (a r) n -> l a (r n)", a=1)[l]
                                  ).then_inc(gatew_in.s, 16)

                def tile(key):
                    return ready(act, l, key)

                def norm(which):
                    c0 = 4 * (which - 1)
                    src = x_new if which == 1 else x_mid
                    for tt in range(TT):
                        act.wait_ge(src.s, l * TT + tt + 1)
                        link(l, F(flat[:, 8192:9216] if which == 1 else pool_a[:, 0:1024], x_sb[:, tt, :], ACT.Square,
                                  accum_out=ssq[:, c0 + tt:c0 + tt + 1]))
                    link(l, F(rstd[:, c0:c0 + 4], ssq[:, c0:c0 + 4], ACT.Ln, bias=eps_c[:, 0:1], scale=1.0 / D))
                    F(rstd[:, c0:c0 + 4], rstd[:, c0:c0 + 4], ACT.Exp, scale=-0.5).then_inc(rstd_done.s, 1)

                def shift(which):
                    a_, b_ = (A1, B1) if which == 1 else (A2, B2)
                    for tt in range(TT):
                        b = tile(("x", which, tt, 0))
                        for k in range(4):
                            last = F(hT[:, k, tt * P:(tt + 1) * P], b[:, k * P:(k + 1) * P], ACT.Identity,
                                     bias=b_[:, k:k + 1], scale=a_[:, k:k + 1])
                        last.then_inc(act_took.s, 1)

                norm(1)
                gates_load()
                act.wait_ge(mod_ready.s, 1)
                shift(1)
                for d in range(2):
                    b = tile(("q", d))
                    for half in range(2):
                        rows = slice(64 * half, 64 * half + 64)
                        last = F(qz[rows, half, d * T:(d + 1) * T], b[rows, :], ACT.Copy, scale=0.125)
                    last.then_inc(act_took.s, 1)
                for d in range(2):
                    b = tile(("k", d))
                    F(kT[:, d * T:(d + 1) * T], b[:, :], ACT.Copy).then_inc(act_took.s, 1)
                b = tile(("lf",))
                wait(act, dve_took, l, taken[("ada", 0)][1])
                F(lfx[0:32, :], b[0:32, :], ACT.Copy).then_inc(act_took.s, 1)
                for m in range(2):
                    for c in range(TT):
                        b = tile(("v", m, c))
                        F(v_tm[:, c, m * 256:(m + 1) * 256], b[:, 0:256], ACT.Copy).then_inc(act_took.s, 1)
                for h in range(4):
                    b = tile(("g", h))
                    F(sg[:, h, :], b[:, :], ACT.Exp, scale=-1.0).then_inc(gexp_done.s, 1)
                for c in range(TT):
                    b = tile(("z", c))
                    t1 = rt[:, c % 2, :]
                    if c >= 2:
                        wait(act, la_done, l, c - 1)
                    link(l, F(t1, b[:, :], ACT.Abs))
                    link(l, F(t1, t1, ACT.Exp, scale=-1.0))
                    F(t1, t1, ACT.Ln, bias=one_c[:, 0:1]).then_inc(ln_done.s, 1)
                for r in range(2):
                    for d in range(2):
                        b = tile(("b", r, d))
                        F(bT[:, r, d * T:(d + 1) * T], b[:, :], ACT.Copy).then_inc(act_took.s, 1)
                wait(act, act_took, l, taken[("b", 1, 1)][1])
                for c in range(TT):
                    b = tile(("kx", c))
                    if c >= 2:
                        wait(act, khat_done, l, c - 1)
                    F(ekx[:, c % 2, :], b[:, :], ACT.Exp, scale=TAU_INV).then_inc(act_took.s, 1)
                for r in range(2):
                    F(qd[:, r, :], bT[:, r, :], ACT.Exp, scale=TAU_INV)
                    ends = bT[:, r, :].rearrange("p (n i) -> p n i", i=P)[:, :, P - 1 if r == 0 else 0]
                    last = F(dec[:, r, :], ends, ACT.Exp, scale=TAU_INV)
                last.then_inc(dec_done.s, 1)
                for c in range(TT):
                    b = tile(("P", 7, c))
                    F(amat[:, c, :, :].rearrange("p h i -> p (h i)"), b[:, :], ACT.Copy).then_inc(act_took.s, 1)

                def squares(key, n):
                    b = tile(key)
                    if n >= 2:
                        ms = {"kn": "kms", "qn": "qms", "o": "oms"}
                        prev = [(a, i) for a in ("kn", "qn", "o") for i in range(4)][n - 2]
                        wait(act, tile_ready, l, index[(ms[prev[0]], prev[1])] + 1)
                    F(sq[:, n % 2, :], b[:, :], ACT.Square).then_inc(sq_done.s, 1)

                def scales(key, n):
                    b = tile(key)
                    if n >= 2:
                        prev = [(a, i) for a in ("kn", "qn", "o") for i in range(4)][n - 2]
                        wait(act, dve_took, l, taken[prev][1])
                    F(rt[:, n % 2, :], b[:, :], ACT.Ln, bias=eps_c[:, 0:1],
                      scale=1.0 if n < 8 else 1.0 / 128).then_inc(act_took.s, 1)
                    wait(act, act_took, l, taken[key][1])
                    F(rt[:, n % 2, :], rt[:, n % 2, :], ACT.Exp, scale=-0.5).then_inc(rt_done.s, 1)

                for n, lev in enumerate(LEVELS):
                    wait(act, diff_q, l, n + 1)
                    F(eq, eq, ACT.Exp, scale=TAU_INV).then_inc(exp_q.s, 1)
                    wait(act, diff_k, l, n + 1)
                    F(ek2, ek2, ACT.Exp, scale=TAU_INV).then_inc(exp_k.s, 1)
                    at = index[("P", lev, TT - 1)] + 1
                    while plan[at][0][0] in ("kn", "kms", "vf", "vt"):
                        key = plan[at][0]
                        at += 1
                        if key[0] == "kn":
                            squares(key, key[1])
                        elif key[0] == "kms":
                            scales(key, key[1])
                        else:
                            b = tile(key)
                            f = key[1]
                            if key[0] == "vf":
                                if f >= 2:
                                    wait(act, tile_ready, l, index[("vt", f - 2, 1)] + 1)
                                F(ekx[:, f % 2, :].rearrange("p (c r) -> p r c", r=ROWS),
                                  b[:, :].rearrange("p (r c) -> p r c", c=COLS), ACT.Copy).then_inc(act_took.s, 1)
                            else:
                                n0, n1 = 4 * key[2], min(4 * key[2] + 4, 7)
                                F(vn[:, n0:n1, f * P:(f + 1) * P],
                                  b[:, 0:(n1 - n0) * P].rearrange("p (n f) -> p n f", f=P), ACT.Copy
                                  ).then_inc(act_took.s, 1)
                        if at == len(plan):
                            break
                for pre, n0 in (("qn", 4), ("o", 8)):
                    ms = pre[0] + "ms"
                    squares((pre, 0), n0), squares((pre, 1), n0 + 1)
                    for i in range(4):
                        scales((ms, i), n0 + i)
                        if i < 2:
                            squares((pre, i + 2), n0 + i + 2)
                wait(act, st_done, l, 1)
                wait(act, tile_ready, l, index[("o", 3)] + 1)
                for h in range(8):
                    src = bass.AP(tensor=rpb_pad.tensor, offset=rpb_pad[l][h * RPB_W:h * RPB_W + 1].offset,
                                  ap=[[1, 16], [31, 8], [1, 265]])
                    act.dma_start(gtab[:, h, :], src).then_inc(gtab_in.s, 16)

                for h in range(10):
                    if h < 8:
                        wait(act, smax_done, l, h + 1)
                        for cb in range(4):
                            last = F(P_sb[:, h % 2, cb, :], S_sb[:, h % 2, cb, :], ACT.Exp,
                                     bias=nmx[:, h % 2, cb:cb + 1], accum_out=sm[:, h % 2, cb:cb + 1])
                        last.then_inc(sexp_done.s, 1)
                    if 1 <= h < 9:
                        g = h - 1
                        for i in range(2):
                            b = tile(("PT", g, i))
                            F(PT_sb[:, g % 2, 2 * i:2 * i + 2, :].rearrange("p c n -> p (c n)"), b[:, :], ACT.Copy
                              ).then_inc(act_took.s, 1)
                    if h >= 2 and h % 2 == 1:
                        d = (h - 2) // 2
                        wait(act, on_done, l, d + 1)
                        src = ap_of(bank[6 + d % 2][:, :], T - 1, [[-1, ROWS], [-ROWS, COLS]])
                        F(cat[:, 4 + d, :].rearrange("p (r c) -> p r c", c=COLS), src, ACT.Copy).then_inc(cat_n.s, 1)

                norm(2)
                for tt in range(TT):
                    wait(act, xn_done, l, 4 + tt + 1)
                    act.dma_start(xn_dram[tt * P:(tt + 1) * P, :], xn[:, tt % 2, :]).then_inc(xn_stored[tt % 2].s, 16)
                shift(2)
                b = tile(("logits",))
                F(R["score"], b[:, 0:128], ACT.Exp, scale=-1.0).then_inc(route_exp.s, 1)

                wait(act, routed, l, 1)
                ov0, nov = reg_counts(act)

                def expert_block(u, G, row, back):
                    wait_blk(act, "up_ready", G, 1)
                    wait_blk(act, "gT_ready", G, 1 - back)
                    F(sil[:, u, 0:256], bank[2 + u][:, 0:256], ACT.Exp, scale=-1.0).then_inc(blk["up_exp"].s, 1)
                    wait_blk(act, "gT_ready", G, 1)
                    F(gTs[:, u, :], bank[4 + u][:, 0:256], ACT.Copy).then_inc(blk["gTs_done"].s, 1)
                    wait_blk(act, "y_ready", G, 1)
                    wait_blk(act, "y_saved", G, 1 - back)
                    F(y_sb[:, u, :], bank[6 + u][:, :], ACT.Copy).then_inc(blk["y_evac"].s, 1)
                    wait_blk(act, "y_evac", G, 1)
                    for nh in range(2):
                        act.dma_start(y_blk[row][nh], y_sb[64 * nh:64 * nh + 64, u, :]).then_inc(y_stored[u].s, 16)

                with act.Fori(0, NE // 2) as i:
                    for u in range(2):
                        expert_block(u, l * NE + ov0 + i * 2 + u, i * 2 + u, 2)
                with act.If(nov > 0):
                    with act.Fori(0, nov) as j:
                        expert_block(0, l * NE + NE + ov0 + j, j + NE, 1)
            assert steps[0] == ACT_STEPS, steps

        @block.vector
        def _(dve):
            V = nc.vector
            steps = [0]

            def link(l, ins):
                steps[0] += 1
                ins.then_inc(dve_step.s, 1)
                wait(dve, dve_step, l, steps[0])

            n0 = [0]

            def link0(ins):
                n0[0] += 1
                ins.then_inc(cstep.s, 1)
                dve.wait_ge(cstep.s, n0[0])
            link0(V.memset(brow[:, :, :].rearrange("p u n -> p (u n)"), 0.0))
            V.memset(pad0[:, :], 0.0).then_inc(consts_v.s, 1)
            V.memset(ones[:, :], 1.0)
            link0(V.memset(mean64[:, :], 0.0))
            V.memset(mean64[0:64, 0:64], 1.0 / 64)
            V.memset(mean64[64:128, 64:128], 1.0 / 64)
            V.memset(eps_c[:, :], EPS)
            V.memset(one_c[:, :], 1.0)
            V.memset(gatew[:, :], 0.0)
            V.memset(ov_pair[:, :], 0)
            V.memset(ov_f[:, :], 0.0).then_inc(consts_v.s, 1)
            dve.wait_ge(consts_p.s, 1)
            link0(V.tensor_tensor(xor[:, :], io_p[:, :], io_f[:, :], ALU.bitwise_xor))
            for s_ in range(7):
                link0(V.tensor_scalar(xsh[:, :], xor[:, :], s_, None, ALU.arith_shift_right))
                link0(V.tensor_copy(xfl[:, :], xsh[:, :]))
                link0(V.tensor_scalar(lvl[:, s_, :], xfl[:, :], 1.0, None, ALU.is_equal))
            link0(V.tensor_scalar(xsh[:, 0:1], io_p[:, 0:1], 3, None, ALU.arith_shift_right))
            link0(V.tensor_copy(lo[:, 3:4], xsh[:, 0:1]))
            link0(V.tensor_scalar(lo[:, 1:2], lo[:, 3:4], -1.0, 15.0, ALU.mult, ALU.add))
            link0(V.tensor_scalar(lo[:, 0:1], lo[:, 1:2], -8.0, 0.0, ALU.add, ALU.max))
            link0(V.tensor_scalar(lo[:, 2:3], lo[:, 1:2], 8.0, 16.0, ALU.add, ALU.min))
            for m in range(3):
                link0(V.tensor_scalar(xfl[:, 0:32], iota_s[:, 0:32], lo[:, m:m + 1], None, ALU.subtract))
                link0(V.tensor_scalar(xfl[:, 32:64], xfl[:, 0:32], 0.0, None, ALU.is_ge))
                link0(V.tensor_scalar(xfl[:, 64:96], xfl[:, 0:32], 15.5, None, ALU.is_lt))
                link0(V.tensor_tensor(xfl[:, 96:128], xfl[:, 32:64], xfl[:, 64:96], ALU.mult))
                link0(V.tensor_scalar(wneg[:, m, :], xfl[:, 96:128], -1.0, -NEG, ALU.add, ALU.mult))
            dve.wait_ge(c_act.s, 1)
            dve.wait_ge(par_in.s, 16 * 18)
            link0(V.tensor_scalar(ctmp[:, :], ctmp[:, :], 1.0, None, ALU.add))
            link0(V.reciprocal(ctmp[:, :], ctmp[:, :]))
            link0(V.tensor_tensor(ctmp[:, :], ctmp[:, :], c_sb[:, :], ALU.mult))
            for n in ("hg_done", "g_done"):
                dve.sem_inc(blk[n].s, 2)

            def ada_piece(slot, quarter, step):
                out = acc[:, quarter * 256:(quarter + 1) * 256]
                for k in range(KD):
                    src = brow[:, slot, :] if k == 0 else out
                    ins = V.scalar_tensor_tensor(out=out, in0=ada_w[slot][:, k, :], scalar=ctmp[:, k:k + 1], in1=src,
                                                 op0=ALU.mult, op1=ALU.add)
                    if k < KD - 1:
                        step(ins)
                    else:
                        ins.then_inc(ada_used.s, 1)

            for m in range(8):
                if m == 4:
                    dve.wait_ge(mod0.s, 1)
                dve.wait_ge(ada_in[m % 2].s, 32 * (m // 2 + 1))
                ada_piece(m % 2, m % 4, link0)
            dve.wait_ge(mod0.s, 2)
            V.tensor_copy(B1[:, :], bank[7][:, 0:8])
            V.scalar_tensor_tensor(out=A1[:, :], in0=bank[7][:, 8:16], scalar=1.0, in1=anorm0[:, :],
                                   op0=ALU.add, op1=ALU.mult).then_inc(mod_ready.s, 1)
            dve.wait_ge(x_in.s, 16)
            dve.sem_inc(x_new.s, TT)

            with dve.Fori(0, L) as l:
                steps[0] = 0

                def step(ins):
                    link(l, ins)

                def tile(key):
                    return ready(dve, l, key)

                def norm(which):
                    a_, b_ = (A1, B1) if which == 1 else (A2, B2)
                    c0 = 4 * (which - 1)
                    wait(dve, rstd_done, l, which)
                    for tt in range(TT):
                        if tt >= 2:
                            wait(dve, tile_ready, l, index[("x", which, tt - 2, 1)] + 1)
                            if which == 2:
                                wait(dve, xn_stored[tt % 2], l, 16)
                        V.tensor_scalar(xn[:, tt % 2, :], x_sb[:, tt, :], rstd[:, c0 + tt:c0 + tt + 1], None,
                                        ALU.mult).then_inc(xn_done.s, 1)
                        if tt >= 1:
                            shift_tile(which, tt - 1, a_, b_)
                    shift_tile(which, TT - 1, a_, b_)

                def shift_tile(which, tt, a_, b_):
                    b = tile(("x", which, tt, 1))
                    for k in range(4):
                        last = V.tensor_scalar(hT[:, 4 + k, tt * P:(tt + 1) * P], b[:, k * P:(k + 1) * P],
                                               a_[:, 4 + k:5 + k], b_[:, 4 + k:5 + k], ALU.mult, ALU.add)
                    last.then_inc(dve_took.s, 1)

                def ada_chunk(n):
                    for m in range(4 * n, 4 * n + 4):
                        wait(dve, ada_in[m % 2], l, 32 * (m // 2 + 1))
                        ada_piece(m % 2, m % 4, step)

                norm(1)
                step(V.tensor_copy(par[:, :], par_all[:, bass.ds(l, 1), :].rearrange("p a n -> p (a n)")))
                wait(dve, tile_ready, l, index[("x", 1, TT - 1, 1)] + 1)
                V.memset(lfx[32:33, :], 1.0)
                ada_chunk(0)
                b = tile(("ada", 0))
                V.tensor_copy(g1_bc[:, 0:512], b[:, :]).then_inc(dve_took.s, 1)
                V.tensor_copy(g1_bc[:, 512:1024], ready(dve, l, ("ada", 0, 1))[:, :]).then_inc(dve_took.s, 1)
                ada_chunk(1)
                b = tile(("ada", 1))
                V.tensor_copy(B2[:, :], b[:, 0:8]).then_inc(dve_took.s, 1)
                ada_chunk(2)
                b = tile(("ada", 2))
                V.scalar_tensor_tensor(out=A2[:, :], in0=b[:, 0:8], scalar=1.0, in1=par[:, 0:8], op0=ALU.add,
                                       op1=ALU.mult).then_inc(dve_took.s, 1)
                ada_chunk(3)
                for i in range(2):
                    b = ready(dve, l, ("ada", 3, i) if i else ("ada", 3))
                    V.tensor_copy(g2_bc[:, i * 512:(i + 1) * 512], b[:, :]).then_inc(dve_took.s, 1)
                for h in range(4):
                    b = tile(("g", h))
                    wait(dve, gexp_done, l, h + 1)
                    step(V.tensor_scalar(sg[:, h, :], sg[:, h, :], 1.0, None, ALU.add))
                    step(V.reciprocal(sg[:, h, :], sg[:, h, :]))
                    V.tensor_tensor(sg[:, h, :], b[:, :], sg[:, h, :], ALU.mult).then_inc(dve_took.s, 1)
                for c in range(TT):
                    b = tile(("z", c))
                    wait(dve, ln_done, l, c + 1)
                    V.scalar_tensor_tensor(out=la[:, c, :], in0=b[:, :], scalar=0.0, in1=rt[:, c % 2, :],
                                           op0=ALU.min, op1=ALU.subtract).then_inc(dve_took.s, 1)
                    wait(dve, dve_took, l, taken[("z", c)][1])
                    dve.sem_inc(la_done.s, 1)
                for c in range(TT):
                    b = tile(("kt", c))
                    wait(dve, act_took, l, taken[("kx", c)][1])
                    V.tensor_tensor(khat[:, c, :].rearrange("p (r n) -> p r n", r=2),
                                    ekx[:, c % 2, :].rearrange("p (r n) -> p r n", r=2), again(b[:, 0:256], 2),
                                    ALU.mult).then_inc(dve_took.s, 1)
                    wait(dve, dve_took, l, taken[("kt", c)][1])
                    dve.sem_inc(khat_done.s, 1)

                def level_diff(n):
                    hh = 1 << LEVELS[n]
                    e = eq.rearrange("p (n a h) -> p n a h", a=2, h=hh)
                    f, g = (bT[:, r, :].rearrange("p (n a h) -> p n a h", a=2, h=hh) for r in range(2))
                    V.tensor_tensor(e[:, :, 1, :], f[:, :, 1, :], rep(f[:, :, 0, hh - 1], hh), ALU.subtract)
                    V.tensor_tensor(e[:, :, 0, :], g[:, :, 0, :], rep(g[:, :, 1, 0], hh), ALU.subtract
                                    ).then_inc(diff_q.s, 1)

                wait(dve, act_took, l, taken[("b", 1, 1)][1])
                level_diff(0)
                wait(dve, dec_done, l, 1)
                for r, c in [(0, 0), (0, 1), (0, 2), (1, 3), (1, 2), (1, 1)]:
                    b = tile(("U", r, c))
                    to = c if r == 0 else c - 1
                    if c in (0, 3):
                        V.tensor_copy(st[:, r, to, :], b[:, 0:256]).then_inc(dve_took.s, 1)
                    else:
                        prev = to - 1 if r == 0 else to + 1
                        for d in range(2):
                            last = V.scalar_tensor_tensor(out=st[:, r, to, d * P:(d + 1) * P],
                                                          in0=st[:, r, prev, d * P:(d + 1) * P],
                                                          scalar=dec[:, r, d * 4 + c:d * 4 + c + 1],
                                                          in1=b[:, d * P:(d + 1) * P], op0=ALU.mult, op1=ALU.add)
                        last.then_inc(dve_took.s, 1)
                    wait(dve, dve_took, l, taken[("U", r, c)][1])
                for half in range(2):
                    rows = slice(64 * half, 64 * half + 64)
                    last = V.tensor_tensor(qd[rows, :, :], qd[rows, :, :], again(qz[rows, half, :], 2), ALU.mult)
                last.then_inc(st_done.s, 1)

                for n, lev in enumerate(LEVELS):
                    wait(dve, exp_q, l, n + 1)
                    if n == 0:
                        wait(dve, zeroed_q, l, 1)
                    else:
                        wait(dve, tile_ready, l, index[("P", LEVELS[n - 1], TT - 1)] + 1)
                    for half in range(2):
                        rows = slice(64 * half, 64 * half + 64)
                        last = V.tensor_tensor(qz_l[rows, half * 1024:(half + 1) * 1024], eq[rows, :], qz[rows, half, :],
                                               ALU.mult)
                    last.then_inc(lev_q.s, 1)
                    wait(dve, lev_q, l, n + 1)
                    if n < 6:
                        level_diff(n + 1)
                    for c in range(TT):
                        b = tile(("P", lev, c))
                        if n == 0:
                            wait(dve, act_took, l, taken[("P", 7, c)][1])
                        pass_on(dve)
                        V.copy_predicated(out=amat[:, c, :, :], mask=again(lvl[:, lev, :], 4),
                                          data=b[:, :].rearrange("p (h i) -> p h i", h=4)).then_inc(dve_took.s, 1)
                    wait(dve, dve_took, l, taken[("P", lev, TT - 1)][1])
                    at = index[("P", lev, TT - 1)] + 1
                    while plan[at][0][0] in ("kn", "kms", "vf", "vt"):
                        key = plan[at][0]
                        at += 1
                        if key[0] == "kms":
                            i = key[1]
                            b = tile(("kn", i))
                            wait(dve, rt_done, l, i + 1)
                            V.scalar_tensor_tensor(
                                out=kn[:, i, :].rearrange("p (c r) -> p r c", r=ROWS),
                                in0=b[:, :].rearrange("p (r c) -> p r c", c=COLS), scalar=par[:, 18:19],
                                in1=rt[:, i % 2, :].rearrange("p (r c) -> p r c", c=COLS), op0=ALU.mult, op1=ALU.mult
                            ).then_inc(dve_took.s, 1)

                def query_tile(i):
                    b = tile(("qn", i))
                    wait(dve, rt_done, l, 4 + i + 1)
                    for half in range(2):
                        rows = slice(64 * half, 64 * half + 64)
                        last = V.scalar_tensor_tensor(
                            out=ap_of(qnz[rows, i, half, :], T - 1, [[-1, ROWS], [-ROWS, COLS]]),
                            in0=b[rows, :].rearrange("p (r c) -> p r c", c=COLS), scalar=qscale[rows, 0:1],
                            in1=rt[rows, i % 2, :].rearrange("p (r c) -> p r c", c=COLS), op0=ALU.mult, op1=ALU.mult)
                    last.then_inc(dve_took.s, 1)

                step(V.tensor_scalar(qscale[:, :], par[:, 17:18], 0.125, None, ALU.mult))
                wait(dve, zeroed_n, l, 1)
                query_tile(0)
                ada_chunk(4)
                b = tile(("ada", 4))
                V.tensor_copy(B1[:, :], b[:, 0:8]).then_inc(dve_took.s, 1)
                query_tile(1)
                query_tile(2)
                query_tile(3)
                ada_chunk(5)
                b = tile(("ada", 5))
                V.scalar_tensor_tensor(out=A1[:, :], in0=b[:, 0:8], scalar=1.0, in1=par[:, 8:16], op0=ALU.add,
                                       op1=ALU.mult).then_inc(dve_took.s, 1)
                for i in range(4):
                    b = tile(("o", i))
                    wait(dve, rt_done, l, 8 + i + 1)
                    V.scalar_tensor_tensor(out=cat[:, i, :], in0=b[:, :], scalar=par[:, 16:17], in1=rt[:, i % 2, :],
                                           op0=ALU.mult, op1=ALU.mult).then_inc(dve_took.s, 1)
                    wait(dve, dve_took, l, taken[("o", i)][1])
                    last = V.tensor_tensor(cat[:, i, :], cat[:, i, :], sg[:, i, :], ALU.mult)
                last.then_inc(cat_g.s, 1)

                for h in range(9):
                    if h < 8:
                        wait(dve, bm_done, l, h + 1)
                        for cb in range(4):
                            if cb % 2 == 0:
                                b = tile(("S", h, cb // 2))
                                pass_on(dve)
                            last = V.tensor_tensor_reduce(
                                out=S_sb[:, h % 2, cb, :], in0=b[:, (cb % 2) * 256:(cb % 2 + 1) * 256],
                                in1=bm[:, h % 2, MASK_OF[cb], :], scale=1.0, scalar=3.0 * NEG,
                                op0=ALU.add, op1=ALU.max, accum_out=mx[:, h % 2, cb:cb + 1])
                            if cb % 2:
                                last.then_inc(dve_took.s, 1)
                        wait(dve, dve_took, l, taken[("S", h, 1)][1])
                        V.tensor_scalar(nmx[:, h % 2, :], mx[:, h % 2, :], -1.0, None, ALU.mult
                                        ).then_inc(smax_done.s, 1)
                    if h >= 1:
                        g = h - 1
                        wait(dve, sexp_done, l, g + 1)
                        step(V.reciprocal(rsm[:, g % 2, :], sm[:, g % 2, :]))
                        V.tensor_tensor(P_sb[:, g % 2, :, :], P_sb[:, g % 2, :, :], rep(rsm[:, g % 2, :], 256), ALU.mult
                                        ).then_inc(prob_done.s, 1)

                for m in range(4):
                    for tt in range(TT):
                        b = tile(("y", m, tt))
                        cols = slice(m * 256, (m + 1) * 256)
                        tmp = pool_c[:, (tt % 2) * 256:(tt % 2 + 1) * 256]
                        V.tensor_tensor(tmp, b[:, 0:256], g1_bc[:, cols], ALU.mult).then_inc(dve_took.s, 1)
                        wait(dve, dve_took, l, taken[("y", m, tt)][1])
                        last = V.tensor_tensor(x_sb[:, tt, cols], x_sb[:, tt, cols], tmp, ALU.add)
                        if m == 3:
                            last.then_inc(x_mid.s, 1)
                norm(2)

                def v4(a):
                    return a.rearrange("p (t g e) -> p (t g) e", g=NG, e=EG)
                score, sel, oh1, oh2, tmp, sel2 = (R[n] for n in ("score", "sel", "oh1", "oh2", "tmp", "sel2"))
                pick1, pick2, mask, rank, dst, ge, t2, t3 = (
                    R[n] for n in ("pick1", "pick2", "mask", "rank", "dst", "ge", "t2", "t3"))
                m1, m2, gs, mf, gh, q4 = (small[i][:, 0:16] for i in range(6))
                gm = small[6][:, 0:4]
                b = tile(("logits",))
                wait(dve, route_exp, l, 1)
                V.tensor_scalar(score, score, 1.0, None, ALU.add).then_inc(dve_took.s, 1)
                wait(dve, dve_took, l, taken[("logits",)][1])
                step(V.reciprocal(score, score))
                step(V.tensor_tensor(sel.rearrange("p (t e) -> p t e", e=NE), score.rearrange("p (t e) -> p t e", e=NE),
                                     again(rb_sb[:, :], TT), ALU.add))

                def first_of(vals, best, n, order, out, scratch):
                    step(V.tensor_tensor(scratch, vals, rep(best, n), ALU.is_equal))
                    step(V.tensor_tensor(scratch, scratch, order, ALU.mult))
                    step(V.tensor_reduce(mf[:, 0:best.shape[1]], scratch, AX, ALU.max))
                    step(V.tensor_tensor(out, scratch, rep(mf[:, 0:best.shape[1]], n), ALU.is_equal))

                order8 = again(iota8[:, 0:EG], TT * NG)
                step(V.tensor_reduce(m1, v4(sel), AX, ALU.max))
                first_of(v4(sel), m1, EG, order8, v4(oh1), v4(tmp))
                step(V.scalar_tensor_tensor(out=sel2, in0=oh1, scalar=NEG, in1=sel, op0=ALU.mult, op1=ALU.add))
                step(V.tensor_reduce(m2, v4(sel2), AX, ALU.max))
                first_of(v4(sel2), m2, EG, order8, v4(oh2), v4(tmp))
                step(V.tensor_tensor(gs, m1, m2, ALU.add))
                gs_v = gs.rearrange("p (t g) -> p t g", g=NG)
                step(V.tensor_reduce(gm, gs_v, AX, ALU.max))
                first_of(gs_v, gm, NG, again(iota4[:, :], TT), gh.rearrange("p (t g) -> p t g", g=NG),
                         q4.rearrange("p (t g) -> p t g", g=NG))
                step(V.tensor_tensor(v4(pick1), v4(oh1), rep(gh, EG), ALU.mult))
                step(V.tensor_tensor(v4(pick2), v4(oh2), rep(gh, EG), ALU.mult))
                V.tensor_tensor(mask, pick1, pick2, ALU.add).then_inc(mask_done.s, 1)
                def te(a):
                    return a.rearrange("p (t e) -> p t e", e=NE)
                for j, pk in enumerate((pick1, pick2)):
                    step(V.tensor_tensor(tmp, pk, score, ALU.mult))
                    step(V.tensor_reduce(gwt[:, j, :], te(tmp), AX, ALU.add))
                wsum = small[7][:, 0:4]
                step(V.tensor_tensor(wsum, gwt[:, 0, :], gwt[:, 1, :], ALU.add))
                step(V.reciprocal(wsum, wsum))
                step(V.tensor_tensor(gwt[:, :, :], gwt[:, :, :], again(wsum, 2), ALU.mult))
                b = tile(("rank",))
                step(V.tensor_copy(rank, b[:, 0:128]))
                cntT, cnt = small[8], small[9]
                step(V.tensor_copy(cnt, b[:, 128:160]))
                V.tensor_copy(cntT[0:NE, 0:1], b[0:NE, 160:161]).then_inc(dve_took.s, 1)
                wait(dve, dve_took, l, taken[("rank",)][1])
                thr = small[10]
                step(V.tensor_scalar(thr[:, 0:7], iota_s[:, 1:8], 64.0, None, ALU.mult))
                novT, c7 = small[11], small[12]
                step(V.tensor_tensor(c7[0:NE, 0:7], rep(cntT[0:NE, 0], 7), thr[0:NE, 0:7], ALU.is_gt))
                step(V.tensor_reduce(novT[0:NE, 0:1], c7[0:NE, 0:7], AX, ALU.add))
                V.tensor_scalar(t3[0:NE, :], ones[0:NE, :], novT[0:NE, 0:1], None, ALU.mult).then_inc(over_in.s, 1)
                cmp7 = wide.rearrange("p b e -> p (b e)")[:, 0:NE * 7].rearrange("p (e m) -> p e m", m=7)
                step(V.tensor_tensor(cmp7, rep(cnt, 7), again(thr[:, 0:7], NE), ALU.is_gt))
                nov = small[13]
                step(V.tensor_reduce(nov, cmp7, AX, ALU.add))
                b = tile(("over",))
                before_e, total = small[14], small[15]
                step(V.tensor_copy(before_e, b[:, 0:NE]))
                V.tensor_copy(total[:, 0:1], b[:, NE:NE + 1]).then_inc(dve_took.s, 1)
                wait(dve, dve_took, l, taken[("over",)][1])
                upto_e, ex = small[16], small[17]
                step(V.tensor_tensor(upto_e, before_e, nov, ALU.add))
                step(V.tensor_tensor(wide, again(upto_e, MAXOV), rep(iota_s[:, 0:MAXOV], NE), ALU.is_le))
                step(V.tensor_reduce(ex[:, 0:MAXOV], wide, AX, ALU.add))
                step(V.tensor_scalar(ex[:, 0:MAXOV], ex[:, 0:MAXOV], float(NE - 1), None, ALU.min))
                V.tensor_copy(ov_exp[:, :], ex[:, 0:MAXOV])
                V.tensor_copy(ov_pair[:, 1:2], total[:, 0:1])
                step(V.tensor_copy(ov_pair[:, 0:1], ov_f[:, 0:1]))
                step(V.tensor_tensor(ov_f[:, 0:1], ov_f[:, 0:1], total[:, 0:1], ALU.add))
                shift_e = small[18]
                step(V.tensor_scalar(shift_e, before_e, float(NE - 1), 64.0, ALU.add, ALU.mult))
                step(V.tensor_tensor(shift_e, shift_e, iota_e[:, :], ALU.subtract))
                step(V.tensor_scalar(ge, rank, float(SLOTS), None, ALU.is_ge))
                step(V.tensor_tensor(te(ge), te(ge), again(shift_e, TT), ALU.mult))
                step(V.tensor_tensor(dst, rank, ge, ALU.add))
                step(V.tensor_tensor(te(dst), te(dst), again(iota_e[:, :], TT), ALU.add))
                rowf = small[19][:, 0:8]
                for j, pk in enumerate((pick1, pick2)):
                    step(V.tensor_tensor(tmp, pk, dst, ALU.mult))
                    step(V.tensor_reduce(rowf[:, j * 4:(j + 1) * 4], te(tmp), AX, ALU.add))
                row_v = row_of[:, :, :].rearrange("p j t -> p (j t)")
                step(V.tensor_copy(row_v, rowf))
                ia, fa = (small[20][:, 0:8].bitcast(I32), small[21][:, 0:8])
                ib, fb = (small[22][:, 0:8].bitcast(I32), small[23][:, 0:8])
                step(V.tensor_scalar(ia, row_v, 6, None, ALU.arith_shift_right))
                step(V.tensor_scalar(ib, row_v, SLOTS - 1, None, ALU.bitwise_and))
                step(V.tensor_copy(fa, ia))
                step(V.tensor_copy(fb, ib))
                step(V.tensor_tensor(oslot, again(iota_s[:, :], 8), rep(fb, SLOTS), ALU.is_equal))
                step(V.tensor_tensor(oblk, again(iota_s[:, 0:NBLK], 8), rep(fa, NBLK), ALU.is_equal))
                V.tensor_tensor(oblk, oblk, rep(tok8[:, :], NBLK), ALU.mult).then_inc(slot1h.s, 1)
                b = tile(("slot",))
                V.tensor_copy(slot_tok[:, :], b[0:SLOTS, 0:NBLK]).then_inc(dve_took.s, 1)
                wait(dve, dve_took, l, taken[("slot",)][1])
                dve.sem_inc(routed.s, 1)
                ov0, nov = reg_counts(dve)

                def expert_block(u, G, back):
                    def own(ins, n):
                        ins.then_inc(dve_blk.s, 1)
                        dve.wait_ge(dve_blk.s, G * 4 + n)
                    b = bank[u][:, :].rearrange("p (k s) -> p k s", k=KD)
                    wait_blk(dve, "xg_T", G, 1)
                    wait_blk(dve, "up_ready", G, 1 - back)
                    own(V.tensor_tensor(hgT[:, u, :, :], b, rep(A2[:, :], SLOTS), ALU.mult), 1)
                    V.tensor_tensor(hgT[:, u, :, :], hgT[:, u, :, :], rep(B2[:, :], SLOTS), ALU.add
                                    ).then_inc(blk["hg_done"].s, 1)
                    wait_blk(dve, "up_exp", G, 1)
                    e1 = sil[:, u, 0:256]
                    own(V.tensor_scalar(e1, e1, 1.0, None, ALU.add), 2)
                    own(V.reciprocal(e1, e1), 3)
                    own(V.tensor_tensor(e1, bank[2 + u][:, 0:256], e1, ALU.mult), 4)
                    V.tensor_tensor(sil[:, u, 256:512], e1, bank[2 + u][:, 256:512], ALU.mult
                                    ).then_inc(blk["g_done"].s, 1)

                with dve.Fori(0, NE // 2) as i:
                    for u in range(2):
                        expert_block(u, l * NE + ov0 + i * 2 + u, 2)
                with dve.If(nov > 0):
                    with dve.Fori(0, nov) as j:
                        expert_block(0, l * NE + NE + ov0 + j, 1)

                for tt in range(TT):
                    u = tt % 2
                    wait(dve, yrows_in[u], l, 32 * (tt // 2 + 1))
                    y0, y1 = yg[:, u, 0, :], yg[:, u, 1, :]
                    step(V.tensor_scalar(y0, y0, gwt[:, 0, tt:tt + 1], None, ALU.mult))
                    step(V.scalar_tensor_tensor(out=y0, in0=y1, scalar=gwt[:, 1, tt:tt + 1], in1=y0, op0=ALU.mult,
                                                op1=ALU.add))
                    step(V.tensor_tensor(y0, y0, g2_bc[:, :], ALU.mult))
                    V.tensor_tensor(x_sb[:, tt, :], x_sb[:, tt, :], y0, ALU.add).then_inc(x_new.s, 1)
            assert steps[0] == DVE_STEPS, steps

        @block.gpsimd
        def _(pool):
            G_ = nc.gpsimd
            n0 = [0]
            steps = [0]

            def link0(ins):
                n0[0] += 1
                ins.then_inc(pstep.s, 1)
                pool.wait_ge(pstep.s, n0[0])

            def link(l, ins):
                steps[0] += 1
                ins.then_inc(pool_step.s, 1)
                wait(pool, pool_step, l, steps[0])

            G_.memset(pool_b[:, 0:D], 0.0).then_inc(y_zeros.s, 1)
            for t_ in (ident, upto, since, after, before):
                last = G_.memset(t_[:, :], 0.0 if t_ is ident else 1.0)
            link0(last)
            for t_, op, fill, cm, st_, base in ((ident, ALU.not_equal, 1.0, 1, -1, 0),
                                                (upto, ALU.is_ge, 0.0, -1, 1, 0),
                                                (since, ALU.is_ge, 0.0, 1, -1, 0),
                                                (after, ALU.is_gt, 0.0, 1, -1, 0),
                                                (before, ALU.is_gt, 0.0, -1, 1, 0)):
                last = G_.affine_select(out=t_[:, :], in_=t_[:, :], compare_op=op, fill=fill, base=base,
                                        pattern=[[st_, P]], channel_multiplier=cm)
            link0(last)
            G_.iota(io_p[:, :], pattern=[[0, P]], base=0, channel_multiplier=1)
            G_.iota(io_f[:, :], pattern=[[1, P]], base=0, channel_multiplier=0)
            G_.iota(io_8[:, :], pattern=[[-1, EG]], base=EG, channel_multiplier=0)
            link0(G_.iota(io_t[:, :], pattern=[[0, 2], [P, TT]], base=0, channel_multiplier=1))
            link0(G_.iota(io_e[:, :], pattern=[[SLOTS, NE]], base=0, channel_multiplier=0))
            G_.tensor_copy(iota_s[:, :], io_f[:, 0:64])
            G_.tensor_copy(iota8[:, 0:EG], io_8[:, :])
            G_.tensor_copy(iota4[:, :], io_8[:, 4:8])
            G_.tensor_copy(tok8[:, :], io_t[:, :])
            link0(G_.tensor_copy(iota_e[:, :], io_e[:, :]))
            pool.sem_inc(consts_p.s, 1)
            pool.sem_inc(blk["y_saved"].s, 2)

            with pool.Fori(0, L) as l:
                steps[0] = 0
                pool.wait_ge(x_new.s, l * TT + TT)
                pass_on(pool)
                for half in range(2):
                    rows = slice(64 * (1 - half), 64 * (1 - half) + 64)
                    G_.memset(qz[rows, half, :], 0.0)
                    last = G_.memset(qz_l[rows, half * 1024:(half + 1) * 1024], 0.0)
                last.then_inc(zeroed_q.s, 1)
                wait(pool, zeroed_q, l, 1)
                pool.wait_ge(y_zeroed.s, 16)
                wait(pool, act_took, l, taken[("b", 1, 1)][1])
                for n, lev in enumerate(LEVELS):
                    hh = 1 << lev
                    e = ek2.rearrange("p (n a h) -> p n a h", a=2, h=hh)
                    f, g = (bT[:, r, :].rearrange("p (n a h) -> p n a h", a=2, h=hh) for r in range(2))
                    G_.tensor_tensor(e[:, :, 0, :], rep(f[:, :, 0, hh - 1], hh), f[:, :, 0, :], ALU.subtract)
                    G_.tensor_tensor(e[:, :, 1, :], rep(g[:, :, 1, 0], hh), g[:, :, 1, :], ALU.subtract
                                     ).then_inc(diff_k.s, 1)
                    wait(pool, exp_k, l, n + 1)
                    if n > 0:
                        wait(pool, tile_ready, l, index[("P", LEVELS[n - 1], TT - 1)] + 1)
                    G_.tensor_tensor(kz_l, ek2, kT, ALU.mult).then_inc(lev_k.s, 1)
                    wait(pool, lev_k, l, n + 1)
                wait(pool, tile_ready, l, index[("P", 0, TT - 1)] + 1)
                pass_on(pool)
                for half in range(2):
                    rows = slice(64 * (1 - half), 64 * (1 - half) + 64)
                    last = G_.memset(qnz[rows, :, half, :], 0.0)
                last.then_inc(zeroed_n.s, 1)
                wait(pool, zeroed_n, l, 1)
                wait(pool, gtab_in, l, 16 * 8)
                for h in range(8):
                    if h >= 2:
                        wait(pool, smax_done, l, h - 1)
                    for m in range(3):
                        src = ap_of(gtab[:, h, :], RPB_PAD - 8 * m, [[1, 32], [31, ROWS]])
                        last = G_.tensor_tensor(bm[:, h % 2, m, :].rearrange("p (c r) -> p c r", r=ROWS), src,
                                                rep(wneg[:, m, :], ROWS), ALU.add)
                    last.then_inc(bm_done.s, 1)

                wait(pool, bm_done, l, 8)
                wait(pool, routed, l, 1)
                for i in range(2):
                    wait(pool, xn_stored[i], l, 32)
                ov0, nov = reg_counts(pool)

                def gather(u, G, row, back):
                    wait_blk(pool, "xg_T", G, 1 - back)
                    pass_on(pool)
                    G_.tensor_copy(tok_now[:, u:u + 1], slot_tok[:, bass.ds(row, 1)]).then_inc(tok_set.s, 1)
                    pool.wait_ge(tok_set.s, G + 1)
                    pass_on(pool)
                    G_.indirect_dma_start(xg[:, u, :], None, xn_dram, bass.IndirectOffsetOnAxis(tok_now[:, u:u + 1], 0)
                                          ).then_inc(gathered[u].s, 16)

                def saved(u, uses):
                    pool.wait_ge(y_stored[u].s, uses * 32 + 32)
                    pool.sem_inc(blk["y_saved"].s, 1)

                base = l * NE + ov0
                half_l = l * (NE // 2)
                gather(0, base, 0, 2)
                gather(1, base + 1, 1, 2)
                with pool.Fori(0, NE // 2 - 1) as i:
                    saved(0, half_l + ov0 + i)
                    gather(0, base + i * 2 + 2, i * 2 + 2, 2)
                    saved(1, half_l + i)
                    gather(1, base + i * 2 + 3, i * 2 + 3, 2)
                saved(0, half_l + ov0 + (NE // 2 - 1))
                saved(1, half_l + (NE // 2 - 1))
                with pool.If(nov > 0):
                    with pool.Fori(0, nov) as j:
                        gather(0, base + NE + j, j + NE, 1)
                        saved(0, half_l + ov0 + (NE // 2) + j)
                for tt in range(TT):
                    if tt >= 2:
                        pool.wait_ge(x_new.s, l * TT + TT + tt - 1)
                        pass_on(pool)
                    for j in range(2):
                        G_.indirect_dma_start(yg[:, tt % 2, j, :], None, y_dram,
                                              bass.IndirectOffsetOnAxis(row_of[:, j, tt:tt + 1], 0)
                                              ).then_inc(yrows_in[tt % 2].s, 16)
            assert steps[0] == POOL_STEPS, steps


_INS = ["x", "c", "w_ada", "b_ada", "attn_norm", "ffn_norm", "w_in", "gla_gate_w", "gla_gate_b", "gla_out_norm",
        "na_q_norm", "na_k_norm", "na_rpb", "w_out", "router_w", "router_b", "w1", "w3", "w2"]


def kernel(**inputs):
    import numpy as np
    import concourse.bacc as bacc
    from concourse.bass_utils import run_bass_kernel_spmd

    nc = bacc.Bacc("TRN2", target_bir_lowering=False, num_devices=1)
    arrays, aps = {}, {}
    for name in _INS:
        a = np.ascontiguousarray(inputs[name])
        arrays[name] = a
        aps[name] = nc.dram_tensor(name, a.shape, mybir.dt.from_np(a.dtype), kind="ExternalInput").ap()
    aps["out"] = nc.dram_tensor("out", (1, T, D), F32, kind="ExternalOutput").ap()
    build(nc, aps)
    r = run_bass_kernel_spmd(nc, [arrays], core_ids=[0])
    return r.results[0]["out"]
```

```python
from contextlib import ExitStack

import concourse.bass as bass
from concourse import mybir

F32 = mybir.dt.float32
I32 = mybir.dt.int32
ALU = mybir.AluOpType
ACT = mybir.ActivationFunctionType
AX = mybir.AxisListType.X

P = 128
T = 512
D = 1024
L = 2
KD = D // P
TT = T // P
ROWS, COLS = 8, 64
NE, NG, EG = 32, 4, 8
DE = 512
SLOTS = 64
MAXOV = 2 * T // SLOTS
NBLK = NE + MAXOV
EPS = 1e-6
NEG = -1e30
TAU_INV = 1.0 / 16.0
C_QK, C_V, C_G, C_LF, C_QN, C_KN, C_VN = 0, 512, 1024, 1536, 1568, 2080, 2592
IN_W = 3104
RPB_W = 15 * 31
RPB_PAD = 16
KEY_AT = [0, 1, 3, 4]
RPB_OFF = [0, -8, -8, -16]
MASK_OF = [0, 1, 1, 2]
LEVELS = [6, 5, 4, 3, 2, 1, 0]
FILLERS = ("kn", "kms", "vf", "vt", "ada")
RING = 6
NPAR = 19
ADA_PIECES = 24
WIN_PIECES = 12
DVE_STEPS, ACT_STEPS, POOL_STEPS = 263, 18, 0



class Signal:

    def __init__(self, nc, ctx, name, per, first=0):
        self.s = ctx.enter_context(nc.semaphore(name))
        self.per, self.first = per, first

    def at(self, l, n):
        return l * self.per + self.first + n


def tile_plan():
    t = [(("x", 1, tt, h), "ad"[h]) for tt in range(TT) for h in range(2)]
    t += [(("q", d), "a") for d in range(2)] + [(("ada", 0), "d"), (("ada", 0, 1), "d")]
    t += [(("k", d), "a") for d in range(2)] + [(("lf",), "a"), (("ada", 1), "d")]
    t += [(("v", 0, c), "a") for c in range(TT)] + [(("ada", 2), "d")]
    t += [(("v", 1, c), "a") for c in range(TT)] + [(("ada", 3), "d"), (("ada", 3, 1), "d")]
    t += [(("g", h), "d") for h in range(4)]
    t += [(("z", c), "d") for c in range(TT)]
    t += [(("b", r, d), "a") for r in range(2) for d in range(2)]
    for c in range(TT):
        t += [(("kx", c), "a"), (("kt", c), "d")]
    t += [(("U", 0, c), "d") for c in (0, 1, 2)] + [(("U", 1, c), "d") for c in (3, 2, 1)]
    t += [(("P", 7, c), "a") for c in range(TT)]
    fill = [[("kn", 0)], [("kms", 0), ("kn", 1)], [("kms", 1), ("kn", 2)], [("kms", 2), ("kn", 3)],
            [("kms", 3), ("ada", 4), ("vf", 0)], [("vf", 1), ("vt", 0, 0), ("vt", 0, 1)],
            [("vf", 2), ("vt", 1, 0), ("vt", 1, 1), ("vf", 3), ("vt", 2, 0), ("vt", 2, 1), ("vt", 3, 0), ("vt", 3, 1)]]
    who = {"kn": "d", "ada": "d", "kms": "a", "vf": "a", "vt": "a"}
    for n, lev in enumerate(LEVELS):
        t += [(("P", lev, c), "d") for c in range(TT)]
        t += [(k, who[k[0]]) for k in fill[n]]
    for pre in ("qn", "o"):
        ms = pre[0] + "ms"
        t += [((pre, 0), "d"), ((pre, 1), "d"), ((ms, 0), "a")]
        t += [((pre, 2), "d"), ((ms, 1), "a"), ((pre, 3), "d"), ((ms, 2), "a"), ((ms, 3), "a")]
        t += [(("ada", 5), "d")] if pre == "qn" else []
    for h in range(10):
        if h < 8:
            t += [(("S", h, i), "d") for i in range(2)]
        if h >= 2:
            t += [(("PT", h - 2, i), "a") for i in range(2)]
    t += [(("y", m, tt), "d") for m in range(4) for tt in range(TT)]
    t += [(("x", 2, tt, h), "ad"[h]) for tt in range(TT) for h in range(2)]
    t += [(("logits",), "d"), (("rank",), "d"), (("over",), "d"), (("slot",), "d")]
    return t


def build(nc, A):
    plan = tile_plan()
    index = {key: n for n, (key, _) in enumerate(plan)}
    taken, seen = {}, {"a": 0, "d": 0}
    mean_of = {"kn": "kms", "qn": "qms", "o": "oms"}
    order = sorted(plan, key=lambda e: index[(mean_of[e[0][0]], e[0][1])] + 0.5 if e[0][0] in mean_of else index[e[0]])
    for key, who in order:
        seen[who] += 1
        taken[key] = (who, seen[who])

    with ExitStack() as ctx:
        def sb(name, shape, dt=F32):
            return ctx.enter_context(nc.sbuf_tensor(name, shape, dt))

        def sig(name, per, first=0):
            return Signal(nc, ctx, name, per, first)

        ring = sb("ring", [P, 6, 4096])
        x_sb = sb("x_sb", [P, TT, D])
        hT = sb("hT", [P, KD, T])
        pool_a = sb("pool_a", [P, 6656])
        pool_b = sb("pool_b", [P, 5632])
        pool_c = sb("pool_c", [P, 2048])
        g1_bc = sb("g1_bc", [P, D])
        g2_bc = sb("g2_bc", [P, D])
        acc = sb("acc", [P, D])
        brow = sb("brow", [P, 2, 256])
        ident = sb("ident", [P, P])
        ones = sb("ones", [P, P])
        mean64 = sb("mean64", [P, P])
        upto = sb("upto", [P, P])
        since = sb("since", [P, P])
        after = sb("after", [P, P])
        before = sb("before", [P, P])
        lvl = sb("lvl", [P, 7, P], mybir.dt.uint8)
        par_all = sb("par_all", [P, L, NPAR])
        par = sb("par", [P, NPAR])
        anorm0 = sb("anorm0", [P, KD])
        c_sb = sb("c_sb", [P, KD])
        A1, B1 = sb("A1", [P, KD]), sb("B1", [P, KD])
        A2, B2 = sb("A2", [P, KD]), sb("B2", [P, KD])
        eps_c = sb("eps_c", [P, 1])
        gatew = sb("gatew", [33, 512])
        rw_sb = sb("rw_sb", [P, KD, NE])
        rb_sb = sb("rb_sb", [P, NE])
        ssq = sb("ssq", [P, 8])
        rstd = sb("rstd", [P, 8])
        mx = sb("mx", [P, 2, 4])
        nmx = sb("nmx", [P, 2, 4])
        sm = sb("sm", [P, 2, 4])
        rsm = sb("rsm", [P, 2, 4])
        dec = sb("dec", [P, 2, 8])
        gwt = sb("gwt", [P, 2, TT])
        row_of = sb("row_of", [P, 2, TT], I32)
        slot_tok = sb("slot_tok", [SLOTS, NBLK], I32)
        tok_now = sb("tok_now", [SLOTS, 2], I32)
        wneg = sb("wneg", [P, 3, 32])
        pairs = sb("pairs", [P, 2], I32)
        pairs_f = sb("pairs_f", [P, 1])
        one_c = sb("one_c", [P, 1])
        pad0 = sb("pad0", [L, RPB_PAD])
        ctmp = sb("ctmp", [P, KD])
        qscale = sb("qscale", [P, 1])
        lo = sb("lo", [P, 4])
        tok8 = sb("tok8", [P, 8])

        flat = ring[:, :, :].rearrange("p s n -> p (s n)")
        win_w = [flat[:, i * 2048:(i + 1) * 2048].rearrange("p (k n) -> p k n", k=KD) for i in range(2)]
        ada_w = [v[:, a:a + 2048].rearrange("p (k n) -> p k n", k=KD)
                 for v, a in ((flat, 4096), (flat, 6144), (pool_b, 0), (pool_b, 2048))]
        bias_row = [brow[:, 0, :], brow[:, 1, :], pool_b[:, 4608:4864], pool_b[:, 4864:5120]]
        Z = 8192

        def z(n):
            nonlocal Z
            Z += n
            return flat[:, Z - n:Z]
        eq, ek2, qz_l, kz_l = z(1024), z(1024), z(2048), z(1024)
        wlf = ek2[:, 0:256].rearrange("p (k n) -> p k n", k=KD)
        qnz = flat[:, 8192:8192 + 4096].rearrange("p (d r t) -> p d r t", d=4, r=2)
        la = z(2048).rearrange("p (c n) -> p c n", c=TT)
        amat = la.rearrange("p c n -> p (c n)").rearrange("p (c h i) -> p c h i", c=TT, h=4)
        ekx = z(1024).rearrange("p (u n) -> p u n", u=2)
        bT = z(2048).rearrange("p (r n) -> p r n", r=2)
        khat = z(2048).rearrange("p (c n) -> p c n", c=TT)
        zeros_y = bT[:, 0, :]
        q_lev = [qz_l, khat.rearrange("p c n -> p (c n)")]
        k_lev = [kz_l, ek2]
        gtab = flat[:, Z - 4096:Z - 4096 + 8 * 265].rearrange("p (h m) -> p h m", h=8)
        bm = flat[:, Z - 4096 + 2120:Z - 4096 + 2120 + 1536].rearrange("p (u s n) -> p u s n", u=2, s=3)
        v_tm = z(2048).rearrange("p (c n) -> p c n", c=TT)
        sg = z(2048).rearrange("p (h n) -> p h n", h=4)
        assert Z == 6 * 4096
        cat = hT
        qz = pool_a[:, 0:2048].rearrange("p (r n) -> p r n", r=2)
        kT = pool_a[:, 2048:3072]
        qd = pool_a[:, 3072:5120].rearrange("p (r n) -> p r n", r=2)
        st = pool_a[:, 5120:6656].rearrange("p (r c n) -> p r c n", r=2, c=3)
        P_sb = pool_a[:, 0:3072].rearrange("p (u c n) -> p u c n", u=3, c=4)
        PT_sb = pool_a[:, 4096:6144].rearrange("p (u c n) -> p u c n", u=2, c=4)
        xg = pool_a[0:SLOTS, 0:2048].rearrange("p (u n) -> p u n", u=2)
        hgT = pool_a[:, 2048:3072].rearrange("p (u k s) -> p u k s", u=2, k=KD)
        sil = pool_a[:, 3072:4096].rearrange("p (u n) -> p u n", u=2)
        gTs = pool_a[:, 4096:4608].rearrange("p (u n) -> p u n", u=2)
        y_sb = pool_a[:, 4608:5632].rearrange("p (u n) -> p u n", u=2)
        kn = pool_b[:, 0:2048].rearrange("p (d t) -> p d t", d=4)
        vn = pool_b[:, 2048:5632].rearrange("p (n f) -> p n f", n=7)
        sq = pool_c[:, 0:1024].rearrange("p (u n) -> p u n", u=2)
        rt = pool_c[:, 1024:2048].rearrange("p (u n) -> p u n", u=2)
        lfx = pool_c[0:33, 0:512]
        xn = pool_c[:, :].rearrange("p (u n) -> p u n", u=2)
        yg = hT[:, :, :].rearrange("p k t -> p (k t)").rearrange("p (u j n) -> p u j n", u=2, j=2)
        w13 = [[ring[:, 3 * u + i, :].rearrange("p (k n) -> p k n", k=KD) for i in range(2)] for u in range(2)]
        w2s = [ring[:, 3 * u + 2, :].rearrange("p (h q n) -> p h q n", h=2, q=2) for u in range(2)]

        def rt_at(a, n, dt=F32):
            v = pool_b[:, a:a + n]
            return v if dt == F32 else v.bitcast(dt)
        R = {name: rt_at(i * 128, 128) for i, name in enumerate(
            ("score", "sel", "oh1", "oh2", "tmp", "sel2", "first", "lin", "pick1", "pick2", "mask",
             "rank", "dst", "ge", "t2", "t3"))}
        small = [rt_at(2048 + i * 32, 32) for i in range(24)]
        oslot = rt_at(2816, 8 * 64).rearrange("p (j n) -> p j n", j=8)
        oblk = rt_at(3328, 8 * NBLK).rearrange("p (j n) -> p j n", j=8)
        wide = rt_at(3712, MAXOV * NE).rearrange("p (b e) -> p b e", b=MAXOV)
        blk_exp = rt_at(4224, NBLK, I32)
        iota8 = sb("iota8", [P, NE])
        iota4 = sb("iota4", [P, NG])
        iota_e = sb("iota_e", [P, NE])
        iota_s = sb("iota_s", [P, 64])
        io_p, io_f, xor, xsh = (pool_c[:, i * P:(i + 1) * P].bitcast(I32) for i in range(4))
        xfl = pool_c[:, 512:640]
        io_8, io_t, io_e = (pool_c[:, a:b].bitcast(I32) for a, b in ((640, 648), (648, 656), (656, 688)))

        bank = [ctx.enter_context(nc.psum_tensor(f"bank{i}", [P, 512], F32)) for i in range(8)]

        rpb_pad = nc.dram_tensor("rpb_padded", [L, 8 * RPB_W + 2 * RPB_PAD], F32).ap()
        xn_dram = nc.dram_tensor("xn_rows", [T, D], F32).ap()
        y_dram = nc.dram_tensor("y_rows", [NBLK * SLOTS, D], F32).ap()

        tile_ready = sig("tile_ready", len(plan))
        act_took = sig("act_took", seen["a"])
        dve_took = sig("dve_took", seen["d"])
        dve_step = sig("dve_step", DVE_STEPS)
        act_step = sig("act_step", ACT_STEPS)
        pool_step = sig("pool_step", POOL_STEPS)
        consts_p, consts_v = sig("consts_p", 0), sig("consts_v", 0)
        zeros_done, pads_done, rpb_copied = sig("zeros_done", 0), sig("pads_done", 0), sig("rpb_copied", 0)
        x_in, par_in = sig("x_in", 0), sig("par_in", 0)
        c_act = sig("c_act", 0)
        x_new = sig("x_new", TT, TT)
        mod0 = sig("mod0", 0)
        mod_ready = sig("mod_ready", 0)
        win_in = [sig(f"win_in{i}", 16 * WIN_PIECES // 2) for i in range(2)]
        lf_in, gatew_in, gtab_in = sig("lf_in", 16), sig("gatew_in", 48), sig("gtab_in", 16 * 8)
        ada_in = [sig(f"ada_in{i}", 32 * (8 if i < 2 else 4), 32 * 2) for i in range(4)]
        bias_zero = sig("bias_zero", 1)
        ada_used = sig("ada_used", ADA_PIECES, 8)
        wo_in = [sig(f"wo_in{i}", 32) for i in range(2)]
        rstd_done = sig("rstd_done", 2)
        xn_done = sig("xn_done", 8)
        xn_stored = [sig(f"xn_stored{i}", 32) for i in range(2)]
        zeroed_q = sig("zeroed_q", 1)
        zeroed_l = sig("zeroed_l", 1)
        zeroed_n = sig("zeroed_n", 1)
        ln_done, gexp_done = sig("ln_done", 4), sig("gexp_done", 4)
        sg_done = sig("sg_done", 1)
        la_done = sig("la_done", 4)
        dec_done = sig("dec_done", 1)
        ekx_done, khat_done = sig("ekx_done", 4), sig("khat_done", 4)
        st_done = sig("st_done", 1)
        diff_q, diff_k = sig("diff_q", 7), sig("diff_k", 7)
        exp_q, exp_k = sig("exp_q", 7), sig("exp_k", 7)
        lev_q, lev_k = sig("lev_q", 7), sig("lev_k", 7)
        sq_done, rt_done = sig("sq_done", 12), sig("rt_done", 12)
        cat_g = sig("cat_g", 1)
        bm_done = sig("bm_done", 8)
        smax_done, sexp_done = sig("smax_done", 8), sig("sexp_done", 8)
        prob_done = sig("prob_done", 8)
        on_done = sig("on_done", 4)
        cat_n = sig("cat_n", 4)
        x_mid = sig("x_mid", TT)
        mask_done, over_in, slot1h = sig("mask_done", 1), sig("over_in", 1), sig("slot1h", 1)
        routed = sig("routed", 1)
        blk = {n: sig(n, 0) for n in ("xg_T", "hg_done", "up_ready", "up_exp", "g_done", "gT_ready",
                                      "gTs_done", "y_ready", "y_evac")}
        dve_blk = sig("dve_blk", 0)
        w_blk = [[sig(f"{n}_in{u}", 0) for n in ("w1", "w3", "w2")] for u in range(2)]
        gathered = [sig(f"gathered{u}", 0) for u in range(2)]
        tok_set = sig("tok_set", 0)
        y_stored = [sig(f"y_stored{u}", 0) for u in range(2)]
        yrows_in = [sig(f"yrows_in{u}", 64) for u in range(2)]
        out_done = sig("out_done", 0)
        y_zeros, y_zeroed = sig("y_zeros", 0), sig("y_zeroed", 0)
        cstep, pstep = sig("cstep", 0), sig("pstep", 0)
        route_exp = sig("route_exp", 1)

        def wait(eng, s, l, n):
            assert s.first + n > 0
            eng.wait_ge(s.s, s.at(l, n))

        def ready(eng, l, key):
            wait(eng, tile_ready, l, index[key] + 1)
            return bank[index[key] % RING]

        passed = {id(e): sig(n, 0) for e, n in ((nc.sync, "passed_sp"), (nc.tensor, "passed_pe"),
                                                (nc.scalar, "passed_act"), (nc.vector, "passed_dve"),
                                                (nc.gpsimd, "passed_pool"))}
        block = ctx.enter_context(nc.Block())


        def pass_on(eng):
            eng.sem_inc(passed[id(eng)].s, 1)

        def wait_blk(eng, name, G, n):
            eng.wait_ge(blk[name].s, G + (2 + n))

        def free_bank(pe, l, key):
            n = index[key]
            if n >= RING:
                who, count = taken[plan[n - RING][0]]
                wait(pe, act_took if who == "a" else dve_took, l, count)
            return bank[n % RING]

        def reg_counts(eng):
            pass_on(eng)
            return (eng.value_load(pairs[0:1, 0:1], min_val=0, max_val=L * NBLK // 2),
                    eng.value_load(pairs[0:1, 1:2], min_val=NE // 2 - 1, max_val=NBLK // 2 - 1))

        def ap_of(v, off, dims):
            return bass.AP(tensor=v.tensor, offset=v.offset + off, ap=[v.ap[0]] + dims)

        def rep(v, n):
            return bass.AP(tensor=v.tensor, offset=v.offset, ap=list(v.ap) + [[0, n]])

        def again(v, n):
            return bass.AP(tensor=v.tensor, offset=v.offset, ap=[v.ap[0], [0, n]] + list(v.ap[1:]))

        ada_cols = [2048 + 256 * m for m in range(16)] + [256 * m for m in range(8)]
        win_cols = [0, 256, C_V, C_V + 256, C_G, C_G + 256, C_KN, C_KN + 256, C_VN, C_VN + 256, C_QN, C_QN + 256]
        last_of_piece = [("q", 1), ("k", 1), ("v", 0, 3), ("v", 1, 3), ("g", 1), ("g", 3), ("kn", 1), ("kn", 3),
                         ("vf", 1), ("vf", 3), ("qn", 1), ("qn", 3)]
        w_ada_v = A["w_ada"].rearrange("l (p k) n -> l p k n", k=KD)
        w_in_v = A["w_in"].rearrange("l (p k) n -> l p k n", k=KD)
        w_out_v = A["w_out"].rearrange("l (k p) n -> l p k n", p=P)
        w1_v = A["w1"].rearrange("l e (p k) n -> (l e) p (k n)", k=KD)
        w3_v = A["w3"].rearrange("l e (p k) n -> (l e) p (k n)", k=KD)
        w2_v = A["w2"].rearrange("l e (h p q) n -> (l e) p h (q n)", h=2, q=2)
        y_blk = y_dram.rearrange("(b s) (h n) -> b h s n", s=SLOTS, h=2)

        @block.sync
        def _(sp):
            def ada_piece(slot, layer, col):
                sp.dma_start(ada_w[slot], w_ada_v[layer][:, :, col:col + 256]).then_inc(ada_in[slot].s, 16)
                sp.dma_start(bias_row[slot][0:1, :], A["b_ada"].rearrange("l (a n) -> l a n", a=1)[layer][:, col:col + 256]
                             ).then_inc(ada_in[slot].s, 16)

            def load_w1(u, e):
                sp.dma_start(ring[:, 3 * u, :], w1_v[e]).then_inc(w_blk[u][0].s, 16)

            def load_w3(u, e):
                sp.dma_start(ring[:, 3 * u + 1, :], w3_v[e]).then_inc(w_blk[u][1].s, 16)

            def load_w2(u, e):
                sp.dma_start(ring[:, 3 * u + 2, :].rearrange("p (h n) -> p h n", h=2), w2_v[e]
                             ).then_inc(w_blk[u][2].s, 16)

            sp.dma_start(c_sb[:, :], A["c"][0].rearrange("(p k) -> p k", k=KD)).then_inc(par_in.s, 16)
            sp.dma_start(x_sb[:, :, :], A["x"][0].rearrange("(t p) d -> p t d", p=P)).then_inc(x_in.s, 16)
            sp.wait_ge(consts_v.s, 1)
            sp.wait_ge(bias_zero.s, 1)
            for m in range(8):
                if m >= 4:
                    sp.wait_ge(ada_used.s, m - 3)
                ada_piece(m % 4, 0, 256 * m)

            with sp.Fori(0, L) as l:
                def win_piece(m):
                    if m >= 2:
                        wait(sp, tile_ready, l, index[last_of_piece[m - 2]] + 1)
                    sp.dma_start(win_w[m % 2], w_in_v[l][:, :, win_cols[m]:win_cols[m] + 256]
                                 ).then_inc(win_in[m % 2].s, 16)

                def ada(m):
                    if m == 2:
                        wait(sp, bias_zero, l, 1)
                    wait(sp, ada_used, l, m - 3 if 2 <= m < 18 else m - 1)
                    pass_on(sp)
                    ada_piece(m % 4 if m < 16 else m % 2, l if m < 16 else (1 - l), ada_cols[m])

                win_piece(0)
                sp.dma_start(wlf[:, :, :], w_in_v[l][:, :, C_LF:C_LF + 32]).then_inc(lf_in.s, 16)
                win_piece(1)
                for m in range(4):
                    ada(m)
                for m in (4, 5, 6):
                    ada(m)
                win_piece(2)
                for m in (7, 8):
                    ada(m)
                win_piece(3)
                for m in range(9, 13):
                    ada(m)
                win_piece(4)
                ada(13), ada(14), ada(15)
                win_piece(5)
                ada(16), ada(17)
                sp.wait_ge(y_zeros.s, 1)
                pass_on(sp)
                with sp.If(l < 1):
                    sp.dma_start(y_dram[NE * SLOTS:].rearrange("(p a) d -> p a d", p=P),
                                 again(zeros_y, MAXOV * SLOTS // P)).then_inc(y_zeroed.s, 16)
                win_piece(6), win_piece(7)
                ada(18), win_piece(8)
                ada(19), ada(20), win_piece(9)
                ada(21), ada(22), win_piece(10)
                ada(23), win_piece(11)
                wait(sp, tile_ready, l, index[("qn", 3)] + 1)
                load_w1(0, l * NE)

                def wo_piece(m):
                    sp.dma_start(ada_w[m % 2], w_out_v[l][:, :, m * 256:(m + 1) * 256]).then_inc(wo_in[m % 2].s, 16)
                for m in range(2):
                    wait(sp, ada_used, l, ADA_PIECES - 1 + m)
                    wo_piece(m)
                wait(sp, cat_n, l, 4)
                load_w2(0, l * NE)
                load_w1(1, l * NE + 1), load_w3(1, l * NE + 1), load_w2(1, l * NE + 1)
                for m in range(2, 4):
                    wait(sp, tile_ready, l, index[("y", m - 2, TT - 1)] + 1)
                    wo_piece(m)
                wait(sp, tile_ready, l, index[("y", 3, TT - 1)] + 1)
                load_w3(0, l * NE)
                wait(sp, routed, l, 1)
                pairs0, more = reg_counts(sp)
                with sp.Fori(0, more) as i:
                    for u in range(2):
                        G = pairs0 * 2 + i * 2 + (2 + u)
                        e = l * NE + sp.value_load(blk_exp[0:1, bass.ds(i * 2 + (2 + u), 1)], min_val=0,
                                                   max_val=NE - 1)
                        wait_blk(sp, "up_ready", G, -1)
                        pass_on(sp)
                        load_w1(u, e)
                        load_w3(u, e)
                        wait_blk(sp, "y_ready", G, -1)
                        pass_on(sp)
                        load_w2(u, e)
                wait_blk(sp, "y_ready", pairs0 * 2 + more * 2, 1)
                pass_on(sp)
            sp.wait_ge(x_new.s, L * TT + TT)
            sp.dma_start(A["out"][0].rearrange("(t p) d -> p t d", p=P), x_sb[:, :, :]).then_inc(out_done.s, 16)
            sp.wait_ge(out_done.s, 16)

        @block.tensor
        def _(pe):
            def mm(out, lhsT, rhs, start, stop):
                return nc.tensor.matmul(out, lhsT, rhs, start=start, stop=stop, skip_group_check=True)

            def sum_chunk(out, cols):
                for k in range(KD):
                    last = mm(out[:, k:k + 1], acc[:, :].rearrange("p (n k) -> p k n", k=KD)[:, k, :],
                              ones[:, 0:1], True, True)
                return last

            pe.wait_ge(consts_p.s, 1)
            pe.wait_ge(consts_v.s, 2)
            for n in ("xg_T", "up_ready", "gT_ready", "y_ready"):
                pe.sem_inc(blk[n].s, 2)
            for n in range(2):
                pe.wait_ge(ada_used.s, 4 * (n + 1))
                sum_chunk(bank[7][:, n * 8:n * 8 + 8], n).then_inc(mod0.s, 1)

            with pe.Fori(0, L) as l:
                def norm_transposes(which):
                    for tt in range(TT):
                        wait(pe, xn_done, l, 4 * (which - 1) + tt + 1)
                        for h in range(2):
                            out = free_bank(pe, l, ("x", which, tt, h))
                            for k in range(4):
                                src = xn[:, tt % 2, :].rearrange("p (n k) -> p k n", k=KD)[:, 4 * h + k, :]
                                last = nc.tensor.transpose(out[:, k * P:(k + 1) * P], src, ident[:, :])
                            last.then_inc(tile_ready.s, 1)

                def hT_ready(which):
                    wait(pe, act_took, l, taken[("x", which, TT - 1, 0)][1])
                    wait(pe, dve_took, l, taken[("x", which, TT - 1, 1)][1])

                def piece(m):
                    wait(pe, win_in[m % 2], l, 16 * (m // 2 + 1))
                    return win_w[m % 2]

                def feature_tile(key, w, col):
                    out = free_bank(pe, l, key)
                    for k in range(KD):
                        last = mm(out[:, :], w[:, k, col:col + P], hT[:, k, :], k == 0, k == KD - 1)
                    last.then_inc(tile_ready.s, 1)

                def token_tile(key, w, tokens):
                    out = free_bank(pe, l, key)
                    for k in range(KD):
                        last = mm(out[:, 0:256], tokens(k), w[:, k, :], k == 0, k == KD - 1)
                    last.then_inc(tile_ready.s, 1)

                def ada_tile(n):
                    out = free_bank(pe, l, ("ada", n))
                    wait(pe, ada_used, l, 4 * (n + 1))
                    if n in (0, 3):
                        mm(out[:, :], ones[:, :], acc[:, 0:512], True, True).then_inc(tile_ready.s, 1)
                        out = free_bank(pe, l, ("ada", n, 1))
                        mm(out[:, :], ones[:, :], acc[:, 512:1024], True, True).then_inc(tile_ready.s, 1)
                    else:
                        sum_chunk(out, n).then_inc(tile_ready.s, 1)

                norm_transposes(1)
                hT_ready(1)
                w = piece(0)
                for d in range(2):
                    feature_tile(("q", d), w, d * P)
                ada_tile(0)
                w = piece(1)
                for d in range(2):
                    feature_tile(("k", d), w, d * P)
                out = free_bank(pe, l, ("lf",))
                wait(pe, lf_in, l, 16)
                for k in range(KD):
                    last = mm(out[0:32, :], wlf[:, k, :], hT[:, k, :], k == 0, k == KD - 1)
                last.then_inc(tile_ready.s, 1)
                ada_tile(1)
                for m in range(2):
                    w = piece(2 + m)
                    for c in range(TT):
                        token_tile(("v", m, c), w, lambda k: hT[:, k, c * P:(c + 1) * P])
                    ada_tile(2 + m)
                for h in range(4):
                    feature_tile(("g", h), piece(4 + h // 2), (h % 2) * P)

                wait(pe, act_took, l, taken[("lf",)][1])
                wait(pe, gatew_in, l, 48)
                for c in range(TT):
                    out = free_bank(pe, l, ("z", c))
                    mm(out[:, :], lfx[:, c * P:(c + 1) * P], gatew[:, :], True, True).then_inc(tile_ready.s, 1)
                wait(pe, la_done, l, 4)
                for r in range(2):
                    for d in range(2):
                        out = free_bank(pe, l, ("b", r, d))
                        for c in range(TT):
                            f = r * 256 + d * P
                            last = mm(out[:, c * P:(c + 1) * P], la[:, c, f:f + P], (upto, since)[r][:, :], True, True)
                        last.then_inc(tile_ready.s, 1)
                for c in range(TT):
                    out = free_bank(pe, l, ("kx", c))
                    mm(out[:, 0:256], after[:, :], la[:, c, 0:256], True, True)
                    mm(out[:, 256:512], before[:, :], la[:, c, 256:512], True, True).then_inc(tile_ready.s, 1)
                    out = free_bank(pe, l, ("kt", c))
                    for d in range(2):
                        last = nc.tensor.transpose(out[:, d * P:(d + 1) * P],
                                                   kT[:, d * T + c * P:d * T + (c + 1) * P], ident[:, :])
                    last.then_inc(tile_ready.s, 1)
                for r, c in [(0, 0), (0, 1), (0, 2), (1, 3), (1, 2), (1, 1)]:
                    out = free_bank(pe, l, ("U", r, c))
                    wait(pe, khat_done, l, c + 1)
                    for h in range(4):
                        half = 64 * (h % 2)
                        last = mm(out[half:half + 64, (h // 2) * P:(h // 2 + 1) * P],
                                  khat[:, c, r * 256 + h * 64:r * 256 + h * 64 + 64],
                                  v_tm[:, c, h * P:(h + 1) * P], True, True)
                    last.then_inc(tile_ready.s, 1)

                def level_tiles(lev, kv, qv):
                    for c in range(TT):
                        out = free_bank(pe, l, ("P", lev, c))
                        for d in range(2):
                            at = d * T + c * P
                            last = mm(out[:, d * 256:(d + 1) * 256], kv[:, at:at + P], qv[:, :, at:at + P], True, True)
                        last.then_inc(tile_ready.s, 1)

                def mean_tile(key, n, weights):
                    out = free_bank(pe, l, key)
                    wait(pe, sq_done, l, n + 1)
                    mm(out[:, :], weights[:, :], sq[:, n % 2, :], True, True).then_inc(tile_ready.s, 1)

                wait(pe, zeroed_q, l, 1)
                level_tiles(7, kT, qz)
                done = index[("P", 7, TT - 1)] + 1
                for n, lev in enumerate(LEVELS):
                    wait(pe, lev_q, l, n + 1)
                    wait(pe, lev_k, l, n + 1)
                    level_tiles(lev, k_lev[n % 2], q_lev[n % 2].rearrange("p (r n) -> p r n", r=2))
                    done = index[("P", lev, TT - 1)] + 1
                    while done < len(plan) and plan[done][0][0] in FILLERS:
                        key = plan[done][0]
                        if key[0] == "kn":
                            feature_tile(key, piece(6 + key[1] // 2), (key[1] % 2) * P)
                        elif key[0] == "kms":
                            mean_tile(key, key[1], mean64)
                        elif key[0] == "ada":
                            ada_tile(key[1])
                        elif key[0] == "vf":
                            feature_tile(key, piece(8 + key[1] // 2), (key[1] % 2) * P)
                        else:
                            out = free_bank(pe, l, key)
                            wait(pe, act_took, l, taken[("vf", key[1])][1])
                            for n7 in range(4 * key[2], min(4 * key[2] + 4, 7)):
                                last = nc.tensor.transpose(out[:, (n7 % 4) * P:(n7 % 4 + 1) * P],
                                                           ekx[:, key[1] % 2, n7 * 64:n7 * 64 + P], ident[:, :])
                            last.then_inc(tile_ready.s, 1)
                        done += 1
                for i, ms in ((0, None), (1, 0), (2, 1), (3, 2), (None, 3)):
                    if i is not None:
                        feature_tile(("qn", i), piece(10 + i // 2), (i % 2) * P)
                    if ms is not None:
                        mean_tile(("qms", ms), 4 + ms, mean64)
                ada_tile(5)

                wait(pe, dve_took, l, taken[("P", 0, TT - 1)][1])
                wait(pe, st_done, l, 1)
                for i, ms in ((0, None), (1, 0), (2, 1), (3, 2), (None, 3)):
                    if i is not None:
                        out = free_bank(pe, l, ("o", i))
                        half, d = 64 * (i % 2), i // 2
                        for c in range(TT):
                            o = out[:, c * P:(c + 1) * P]
                            at = d * T + c * P
                            last = mm(o, v_tm[:, c, i * P:(i + 1) * P], amat[:, c, i, :], True, False)
                            for r in range(2):
                                if (c > 0, c < TT - 1)[r]:
                                    last = mm(o, st[half:half + 64, r, c - 1 + r, d * P:(d + 1) * P],
                                              qd[half:half + 64, r, at:at + P], False, r == 1 or c == TT - 1)
                        last.then_inc(tile_ready.s, 1)
                    if ms is not None:
                        mean_tile(("oms", ms), 8 + ms, ones)

                for h in range(11):
                    if h < 8:
                        d, r = h // 2, h % 2
                        if r == 0:
                            wait(pe, dve_took, l, taken[("qn", d)][1])
                        for i in range(2):
                            out = free_bank(pe, l, ("S", h, i))
                            for cb in (2 * i, 2 * i + 1):
                                q0 = T - P * (cb + 1)
                                last = mm(out[:, (cb % 2) * 256:(cb % 2 + 1) * 256], qnz[:, d, r, q0:q0 + P],
                                          kn[:, d, KEY_AT[cb] * 64:KEY_AT[cb] * 64 + 256], True, True)
                            last.then_inc(tile_ready.s, 1)
                    if 2 <= h < 10:
                        g = h - 2
                        wait(pe, prob_done, l, g + 1)
                        for i in range(2):
                            out = free_bank(pe, l, ("PT", g, i))
                            for cb in (2 * i, 2 * i + 1):
                                for half in range(2):
                                    last = nc.tensor.transpose(
                                        out[:, (cb % 2) * 256 + half * P:(cb % 2) * 256 + (half + 1) * P],
                                        P_sb[:, g % 3, cb, half * P:(half + 1) * P], ident[:, :])
                            last.then_inc(tile_ready.s, 1)
                    if h >= 3:
                        g = h - 3
                        d, r = g // 2, g % 2
                        wait(pe, act_took, l, taken[("PT", g, 1)][1])
                        if r == 0 and d >= 2:
                            wait(pe, cat_n, l, d - 1)
                        for cb in range(4):
                            q0 = T - P * (cb + 1)
                            for half in range(2):
                                last = mm(bank[6 + d % 2][64 * r:64 * r + 64, q0:q0 + P],
                                          vn[:, KEY_AT[cb] + 2 * half, g * 64:(g + 1) * 64],
                                          PT_sb[:, g % 2, cb, half * P:(half + 1) * P], half == 0, half == 1)
                        if r == 1:
                            last.then_inc(on_done.s, 1)

                wait(pe, cat_g, l, 1)
                wait(pe, cat_n, l, 4)
                for m in range(4):
                    wait(pe, wo_in[m % 2], l, 16 * (m // 2 + 1))
                    for tt in range(TT):
                        token_tile(("y", m, tt), ada_w[m % 2], lambda k: cat[:, k, tt * P:(tt + 1) * P])
                norm_transposes(2)
                hT_ready(2)
                out = free_bank(pe, l, ("logits",))
                for tt in range(TT):
                    for k in range(KD):
                        last = mm(out[:, tt * NE:(tt + 1) * NE], hT[:, k, tt * P:(tt + 1) * P], rw_sb[:, k, :],
                                  k == 0, k == KD - 1)
                last.then_inc(tile_ready.s, 1)

                out = free_bank(pe, l, ("rank",))
                wait(pe, mask_done, l, 1)
                mask = R["mask"]
                for tt in range(TT):
                    o = out[:, tt * NE:(tt + 1) * NE]
                    mm(o, before[:, :], mask[:, tt * NE:(tt + 1) * NE], True, tt == 0)
                    for t2 in range(tt):
                        mm(o, ones[:, :], mask[:, t2 * NE:(t2 + 1) * NE], False, t2 == tt - 1)
                for tt in range(TT):
                    mm(out[:, 128:128 + NE], ones[:, :], mask[:, tt * NE:(tt + 1) * NE], tt == 0, tt == TT - 1)
                for tt in range(TT):
                    last = mm(out[0:NE, 160:161], mask[:, tt * NE:(tt + 1) * NE], ones[:, 0:1], tt == 0, tt == TT - 1)
                last.then_inc(tile_ready.s, 1)
                out = free_bank(pe, l, ("over",))
                wait(pe, over_in, l, 1)
                nov = R["t3"][0:NE, :]
                mm(out[:, 0:NE], nov, before[0:NE, 0:NE], True, True)
                mm(out[:, NE:NE + 1], nov, ones[0:NE, 0:1], True, True).then_inc(tile_ready.s, 1)
                out = free_bank(pe, l, ("slot",))
                wait(pe, slot1h, l, 1)
                for j in range(8):
                    last = mm(out[0:SLOTS, 0:NBLK], oslot[:, j, :], oblk[:, j, :], j == 0, j == 7)
                last.then_inc(tile_ready.s, 1)

                wait(pe, routed, l, 1)
                pairs0, more = reg_counts(pe)

                def turn(u, G, pair):
                    pe.wait_ge(gathered[u].s, pair * 16 + 16)
                    wait_blk(pe, "hg_done", G, -1)
                    pass_on(pe)
                    for k in range(KD):
                        src = xg[:, u, :].rearrange("p (n k) -> p k n", k=KD)[:, k, :]
                        last = nc.tensor.transpose(bank[u][:, k * SLOTS:(k + 1) * SLOTS], src,
                                                   ident[0:SLOTS, 0:SLOTS])
                    last.then_inc(blk["xg_T"].s, 1)

                def up(u, G, pair):
                    wait_blk(pe, "hg_done", G, 1)
                    wait_blk(pe, "g_done", G, -1)
                    for mat in range(2):
                        pe.wait_ge(w_blk[u][mat].s, pair * 16 + 16)
                        for k in range(KD):
                            for half in range(2):
                                last = mm(bank[2 + u][64 * half:64 * half + 64, mat * 256:(mat + 1) * 256],
                                          hgT[:, u, k, :], w13[u][mat][:, k, half * 256:(half + 1) * 256],
                                          k == 0, k == KD - 1)
                    last.then_inc(blk["up_ready"].s, 1)

                def turn_g(u, G):
                    wait_blk(pe, "g_done", G, 1)
                    wait_blk(pe, "gTs_done", G, -1)
                    for q in range(2):
                        src = sil[:, u, 256:512].rearrange("p (n q) -> p q n", q=2)[:, q, :]
                        last = nc.tensor.transpose(bank[4 + u][:, q * P:(q + 1) * P], src, ident[:, :])
                    last.then_inc(blk["gT_ready"].s, 1)

                def down(u, G, pair):
                    wait_blk(pe, "gTs_done", G, 1)
                    wait_blk(pe, "y_evac", G, -1)
                    pe.wait_ge(w_blk[u][2].s, pair * 16 + 16)
                    for n in range(4):
                        hh, q = n // 2, n % 2
                        for nh in range(2):
                            last = mm(bank[6 + u][64 * nh:64 * nh + 64, :],
                                      gTs[:, u, q * P + hh * 64:q * P + hh * 64 + 64],
                                      w2s[u][:, hh, q, nh * 512:(nh + 1) * 512], n == 0, n == 3)
                    last.then_inc(blk["y_ready"].s, 1)

                G0 = pairs0 * 2
                turn(0, G0, pairs0)
                up(0, G0, pairs0)
                turn(1, G0 + 1, pairs0)
                with pe.Fori(0, more) as i:
                    G, pair = G0 + i * 2, pairs0 + i
                    up(1, G + 1, pair)
                    turn_g(0, G)
                    turn(0, G + 2, pair + 1)
                    down(0, G, pair)
                    up(0, G + 2, pair + 1)
                    turn_g(1, G + 1)
                    turn(1, G + 3, pair + 1)
                    down(1, G + 1, pair)
                G, pair = G0 + more * 2, pairs0 + more
                up(1, G + 1, pair)
                turn_g(0, G)
                down(0, G, pair)
                turn_g(1, G + 1)
                down(1, G + 1, pair)

        @block.scalar
        def _(act):
            steps = [0]

            def link(l, ins):
                steps[0] += 1
                ins.then_inc(act_step.s, 1)
                wait(act, act_step, l, steps[0])

            F = nc.scalar.activation
            nc.scalar.preload_act_table_set("natural_log_exp_and_others")
            act.wait_ge(consts_p.s, 1)
            for n in ("gTs_done", "y_evac", "up_exp"):
                act.sem_inc(blk[n].s, 2)
            for u in range(2):
                act.sem_inc(y_stored[u].s, 32)
            for l0 in range(L):
                def vec(v, n):
                    return v.rearrange("(p k) -> p k", k=n)
                act.dma_start(par_all[:, l0, 0:8], vec(A["ffn_norm"][l0], KD)).then_inc(par_in.s, 16)
                act.dma_start(par_all[:, l0, 8:16], vec(A["attn_norm"][1 - l0], KD)).then_inc(par_in.s, 16)
                act.dma_start(par_all[:, l0, 16:17], vec(A["gla_out_norm"][l0], 1)).then_inc(par_in.s, 16)
                for half in range(2):
                    rows = slice(64 * half, 64 * half + 64)
                    act.dma_start(par_all[rows, l0, 17:18], vec(A["na_q_norm"][l0], 1)).then_inc(par_in.s, 16)
                    act.dma_start(par_all[rows, l0, 18:19], vec(A["na_k_norm"][l0], 1)).then_inc(par_in.s, 16)
            act.dma_start(anorm0[:, :], A["attn_norm"][0].rearrange("(p k) -> p k", k=KD)).then_inc(par_in.s, 16)
            act.dma_start(rw_sb[:, :, :], A["router_w"].rearrange("(p k) n -> p k n", k=KD)).then_inc(par_in.s, 16)
            act.dma_start(rb_sb[:, :], bass.AP(tensor=A["router_b"].tensor, offset=0, ap=[[0, P], [1, NE]])
                          ).then_inc(par_in.s, 16)
            act.dma_start(rpb_pad[:, RPB_PAD:RPB_PAD + 8 * RPB_W], A["na_rpb"].rearrange("l h a b -> l (h a b)")
                          ).then_inc(rpb_copied.s, 16)
            act.wait_ge(consts_v.s, 2)
            act.dma_start(rpb_pad[:, 0:RPB_PAD], pad0[:, :]).then_inc(rpb_copied.s, 16)
            act.dma_start(rpb_pad[:, RPB_PAD + 8 * RPB_W:], pad0[:, :]).then_inc(rpb_copied.s, 16)
            act.wait_ge(rpb_copied.s, 48)
            act.wait_ge(par_in.s, 16 * 18)
            F(ctmp[:, :], c_sb[:, :], ACT.Exp, scale=-1.0).then_inc(c_act.s, 1)

            with act.Fori(0, L) as l:
                steps[0] = 0

                def gates_load():
                    act.dma_start(gatew[0:16, 0:256], A["gla_gate_w"].rearrange("l r a n -> (l r) a n")[l * 2]
                                  ).then_inc(gatew_in.s, 16)
                    act.dma_start(gatew[16:32, 256:512], A["gla_gate_w"].rearrange("l r a n -> (l r) a n")[l * 2 + 1]
                                  ).then_inc(gatew_in.s, 16)
                    act.dma_start(gatew[32:33, :], A["gla_gate_b"].rearrange("l (a r) n -> l a (r n)", a=1)[l]
                                  ).then_inc(gatew_in.s, 16)

                def tile(key):
                    return ready(act, l, key)

                def norm(which):
                    c0 = 4 * (which - 1)
                    src = x_new if which == 1 else x_mid
                    for tt in range(TT):
                        act.wait_ge(src.s, l * TT + tt + 1)
                        link(l, F(flat[:, 8192:9216] if which == 1 else pool_a[:, 0:1024], x_sb[:, tt, :], ACT.Square,
                                  accum_out=ssq[:, c0 + tt:c0 + tt + 1]))
                    link(l, F(rstd[:, c0:c0 + 4], ssq[:, c0:c0 + 4], ACT.Ln, bias=eps_c[:, 0:1], scale=1.0 / D))
                    F(rstd[:, c0:c0 + 4], rstd[:, c0:c0 + 4], ACT.Exp, scale=-0.5).then_inc(rstd_done.s, 1)

                def shift(which):
                    a_, b_ = (A1, B1) if which == 1 else (A2, B2)
                    for tt in range(TT):
                        b = tile(("x", which, tt, 0))
                        for k in range(4):
                            last = F(hT[:, k, tt * P:(tt + 1) * P], b[:, k * P:(k + 1) * P], ACT.Identity,
                                     bias=b_[:, k:k + 1], scale=a_[:, k:k + 1])
                        last.then_inc(act_took.s, 1)

                norm(1)
                gates_load()
                act.wait_ge(mod_ready.s, 1)
                shift(1)
                for d in range(2):
                    b = tile(("q", d))
                    for half in range(2):
                        rows = slice(64 * half, 64 * half + 64)
                        last = F(qz[rows, half, d * T:(d + 1) * T], b[rows, :], ACT.Copy, scale=0.125)
                    last.then_inc(act_took.s, 1)
                for d in range(2):
                    b = tile(("k", d))
                    F(kT[:, d * T:(d + 1) * T], b[:, :], ACT.Copy).then_inc(act_took.s, 1)
                b = tile(("lf",))
                wait(act, dve_took, l, taken[("ada", 0)][1])
                F(lfx[0:32, :], b[0:32, :], ACT.Copy).then_inc(act_took.s, 1)
                for m in range(2):
                    for c in range(TT):
                        b = tile(("v", m, c))
                        F(v_tm[:, c, m * 256:(m + 1) * 256], b[:, 0:256], ACT.Copy).then_inc(act_took.s, 1)
                for h in range(4):
                    b = tile(("g", h))
                    F(sg[:, h, :], b[:, :], ACT.Exp, scale=-1.0).then_inc(gexp_done.s, 1)
                for c in range(TT):
                    b = tile(("z", c))
                    t1 = rt[:, c % 2, :]
                    if c >= 2:
                        wait(act, la_done, l, c - 1)
                    link(l, F(t1, b[:, :], ACT.Abs))
                    link(l, F(t1, t1, ACT.Exp, scale=-1.0))
                    F(t1, t1, ACT.Ln, bias=one_c[:, 0:1]).then_inc(ln_done.s, 1)
                act.wait_ge(y_zeroed.s, 16)
                for r in range(2):
                    for d in range(2):
                        b = tile(("b", r, d))
                        F(bT[:, r, d * T:(d + 1) * T], b[:, :], ACT.Copy).then_inc(act_took.s, 1)
                wait(act, act_took, l, taken[("b", 1, 1)][1])
                for c in range(TT):
                    b = tile(("kx", c))
                    if c >= 2:
                        wait(act, khat_done, l, c - 1)
                    F(ekx[:, c % 2, :], b[:, :], ACT.Exp, scale=TAU_INV).then_inc(act_took.s, 1)
                for r in range(2):
                    F(qd[:, r, :], bT[:, r, :], ACT.Exp, scale=TAU_INV)
                    ends = bT[:, r, :].rearrange("p (n i) -> p n i", i=P)[:, :, P - 1 if r == 0 else 0]
                    last = F(dec[:, r, :], ends, ACT.Exp, scale=TAU_INV)
                last.then_inc(dec_done.s, 1)
                for c in range(TT):
                    b = tile(("P", 7, c))
                    F(amat[:, c, :, :].rearrange("p h i -> p (h i)"), b[:, :], ACT.Copy).then_inc(act_took.s, 1)

                def squares(key, n):
                    b = tile(key)
                    if n >= 2:
                        ms = {"kn": "kms", "qn": "qms", "o": "oms"}
                        prev = [(a, i) for a in ("kn", "qn", "o") for i in range(4)][n - 2]
                        wait(act, tile_ready, l, index[(ms[prev[0]], prev[1])] + 1)
                    F(sq[:, n % 2, :], b[:, :], ACT.Square).then_inc(sq_done.s, 1)

                def scales(key, n):
                    b = tile(key)
                    if n >= 2:
                        prev = [(a, i) for a in ("kn", "qn", "o") for i in range(4)][n - 2]
                        wait(act, dve_took, l, taken[prev][1])
                    F(rt[:, n % 2, :], b[:, :], ACT.Ln, bias=eps_c[:, 0:1],
                      scale=1.0 if n < 8 else 1.0 / 128).then_inc(act_took.s, 1)
                    wait(act, act_took, l, taken[key][1])
                    F(rt[:, n % 2, :], rt[:, n % 2, :], ACT.Exp, scale=-0.5).then_inc(rt_done.s, 1)

                def level_exp(n):
                    wait(act, diff_q, l, n + 1)
                    F(eq, eq, ACT.Exp, scale=TAU_INV).then_inc(exp_q.s, 1)
                    wait(act, diff_k, l, n + 1)
                    F(k_lev[n % 2], k_lev[n % 2], ACT.Exp, scale=TAU_INV).then_inc(exp_k.s, 1)

                level_exp(0)
                for n, lev in enumerate(LEVELS):
                    if n < 6:
                        level_exp(n + 1)
                    at = index[("P", lev, TT - 1)] + 1
                    while plan[at][0][0] in FILLERS:
                        key = plan[at][0]
                        at += 1
                        if key[0] == "kn":
                            squares(key, key[1])
                        elif key[0] == "kms":
                            scales(key, key[1])
                        elif key[0] != "ada":
                            b = tile(key)
                            f = key[1]
                            if key[0] == "vf":
                                if f >= 2:
                                    wait(act, tile_ready, l, index[("vt", f - 2, 1)] + 1)
                                F(ekx[:, f % 2, :].rearrange("p (c r) -> p r c", r=ROWS),
                                  b[:, :].rearrange("p (r c) -> p r c", c=COLS), ACT.Copy).then_inc(act_took.s, 1)
                            else:
                                n0, n1 = 4 * key[2], min(4 * key[2] + 4, 7)
                                F(vn[:, n0:n1, f * P:(f + 1) * P],
                                  b[:, 0:(n1 - n0) * P].rearrange("p (n f) -> p n f", f=P), ACT.Copy
                                  ).then_inc(act_took.s, 1)
                        if at == len(plan):
                            break
                for pre, n0 in (("qn", 4), ("o", 8)):
                    ms = pre[0] + "ms"
                    squares((pre, 0), n0), squares((pre, 1), n0 + 1)
                    for i in range(4):
                        scales((ms, i), n0 + i)
                        if i < 2:
                            squares((pre, i + 2), n0 + i + 2)
                wait(act, st_done, l, 1)
                wait(act, tile_ready, l, index[("o", 3)] + 1)
                for h in range(8):
                    src = bass.AP(tensor=rpb_pad.tensor, offset=rpb_pad[l][h * RPB_W:h * RPB_W + 1].offset,
                                  ap=[[1, 16], [31, 8], [1, 265]])
                    act.dma_start(gtab[:, h, :], src).then_inc(gtab_in.s, 16)

                for h in range(11):
                    if h < 8:
                        wait(act, smax_done, l, h + 1)
                        for cb in range(4):
                            last = F(P_sb[:, h % 3, cb, :], P_sb[:, h % 3, cb, :], ACT.Exp,
                                     bias=nmx[:, h % 2, cb:cb + 1], accum_out=sm[:, h % 2, cb:cb + 1])
                        last.then_inc(sexp_done.s, 1)
                    if 2 <= h < 10:
                        g = h - 2
                        for i in range(2):
                            b = tile(("PT", g, i))
                            F(PT_sb[:, g % 2, 2 * i:2 * i + 2, :].rearrange("p c n -> p (c n)"), b[:, :], ACT.Copy
                              ).then_inc(act_took.s, 1)
                    if h >= 4 and h % 2 == 0:
                        d = (h - 4) // 2
                        wait(act, on_done, l, d + 1)
                        src = ap_of(bank[6 + d % 2][:, :], T - 1, [[-1, ROWS], [-ROWS, COLS]])
                        F(cat[:, 4 + d, :].rearrange("p (r c) -> p r c", c=COLS), src, ACT.Copy).then_inc(cat_n.s, 1)

                norm(2)
                for tt in range(TT):
                    wait(act, xn_done, l, 4 + tt + 1)
                    act.dma_start(xn_dram[tt * P:(tt + 1) * P, :], xn[:, tt % 2, :]).then_inc(xn_stored[tt % 2].s, 16)
                shift(2)
                b = tile(("logits",))
                F(R["score"], b[:, 0:128], ACT.Exp, scale=-1.0).then_inc(route_exp.s, 1)

                wait(act, routed, l, 1)
                pairs0, more = reg_counts(act)
                G0 = pairs0 * 2

                def up_exp(u, G):
                    wait_blk(act, "up_ready", G, 1)
                    wait_blk(act, "gT_ready", G, -1)
                    F(sil[:, u, 0:256], bank[2 + u][:, 0:256], ACT.Exp, scale=-1.0).then_inc(blk["up_exp"].s, 1)

                def take(u, G, pair, row):
                    wait_blk(act, "gT_ready", G, 1)
                    F(gTs[:, u, :], bank[4 + u][:, 0:256], ACT.Copy).then_inc(blk["gTs_done"].s, 1)
                    wait_blk(act, "y_ready", G, 1)
                    act.wait_ge(y_stored[u].s, pair * 32 + 32)
                    F(y_sb[:, u, :], bank[6 + u][:, :], ACT.Copy).then_inc(blk["y_evac"].s, 1)
                    wait_blk(act, "y_evac", G, 1)
                    for nh in range(2):
                        act.dma_start(y_blk[row][nh], y_sb[64 * nh:64 * nh + 64, u, :]).then_inc(y_stored[u].s, 16)

                up_exp(0, G0)
                with act.Fori(0, more) as i:
                    G, pair = G0 + i * 2, pairs0 + i
                    up_exp(1, G + 1)
                    take(0, G, pair, i * 2)
                    up_exp(0, G + 2)
                    take(1, G + 1, pair, i * 2 + 1)
                G, pair = G0 + more * 2, pairs0 + more
                up_exp(1, G + 1)
                take(0, G, pair, more * 2)
                take(1, G + 1, pair, more * 2 + 1)
            assert steps[0] == ACT_STEPS, steps

        @block.vector
        def _(dve):
            V = nc.vector
            steps = [0]

            def link(l, ins):
                steps[0] += 1
                ins.then_inc(dve_step.s, 1)
                wait(dve, dve_step, l, steps[0])

            n0 = [0]

            def link0(ins):
                n0[0] += 1
                ins.then_inc(cstep.s, 1)
                dve.wait_ge(cstep.s, n0[0])
            link0(V.memset(brow[:, :, :].rearrange("p u n -> p (u n)"), 0.0))
            V.memset(pad0[:, :], 0.0).then_inc(consts_v.s, 1)
            V.memset(ones[:, :], 1.0)
            link0(V.memset(mean64[:, :], 0.0))
            V.memset(mean64[0:64, 0:64], 1.0 / 64)
            V.memset(mean64[64:128, 64:128], 1.0 / 64)
            V.memset(eps_c[:, :], EPS)
            V.memset(one_c[:, :], 1.0)
            V.memset(gatew[:, :], 0.0)
            V.memset(pairs[:, :], 0)
            V.memset(pairs_f[:, :], 0.0).then_inc(consts_v.s, 1)
            dve.wait_ge(consts_p.s, 1)
            link0(V.tensor_tensor(xor[:, :], io_p[:, :], io_f[:, :], ALU.bitwise_xor))
            for s_ in range(7):
                link0(V.tensor_scalar(xsh[:, :], xor[:, :], s_, None, ALU.arith_shift_right))
                link0(V.tensor_copy(xfl[:, :], xsh[:, :]))
                link0(V.tensor_scalar(lvl[:, s_, :], xfl[:, :], 1.0, None, ALU.is_equal))
            link0(V.tensor_scalar(xsh[:, 0:1], io_p[:, 0:1], 3, None, ALU.arith_shift_right))
            link0(V.tensor_copy(lo[:, 3:4], xsh[:, 0:1]))
            link0(V.tensor_scalar(lo[:, 1:2], lo[:, 3:4], -1.0, 15.0, ALU.mult, ALU.add))
            link0(V.tensor_scalar(lo[:, 0:1], lo[:, 1:2], -8.0, 0.0, ALU.add, ALU.max))
            link0(V.tensor_scalar(lo[:, 2:3], lo[:, 1:2], 8.0, 16.0, ALU.add, ALU.min))
            for m in range(3):
                link0(V.tensor_scalar(xfl[:, 0:32], iota_s[:, 0:32], lo[:, m:m + 1], None, ALU.subtract))
                link0(V.tensor_scalar(xfl[:, 32:64], xfl[:, 0:32], 0.0, None, ALU.is_ge))
                link0(V.tensor_scalar(xfl[:, 64:96], xfl[:, 0:32], 15.5, None, ALU.is_lt))
                link0(V.tensor_tensor(xfl[:, 96:128], xfl[:, 32:64], xfl[:, 64:96], ALU.mult))
                link0(V.tensor_scalar(wneg[:, m, :], xfl[:, 96:128], -1.0, -NEG, ALU.add, ALU.mult))
            dve.wait_ge(c_act.s, 1)
            dve.wait_ge(par_in.s, 16 * 18)
            link0(V.tensor_scalar(ctmp[:, :], ctmp[:, :], 1.0, None, ALU.add))
            link0(V.reciprocal(ctmp[:, :], ctmp[:, :]))
            link0(V.tensor_tensor(ctmp[:, :], ctmp[:, :], c_sb[:, :], ALU.mult))
            for n in ("hg_done", "g_done"):
                dve.sem_inc(blk[n].s, 2)

            def ada_part(slot, quarter, k):
                out = acc[:, quarter * 256:(quarter + 1) * 256]
                return V.scalar_tensor_tensor(out=out, in0=ada_w[slot][:, k, :], scalar=ctmp[:, k:k + 1],
                                              in1=bias_row[slot] if k == 0 else out, op0=ALU.mult, op1=ALU.add)

            def ada_pieces(pieces, step):
                for k in range(KD):
                    for i, (slot, quarter) in enumerate(pieces):
                        ins = ada_part(slot, quarter, k)
                        if k == KD - 1:
                            ins.then_inc(ada_used.s, 1)
                        else:
                            step(ins, 0 if k == KD - 2 and i == len(pieces) - 1 else len(pieces) - 1)

            def step0(ins, back):
                n0[0] += 1
                ins.then_inc(cstep.s, 1)
                dve.wait_ge(cstep.s, n0[0] - back)

            for m in range(0, 8, 2):
                if m == 4:
                    dve.wait_ge(mod0.s, 1)
                for i in range(2):
                    dve.wait_ge(ada_in[(m + i) % 4].s, 32 * (m // 4 + 1))
                ada_pieces([((m + i) % 4, (m + i) % 4) for i in range(2)], step0)
            dve.wait_ge(mod0.s, 2)
            V.tensor_copy(B1[:, :], bank[7][:, 0:8])
            V.scalar_tensor_tensor(out=A1[:, :], in0=bank[7][:, 8:16], scalar=1.0, in1=anorm0[:, :],
                                   op0=ALU.add, op1=ALU.mult).then_inc(mod_ready.s, 1)
            dve.wait_ge(x_in.s, 16)
            dve.sem_inc(x_new.s, TT)

            with dve.Fori(0, L) as l:
                steps[0] = 0

                def step(ins):
                    link(l, ins)

                def tile(key):
                    return ready(dve, l, key)

                def norm(which):
                    a_, b_ = (A1, B1) if which == 1 else (A2, B2)
                    c0 = 4 * (which - 1)
                    wait(dve, rstd_done, l, which)
                    for tt in range(TT):
                        if tt >= 2:
                            wait(dve, tile_ready, l, index[("x", which, tt - 2, 1)] + 1)
                            if which == 2:
                                wait(dve, xn_stored[tt % 2], l, 16)
                        V.tensor_scalar(xn[:, tt % 2, :], x_sb[:, tt, :], rstd[:, c0 + tt:c0 + tt + 1], None,
                                        ALU.mult).then_inc(xn_done.s, 1)
                        if tt >= 1:
                            shift_tile(which, tt - 1, a_, b_)
                    shift_tile(which, TT - 1, a_, b_)

                def shift_tile(which, tt, a_, b_):
                    b = tile(("x", which, tt, 1))
                    for k in range(4):
                        last = V.tensor_scalar(hT[:, 4 + k, tt * P:(tt + 1) * P], b[:, k * P:(k + 1) * P],
                                               a_[:, 4 + k:5 + k], b_[:, 4 + k:5 + k], ALU.mult, ALU.add)
                    last.then_inc(dve_took.s, 1)

                def ada_step(ins, back):
                    steps[0] += 1
                    ins.then_inc(dve_step.s, 1)
                    wait(dve, dve_step, l, steps[0] - back)

                def ada_sum(*ms):
                    for m in ms:
                        use = m // 4 if m < 16 else 4 + (m - 16) // 2
                        wait(dve, ada_in[m % 4 if m < 16 else m % 2], l, 32 * (use + 1))
                    ada_pieces([(m % 4 if m < 16 else m % 2, m % 4) for m in ms], ada_step)

                def ada_chunk(n):
                    ada_sum(4 * n, 4 * n + 1)
                    ada_sum(4 * n + 2, 4 * n + 3)

                norm(1)
                step(V.tensor_copy(par[:, :], par_all[:, bass.ds(l, 1), :].rearrange("p a n -> p (a n)")))
                wait(dve, tile_ready, l, index[("x", 1, TT - 1, 1)] + 1)
                V.memset(lfx[32:33, :], 1.0)
                ada_chunk(0)
                b = tile(("ada", 0))
                V.tensor_copy(g1_bc[:, 0:512], b[:, :]).then_inc(dve_took.s, 1)
                V.tensor_copy(g1_bc[:, 512:1024], ready(dve, l, ("ada", 0, 1))[:, :]).then_inc(dve_took.s, 1)
                ada_chunk(1)
                b = tile(("ada", 1))
                V.tensor_copy(B2[:, :], b[:, 0:8]).then_inc(dve_took.s, 1)
                ada_chunk(2)
                b = tile(("ada", 2))
                V.scalar_tensor_tensor(out=A2[:, :], in0=b[:, 0:8], scalar=1.0, in1=par[:, 0:8], op0=ALU.add,
                                       op1=ALU.mult).then_inc(dve_took.s, 1)
                ada_chunk(3)
                for i in range(2):
                    b = ready(dve, l, ("ada", 3, i) if i else ("ada", 3))
                    V.tensor_copy(g2_bc[:, i * 512:(i + 1) * 512], b[:, :]).then_inc(dve_took.s, 1)
                for h in range(4):
                    b = tile(("g", h))
                    wait(dve, gexp_done, l, h + 1)
                    step(V.tensor_scalar(sg[:, h, :], sg[:, h, :], 1.0, None, ALU.add))
                    step(V.reciprocal(sg[:, h, :], sg[:, h, :]))
                    V.tensor_tensor(sg[:, h, :], b[:, :], sg[:, h, :], ALU.mult).then_inc(dve_took.s, 1)
                for c in range(TT):
                    b = tile(("z", c))
                    wait(dve, ln_done, l, c + 1)
                    V.scalar_tensor_tensor(out=la[:, c, :], in0=b[:, :], scalar=0.0, in1=rt[:, c % 2, :],
                                           op0=ALU.min, op1=ALU.subtract).then_inc(dve_took.s, 1)
                    wait(dve, dve_took, l, taken[("z", c)][1])
                    dve.sem_inc(la_done.s, 1)
                for c in range(TT):
                    b = tile(("kt", c))
                    wait(dve, act_took, l, taken[("kx", c)][1])
                    V.tensor_tensor(khat[:, c, :].rearrange("p (r n) -> p r n", r=2),
                                    ekx[:, c % 2, :].rearrange("p (r n) -> p r n", r=2), again(b[:, 0:256], 2),
                                    ALU.mult).then_inc(dve_took.s, 1)
                    wait(dve, dve_took, l, taken[("kt", c)][1])
                    dve.sem_inc(khat_done.s, 1)

                def level_diff(n):
                    hh = 1 << LEVELS[n]
                    e = eq.rearrange("p (n a h) -> p n a h", a=2, h=hh)
                    f, g = (bT[:, r, :].rearrange("p (n a h) -> p n a h", a=2, h=hh) for r in range(2))
                    V.tensor_tensor(e[:, :, 1, :], f[:, :, 1, :], rep(f[:, :, 0, hh - 1], hh), ALU.subtract)
                    V.tensor_tensor(e[:, :, 0, :], g[:, :, 0, :], rep(g[:, :, 1, 0], hh), ALU.subtract
                                    ).then_inc(diff_q.s, 1)

                wait(dve, act_took, l, taken[("b", 1, 1)][1])
                level_diff(0)
                wait(dve, dec_done, l, 1)
                for r, c in [(0, 0), (0, 1), (0, 2), (1, 3), (1, 2), (1, 1)]:
                    b = tile(("U", r, c))
                    to = c if r == 0 else c - 1
                    if c in (0, 3):
                        V.tensor_copy(st[:, r, to, :], b[:, 0:256]).then_inc(dve_took.s, 1)
                    else:
                        prev = to - 1 if r == 0 else to + 1
                        for d in range(2):
                            last = V.scalar_tensor_tensor(out=st[:, r, to, d * P:(d + 1) * P],
                                                          in0=st[:, r, prev, d * P:(d + 1) * P],
                                                          scalar=dec[:, r, d * 4 + c:d * 4 + c + 1],
                                                          in1=b[:, d * P:(d + 1) * P], op0=ALU.mult, op1=ALU.add)
                        last.then_inc(dve_took.s, 1)
                    wait(dve, dve_took, l, taken[("U", r, c)][1])
                for half in range(2):
                    rows = slice(64 * half, 64 * half + 64)
                    last = V.tensor_tensor(qd[rows, :, :], qd[rows, :, :], again(qz[rows, half, :], 2), ALU.mult)
                last.then_inc(st_done.s, 1)

                def level_q(n):
                    wait(dve, exp_q, l, n + 1)
                    if n >= 2:
                        wait(dve, tile_ready, l, index[("P", LEVELS[n - 2], TT - 1)] + 1)
                    else:
                        wait(dve, (zeroed_q, zeroed_l)[n], l, 1)
                    for half in range(2):
                        rows = slice(64 * half, 64 * half + 64)
                        last = V.tensor_tensor(q_lev[n % 2][rows, half * 1024:(half + 1) * 1024], eq[rows, :],
                                               qz[rows, half, :], ALU.mult)
                    last.then_inc(lev_q.s, 1)
                    wait(dve, lev_q, l, n + 1)
                    if n < 6:
                        level_diff(n + 1)

                level_q(0)
                for n, lev in enumerate(LEVELS):
                    if n < 6:
                        level_q(n + 1)
                    for c in range(TT):
                        b = tile(("P", lev, c))
                        if n == 0:
                            wait(dve, act_took, l, taken[("P", 7, c)][1])
                        pass_on(dve)
                        V.copy_predicated(out=amat[:, c, :, :], mask=again(lvl[:, lev, :], 4),
                                          data=b[:, :].rearrange("p (h i) -> p h i", h=4)).then_inc(dve_took.s, 1)
                    wait(dve, dve_took, l, taken[("P", lev, TT - 1)][1])
                    at = index[("P", lev, TT - 1)] + 1
                    while plan[at][0][0] in FILLERS:
                        key = plan[at][0]
                        at += 1
                        if key[0] == "kms":
                            i = key[1]
                            b = tile(("kn", i))
                            wait(dve, rt_done, l, i + 1)
                            V.scalar_tensor_tensor(
                                out=kn[:, i, :].rearrange("p (c r) -> p r c", r=ROWS),
                                in0=b[:, :].rearrange("p (r c) -> p r c", c=COLS), scalar=par[:, 18:19],
                                in1=rt[:, i % 2, :].rearrange("p (r c) -> p r c", c=COLS), op0=ALU.mult, op1=ALU.mult
                            ).then_inc(dve_took.s, 1)
                        elif key[0] == "ada":
                            b = tile(key)
                            V.tensor_copy(B1[:, :], b[:, 0:8]).then_inc(dve_took.s, 1)
                    ada_sum(16 + n)
                ada_sum(23)

                def query_tile(i):
                    b = tile(("qn", i))
                    wait(dve, rt_done, l, 4 + i + 1)
                    for half in range(2):
                        rows = slice(64 * half, 64 * half + 64)
                        last = V.scalar_tensor_tensor(
                            out=ap_of(qnz[rows, i, half, :], T - 1, [[-1, ROWS], [-ROWS, COLS]]),
                            in0=b[rows, :].rearrange("p (r c) -> p r c", c=COLS), scalar=qscale[rows, 0:1],
                            in1=rt[rows, i % 2, :].rearrange("p (r c) -> p r c", c=COLS), op0=ALU.mult, op1=ALU.mult)
                    last.then_inc(dve_took.s, 1)

                step(V.tensor_scalar(qscale[:, :], par[:, 17:18], 0.125, None, ALU.mult))
                wait(dve, zeroed_n, l, 1)
                for i in range(4):
                    query_tile(i)
                b = tile(("ada", 5))
                V.scalar_tensor_tensor(out=A1[:, :], in0=b[:, 0:8], scalar=1.0, in1=par[:, 8:16], op0=ALU.add,
                                       op1=ALU.mult).then_inc(dve_took.s, 1)
                for i in range(4):
                    b = tile(("o", i))
                    wait(dve, rt_done, l, 8 + i + 1)
                    V.scalar_tensor_tensor(out=cat[:, i, :], in0=b[:, :], scalar=par[:, 16:17], in1=rt[:, i % 2, :],
                                           op0=ALU.mult, op1=ALU.mult).then_inc(dve_took.s, 1)
                    wait(dve, dve_took, l, taken[("o", i)][1])
                    last = V.tensor_tensor(cat[:, i, :], cat[:, i, :], sg[:, i, :], ALU.mult)
                last.then_inc(cat_g.s, 1)

                for h in range(9):
                    if h < 8:
                        wait(dve, bm_done, l, h + 1)
                        for cb in range(4):
                            if cb % 2 == 0:
                                b = tile(("S", h, cb // 2))
                                pass_on(dve)
                            last = V.tensor_tensor_reduce(
                                out=P_sb[:, h % 3, cb, :], in0=b[:, (cb % 2) * 256:(cb % 2 + 1) * 256],
                                in1=bm[:, h % 2, MASK_OF[cb], :], scale=1.0, scalar=3.0 * NEG,
                                op0=ALU.add, op1=ALU.max, accum_out=mx[:, h % 2, cb:cb + 1])
                            if cb % 2:
                                last.then_inc(dve_took.s, 1)
                        wait(dve, dve_took, l, taken[("S", h, 1)][1])
                        V.tensor_scalar(nmx[:, h % 2, :], mx[:, h % 2, :], -1.0, None, ALU.mult
                                        ).then_inc(smax_done.s, 1)
                    if h >= 1:
                        g = h - 1
                        wait(dve, sexp_done, l, g + 1)
                        step(V.reciprocal(rsm[:, g % 2, :], sm[:, g % 2, :]))
                        V.tensor_tensor(P_sb[:, g % 3, :, :], P_sb[:, g % 3, :, :], rep(rsm[:, g % 2, :], 256), ALU.mult
                                        ).then_inc(prob_done.s, 1)

                for m in range(4):
                    for tt in range(TT):
                        b = tile(("y", m, tt))
                        cols = slice(m * 256, (m + 1) * 256)
                        tmp = pool_c[:, (tt % 2) * 256:(tt % 2 + 1) * 256]
                        V.tensor_tensor(tmp, b[:, 0:256], g1_bc[:, cols], ALU.mult).then_inc(dve_took.s, 1)
                        wait(dve, dve_took, l, taken[("y", m, tt)][1])
                        last = V.tensor_tensor(x_sb[:, tt, cols], x_sb[:, tt, cols], tmp, ALU.add)
                        if m == 3:
                            last.then_inc(x_mid.s, 1)
                norm(2)

                def v4(a):
                    return a.rearrange("p (t g e) -> p (t g) e", g=NG, e=EG)
                score, sel, oh1, oh2, tmp, sel2 = (R[n] for n in ("score", "sel", "oh1", "oh2", "tmp", "sel2"))
                pick1, pick2, mask, rank, dst, ge, t2, t3 = (
                    R[n] for n in ("pick1", "pick2", "mask", "rank", "dst", "ge", "t2", "t3"))
                m1, m2, gs, mf, gh, q4 = (small[i][:, 0:16] for i in range(6))
                gm = small[6][:, 0:4]
                b = tile(("logits",))
                wait(dve, route_exp, l, 1)
                V.tensor_scalar(score, score, 1.0, None, ALU.add).then_inc(dve_took.s, 1)
                wait(dve, dve_took, l, taken[("logits",)][1])
                step(V.reciprocal(score, score))
                step(V.tensor_tensor(sel.rearrange("p (t e) -> p t e", e=NE), score.rearrange("p (t e) -> p t e", e=NE),
                                     again(rb_sb[:, :], TT), ALU.add))

                def first_of(vals, best, n, order, out, scratch):
                    step(V.tensor_tensor(scratch, vals, rep(best, n), ALU.is_equal))
                    step(V.tensor_tensor(scratch, scratch, order, ALU.mult))
                    step(V.tensor_reduce(mf[:, 0:best.shape[1]], scratch, AX, ALU.max))
                    step(V.tensor_tensor(out, scratch, rep(mf[:, 0:best.shape[1]], n), ALU.is_equal))

                order8 = again(iota8[:, 0:EG], TT * NG)
                step(V.tensor_reduce(m1, v4(sel), AX, ALU.max))
                first_of(v4(sel), m1, EG, order8, v4(oh1), v4(tmp))
                step(V.scalar_tensor_tensor(out=sel2, in0=oh1, scalar=NEG, in1=sel, op0=ALU.mult, op1=ALU.add))
                step(V.tensor_reduce(m2, v4(sel2), AX, ALU.max))
                first_of(v4(sel2), m2, EG, order8, v4(oh2), v4(tmp))
                step(V.tensor_tensor(gs, m1, m2, ALU.add))
                gs_v = gs.rearrange("p (t g) -> p t g", g=NG)
                step(V.tensor_reduce(gm, gs_v, AX, ALU.max))
                first_of(gs_v, gm, NG, again(iota4[:, :], TT), gh.rearrange("p (t g) -> p t g", g=NG),
                         q4.rearrange("p (t g) -> p t g", g=NG))
                step(V.tensor_tensor(v4(pick1), v4(oh1), rep(gh, EG), ALU.mult))
                step(V.tensor_tensor(v4(pick2), v4(oh2), rep(gh, EG), ALU.mult))
                V.tensor_tensor(mask, pick1, pick2, ALU.add).then_inc(mask_done.s, 1)
                def te(a):
                    return a.rearrange("p (t e) -> p t e", e=NE)
                for j, pk in enumerate((pick1, pick2)):
                    step(V.tensor_tensor(tmp, pk, score, ALU.mult))
                    step(V.tensor_reduce(gwt[:, j, :], te(tmp), AX, ALU.add))
                wsum = small[7][:, 0:4]
                step(V.tensor_tensor(wsum, gwt[:, 0, :], gwt[:, 1, :], ALU.add))
                step(V.reciprocal(wsum, wsum))
                step(V.tensor_tensor(gwt[:, :, :], gwt[:, :, :], again(wsum, 2), ALU.mult))
                b = tile(("rank",))
                step(V.tensor_copy(rank, b[:, 0:128]))
                cntT, cnt = small[8], small[9]
                step(V.tensor_copy(cnt, b[:, 128:160]))
                V.tensor_copy(cntT[0:NE, 0:1], b[0:NE, 160:161]).then_inc(dve_took.s, 1)
                wait(dve, dve_took, l, taken[("rank",)][1])
                thr = small[10]
                step(V.tensor_scalar(thr[:, 0:7], iota_s[:, 1:8], 64.0, None, ALU.mult))
                novT, c7 = small[11], small[12]
                step(V.tensor_tensor(c7[0:NE, 0:7], rep(cntT[0:NE, 0], 7), thr[0:NE, 0:7], ALU.is_gt))
                step(V.tensor_reduce(novT[0:NE, 0:1], c7[0:NE, 0:7], AX, ALU.add))
                V.tensor_scalar(t3[0:NE, :], ones[0:NE, :], novT[0:NE, 0:1], None, ALU.mult).then_inc(over_in.s, 1)
                cmp7 = wide.rearrange("p b e -> p (b e)")[:, 0:NE * 7].rearrange("p (e m) -> p e m", m=7)
                step(V.tensor_tensor(cmp7, rep(cnt, 7), again(thr[:, 0:7], NE), ALU.is_gt))
                nov = small[13]
                step(V.tensor_reduce(nov, cmp7, AX, ALU.add))
                b = tile(("over",))
                before_e, total = small[14], small[15]
                step(V.tensor_copy(before_e, b[:, 0:NE]))
                V.tensor_copy(total[:, 0:1], b[:, NE:NE + 1]).then_inc(dve_took.s, 1)
                wait(dve, dve_took, l, taken[("over",)][1])
                upto_e, ex = small[16], small[17]
                step(V.tensor_tensor(upto_e, before_e, nov, ALU.add))
                step(V.tensor_tensor(wide, again(upto_e, MAXOV), rep(iota_s[:, 0:MAXOV], NE), ALU.is_le))
                step(V.tensor_reduce(ex[:, 0:MAXOV], wide, AX, ALU.add))
                step(V.tensor_scalar(ex[:, 0:MAXOV], ex[:, 0:MAXOV], float(NE - 1), None, ALU.min))
                V.tensor_copy(blk_exp[:, 0:NE], iota_s[:, 0:NE])
                step(V.tensor_copy(blk_exp[:, NE:NBLK], ex[:, 0:MAXOV]))
                half_i, half_f = small[20][:, 0:1].bitcast(I32), small[21][:, 0:1]
                step(V.tensor_scalar(total[:, 1:2], total[:, 0:1], 1.0, None, ALU.add))
                step(V.tensor_copy(half_i, total[:, 1:2]))
                step(V.tensor_scalar(half_i, half_i, 1, None, ALU.arith_shift_right))
                step(V.tensor_copy(half_f, half_i))
                step(V.tensor_copy(pairs[:, 0:1], pairs_f[:, 0:1]))
                step(V.tensor_scalar(pairs[:, 1:2], half_f, float(NE // 2 - 1), None, ALU.add))
                step(V.scalar_tensor_tensor(out=pairs_f[:, 0:1], in0=half_f, scalar=float(NE // 2),
                                            in1=pairs_f[:, 0:1], op0=ALU.add, op1=ALU.add))
                shift_e = small[18]
                step(V.tensor_scalar(shift_e, before_e, float(NE - 1), 64.0, ALU.add, ALU.mult))
                step(V.tensor_tensor(shift_e, shift_e, iota_e[:, :], ALU.subtract))
                step(V.tensor_scalar(ge, rank, float(SLOTS), None, ALU.is_ge))
                step(V.tensor_tensor(te(ge), te(ge), again(shift_e, TT), ALU.mult))
                step(V.tensor_tensor(dst, rank, ge, ALU.add))
                step(V.tensor_tensor(te(dst), te(dst), again(iota_e[:, :], TT), ALU.add))
                rowf = small[19][:, 0:8]
                for j, pk in enumerate((pick1, pick2)):
                    step(V.tensor_tensor(tmp, pk, dst, ALU.mult))
                    step(V.tensor_reduce(rowf[:, j * 4:(j + 1) * 4], te(tmp), AX, ALU.add))
                row_v = row_of[:, :, :].rearrange("p j t -> p (j t)")
                step(V.tensor_copy(row_v, rowf))
                ia, fa = (small[20][:, 0:8].bitcast(I32), small[21][:, 0:8])
                ib, fb = (small[22][:, 0:8].bitcast(I32), small[23][:, 0:8])
                step(V.tensor_scalar(ia, row_v, 6, None, ALU.arith_shift_right))
                step(V.tensor_scalar(ib, row_v, SLOTS - 1, None, ALU.bitwise_and))
                step(V.tensor_copy(fa, ia))
                step(V.tensor_copy(fb, ib))
                step(V.tensor_tensor(oslot, again(iota_s[:, :], 8), rep(fb, SLOTS), ALU.is_equal))
                step(V.tensor_tensor(oblk, again(iota_s[:, 0:NBLK], 8), rep(fa, NBLK), ALU.is_equal))
                V.tensor_tensor(oblk, oblk, rep(tok8[:, :], NBLK), ALU.mult).then_inc(slot1h.s, 1)
                b = tile(("slot",))
                V.tensor_copy(slot_tok[:, :], b[0:SLOTS, 0:NBLK]).then_inc(dve_took.s, 1)
                wait(dve, dve_took, l, taken[("slot",)][1])
                dve.sem_inc(routed.s, 1)
                pairs0, more = reg_counts(dve)
                G0 = pairs0 * 2

                def own(ins, G, n):
                    ins.then_inc(dve_blk.s, 1)
                    dve.wait_ge(dve_blk.s, G * 4 + n)

                def modulate(u, G):
                    b = bank[u][:, :].rearrange("p (k s) -> p k s", k=KD)
                    wait_blk(dve, "xg_T", G, 1)
                    wait_blk(dve, "up_ready", G, -1)
                    own(V.tensor_tensor(hgT[:, u, :, :], b, rep(A2[:, :], SLOTS), ALU.mult), G, 1)
                    V.tensor_tensor(hgT[:, u, :, :], hgT[:, u, :, :], rep(B2[:, :], SLOTS), ALU.add
                                    ).then_inc(blk["hg_done"].s, 1)

                def silu(u, G):
                    wait_blk(dve, "up_exp", G, 1)
                    e1 = sil[:, u, 0:256]
                    own(V.tensor_scalar(e1, e1, 1.0, None, ALU.add), G, 2)
                    own(V.reciprocal(e1, e1), G, 3)
                    own(V.tensor_tensor(e1, bank[2 + u][:, 0:256], e1, ALU.mult), G, 4)
                    V.tensor_tensor(sil[:, u, 256:512], e1, bank[2 + u][:, 256:512], ALU.mult
                                    ).then_inc(blk["g_done"].s, 1)

                modulate(0, G0)
                silu(0, G0)
                modulate(1, G0 + 1)
                with dve.Fori(0, more) as i:
                    G = G0 + i * 2
                    silu(1, G + 1)
                    modulate(0, G + 2)
                    silu(0, G + 2)
                    modulate(1, G + 3)
                silu(1, G0 + more * 2 + 1)

                for tt in range(TT):
                    u = tt % 2
                    wait(dve, yrows_in[u], l, 32 * (tt // 2 + 1))
                    y0, y1 = yg[:, u, 0, :], yg[:, u, 1, :]
                    step(V.tensor_scalar(y0, y0, gwt[:, 0, tt:tt + 1], None, ALU.mult))
                    step(V.scalar_tensor_tensor(out=y0, in0=y1, scalar=gwt[:, 1, tt:tt + 1], in1=y0, op0=ALU.mult,
                                                op1=ALU.add))
                    step(V.tensor_tensor(y0, y0, g2_bc[:, :], ALU.mult))
                    V.tensor_tensor(x_sb[:, tt, :], x_sb[:, tt, :], y0, ALU.add).then_inc(x_new.s, 1)
            assert steps[0] == DVE_STEPS, steps

        @block.gpsimd
        def _(pool):
            G_ = nc.gpsimd
            n0 = [0]
            steps = [0]

            def link0(ins):
                n0[0] += 1
                ins.then_inc(pstep.s, 1)
                pool.wait_ge(pstep.s, n0[0])

            def link(l, ins):
                steps[0] += 1
                ins.then_inc(pool_step.s, 1)
                wait(pool, pool_step, l, steps[0])

            G_.memset(pool_b[:, 4608:5120], 0.0).then_inc(bias_zero.s, 1)
            G_.memset(zeros_y, 0.0).then_inc(y_zeros.s, 1)
            for t_ in (ident, upto, since, after, before):
                last = G_.memset(t_[:, :], 0.0 if t_ is ident else 1.0)
            link0(last)
            for t_, op, fill, cm, st_, base in ((ident, ALU.not_equal, 1.0, 1, -1, 0),
                                                (upto, ALU.is_ge, 0.0, -1, 1, 0),
                                                (since, ALU.is_ge, 0.0, 1, -1, 0),
                                                (after, ALU.is_gt, 0.0, 1, -1, 0),
                                                (before, ALU.is_gt, 0.0, -1, 1, 0)):
                last = G_.affine_select(out=t_[:, :], in_=t_[:, :], compare_op=op, fill=fill, base=base,
                                        pattern=[[st_, P]], channel_multiplier=cm)
            link0(last)
            G_.iota(io_p[:, :], pattern=[[0, P]], base=0, channel_multiplier=1)
            G_.iota(io_f[:, :], pattern=[[1, P]], base=0, channel_multiplier=0)
            G_.iota(io_8[:, :], pattern=[[-1, EG]], base=EG, channel_multiplier=0)
            link0(G_.iota(io_t[:, :], pattern=[[0, 2], [P, TT]], base=0, channel_multiplier=1))
            link0(G_.iota(io_e[:, :], pattern=[[SLOTS, NE]], base=0, channel_multiplier=0))
            G_.tensor_copy(iota_s[:, :], io_f[:, 0:64])
            G_.tensor_copy(iota8[:, 0:EG], io_8[:, :])
            G_.tensor_copy(iota4[:, :], io_8[:, 4:8])
            G_.tensor_copy(tok8[:, :], io_t[:, :])
            link0(G_.tensor_copy(iota_e[:, :], io_e[:, :]))
            pool.sem_inc(consts_p.s, 1)

            with pool.Fori(0, L) as l:
                steps[0] = 0
                pool.wait_ge(x_new.s, l * TT + TT)
                pass_on(pool)
                for half in range(2):
                    rows = slice(64 * (1 - half), 64 * (1 - half) + 64)
                    G_.memset(qz[rows, half, :], 0.0)
                    last = G_.memset(qz_l[rows, half * 1024:(half + 1) * 1024], 0.0)
                last.then_inc(zeroed_q.s, 1)
                wait(pool, zeroed_q, l, 1)
                pool.wait_ge(y_zeroed.s, 16)
                wait(pool, act_took, l, taken[("b", 1, 1)][1])
                for n, lev in enumerate(LEVELS):
                    if n >= 2:
                        wait(pool, tile_ready, l, index[("P", LEVELS[n - 2], TT - 1)] + 1)
                    hh = 1 << lev
                    e = k_lev[n % 2].rearrange("p (n a h) -> p n a h", a=2, h=hh)
                    f, g = (bT[:, r, :].rearrange("p (n a h) -> p n a h", a=2, h=hh) for r in range(2))
                    G_.tensor_tensor(e[:, :, 0, :], rep(f[:, :, 0, hh - 1], hh), f[:, :, 0, :], ALU.subtract)
                    G_.tensor_tensor(e[:, :, 1, :], rep(g[:, :, 1, 0], hh), g[:, :, 1, :], ALU.subtract
                                     ).then_inc(diff_k.s, 1)
                    wait(pool, exp_k, l, n + 1)
                    if n == 0:
                        wait(pool, tile_ready, l, index[("U", 1, 1)] + 1)
                        pass_on(pool)
                        for half in range(2):
                            rows = slice(64 * (1 - half), 64 * (1 - half) + 64)
                            last = G_.memset(q_lev[1][rows, half * 1024:(half + 1) * 1024], 0.0)
                        last.then_inc(zeroed_l.s, 1)
                        wait(pool, zeroed_l, l, 1)
                    G_.tensor_tensor(k_lev[n % 2], k_lev[n % 2], kT, ALU.mult).then_inc(lev_k.s, 1)
                wait(pool, tile_ready, l, index[("P", 0, TT - 1)] + 1)
                pass_on(pool)
                for half in range(2):
                    rows = slice(64 * (1 - half), 64 * (1 - half) + 64)
                    last = G_.memset(qnz[rows, :, half, :], 0.0)
                last.then_inc(zeroed_n.s, 1)
                wait(pool, zeroed_n, l, 1)
                wait(pool, gtab_in, l, 16 * 8)
                for h in range(8):
                    if h >= 2:
                        wait(pool, smax_done, l, h - 1)
                    for m in range(3):
                        src = ap_of(gtab[:, h, :], RPB_PAD - 8 * m, [[1, 32], [31, ROWS]])
                        last = G_.tensor_tensor(bm[:, h % 2, m, :].rearrange("p (c r) -> p c r", r=ROWS), src,
                                                rep(wneg[:, m, :], ROWS), ALU.add)
                    last.then_inc(bm_done.s, 1)

                wait(pool, bm_done, l, 8)
                wait(pool, routed, l, 1)
                for i in range(2):
                    wait(pool, xn_stored[i], l, 32)
                pairs0, more = reg_counts(pool)
                G0 = pairs0 * 2

                def gather(u, G, row):
                    wait_blk(pool, "xg_T", G, -1)
                    pass_on(pool)
                    G_.tensor_copy(tok_now[:, u:u + 1], slot_tok[:, bass.ds(row, 1)]).then_inc(tok_set.s, 1)
                    pool.wait_ge(tok_set.s, G + 1)
                    pass_on(pool)
                    G_.indirect_dma_start(xg[:, u, :], None, xn_dram, bass.IndirectOffsetOnAxis(tok_now[:, u:u + 1], 0)
                                          ).then_inc(gathered[u].s, 16)

                for u in range(2):
                    gather(u, G0 + u, u)
                G_.memset(pool_b[:, 4608:5120], 0.0).then_inc(bias_zero.s, 1)
                with pool.Fori(0, more) as i:
                    for u in range(2):
                        gather(u, G0 + i * 2 + (2 + u), i * 2 + (2 + u))
                for u in range(2):
                    pool.wait_ge(y_stored[u].s, pairs0 * 32 + more * 32 + 64)
                pass_on(pool)
                for tt in range(TT):
                    if tt >= 2:
                        pool.wait_ge(x_new.s, l * TT + TT + tt - 1)
                        pass_on(pool)
                    for j in range(2):
                        G_.indirect_dma_start(yg[:, tt % 2, j, :], None, y_dram,
                                              bass.IndirectOffsetOnAxis(row_of[:, j, tt:tt + 1], 0)
                                              ).then_inc(yrows_in[tt % 2].s, 16)
            assert steps[0] == POOL_STEPS, steps


_INS = ["x", "c", "w_ada", "b_ada", "attn_norm", "ffn_norm", "w_in", "gla_gate_w", "gla_gate_b", "gla_out_norm",
        "na_q_norm", "na_k_norm", "na_rpb", "w_out", "router_w", "router_b", "w1", "w3", "w2"]


def kernel(**inputs):
    import numpy as np
    import concourse.bacc as bacc
    from concourse.bass_utils import run_bass_kernel_spmd

    nc = bacc.Bacc("TRN2", target_bir_lowering=False, num_devices=1)
    arrays, aps = {}, {}
    for name in _INS:
        a = np.ascontiguousarray(inputs[name])
        arrays[name] = a
        aps[name] = nc.dram_tensor(name, a.shape, mybir.dt.from_np(a.dtype), kind="ExternalInput").ap()
    aps["out"] = nc.dram_tensor("out", (1, T, D), F32, kind="ExternalOutput").ap()
    build(nc, aps)
    r = run_bass_kernel_spmd(nc, [arrays], core_ids=[0])
    return r.results[0]["out"]
```

```python
from contextlib import ExitStack

import concourse.bass as bass
from concourse import mybir

F32 = mybir.dt.float32
I32 = mybir.dt.int32
ALU = mybir.AluOpType
ACT = mybir.ActivationFunctionType
AX = mybir.AxisListType.X

P = 128
T = 512
D = 1024
L = 2
KD = D // P
TT = T // P
ROWS, COLS = 8, 64
NE, NG, EG = 32, 4, 8
DE = 512
SLOTS = 64
MAXOV = 2 * T // SLOTS
NBLK = NE + MAXOV
EPS = 1e-6
NEG = -1e30
TAU_INV = 1.0 / 16.0
C_QK, C_V, C_G, C_LF, C_QN, C_KN, C_VN = 0, 512, 1024, 1536, 1568, 2080, 2592
IN_W = 3104
RPB_W = 15 * 31
RPB_PAD = 16
KEY_AT = [0, 1, 3, 4]
RPB_OFF = [0, -8, -8, -16]
MASK_OF = [0, 1, 1, 2]
LEVELS = [6, 5, 4, 3, 2, 1, 0]
LAST_Y = [("y", 0), ("y", 1), ("y", 2), ("x", 0), ("y", 3), ("x", 1), ("x", 2), ("x", 3)]
FILLERS = ("kn", "vf", "vt", "ada")
RING = 6
NPAR = 19
ADA_PIECES = 24
WIN_PIECES = 12
DVE_STEPS, ACT_STEPS = 254, 24


class Signal:

    def __init__(self, nc, ctx, name, per, first=0):
        self.s = ctx.enter_context(nc.semaphore(name))
        self.per, self.first = per, first

    def at(self, l, n):
        assert self.first + n > 0
        return l * self.per + self.first + n

def tile_plan():
    t = [(("x", 1, tt, h), "ad"[h]) for tt in range(TT) for h in range(2)]
    t += [(("q", d), "a") for d in range(2)] + [(("ada", 0), "d"), (("ada", 0, 1), "d")]
    t += [(("k", d), "a") for d in range(2)] + [(("ada", 1), "d"), (("lf",), "a")]
    t += [(("v", 0, c), "a") for c in range(3)] + [(("ada", 2), "d"), (("v", 0, 3), "a")]
    t += [(("z", c), "d") for c in range(TT)]
    t += [(("v", 1, c), "a") for c in range(2)]
    t += [(("b", r, d), "a") for r in range(2) for d in range(2)]
    t += [(("v", 1, c), "a") for c in range(2, TT)]
    for c in range(TT):
        t += [(("kx", c), "a"), (("kt", c), "d")]
    t += [(("ada", 3), "d"), (("ada", 3, 1), "d")] + [(("g", h), "a") for h in range(2)]
    t += [(("U", 0, c), "d") for c in (0, 1, 2)] + [(("U", 1, c), "d") for c in (3, 2, 1)]
    t += [(("P", 7, c), "a") for c in range(TT)] + [(("g", h), "a") for h in range(2, 4)]
    fill = [[("kn", 0)], [("kn", 1)], [("kn", 2)], [("kn", 3)], [("ada", 4), ("vf", 0)],
            [("vf", 1), ("vt", 0, 0), ("vt", 0, 1)],
            [("vf", 2), ("vt", 1, 0), ("vt", 1, 1), ("vf", 3), ("vt", 2, 0), ("vt", 2, 1), ("vt", 3, 0), ("vt", 3, 1)]]
    who = {"kn": "d", "ada": "d", "kms": "a", "vf": "a", "vt": "a"}
    for n, lev in enumerate(LEVELS):
        for c in range(TT):
            t += [(("P", lev, c), "d")]
            t += [(("kms", n - 1), "a")] if c == 0 and 1 <= n <= 4 else []
        t += [(k, who[k[0]]) for k in fill[n]]
    for pre in ("qn", "o"):
        ms = pre[0] + "ms"
        t += [((pre, 0), "d"), ((pre, 1), "d"), ((ms, 0), "a")]
        t += [((pre, 2), "d"), ((ms, 1), "a"), ((pre, 3), "d"), ((ms, 2), "a"), ((ms, 3), "a")]
        t += [(("ada", 5), "d")] if pre == "qn" else []
    for h in range(10):
        if h < 8:
            t += [(("S", h, i), "d") for i in range(2)]
        if h >= 2:
            t += [(("PT", h - 2, i), "a") for i in range(2)]
    t += [(("y", m, tt), "d") for m in range(3) for tt in range(TT)]
    for kind, tt in LAST_Y:
        t += [(("y", 3, tt), "d")] if kind == "y" else [(("x", 2, tt, h), "ad"[h]) for h in range(2)]
    t += [(("log_T",), "a"), (("logits",), "d"), (("rank",), "d"), (("over",), "d"), (("slot",), "d")]
    return t

def build(nc, A):
    plan = tile_plan()
    index = {key: n for n, (key, _) in enumerate(plan)}
    taken, seen = {}, {"a": 0, "d": 0}
    mean_of = {"kn": "kms", "qn": "qms", "o": "oms"}
    order = sorted(plan, key=lambda e: index[(mean_of[e[0][0]], e[0][1])] + 0.5 if e[0][0] in mean_of else index[e[0]])
    for key, who in order:
        seen[who] += 1
        taken[key] = (who, seen[who])

    with ExitStack() as ctx:
        def sb(name, shape, dt=F32):
            return ctx.enter_context(nc.sbuf_tensor(name, shape, dt))

        def sig(name, per, first=0):
            return Signal(nc, ctx, name, per, first)

        ring = sb("ring", [P, 6, 4096])
        x_sb = sb("x_sb", [P, TT, D])
        hT = sb("hT", [P, KD, T])
        pool_a = sb("pool_a", [P, 6656])
        pool_b = sb("pool_b", [P, 5632])
        pool_c = sb("pool_c", [P, 2048])
        g1_bc = sb("g1_bc", [P, D])
        g2_bc = sb("g2_bc", [P, D])
        acc = sb("acc", [P, D])
        brow = sb("brow", [P, 2, 256])
        ident = sb("ident", [P, P])
        ones = sb("ones", [P, P])
        mean64 = sb("mean64", [P, P])
        upto = sb("upto", [P, P])
        since = sb("since", [P, P])
        after = sb("after", [P, P])
        before = sb("before", [P, P])
        lvl = sb("lvl", [P, 7, P], mybir.dt.uint8)
        par_all = sb("par_all", [P, L, NPAR])
        par = sb("par", [P, NPAR])
        anorm0 = sb("anorm0", [P, KD])
        c_sb = sb("c_sb", [P, KD])
        A1, B1 = sb("A1", [P, KD]), sb("B1", [P, KD])
        A2, B2 = sb("A2", [P, KD]), sb("B2", [P, KD])
        eps_c = sb("eps_c", [P, 1])
        gatew = sb("gatew", [33, 512])
        rw_sb = sb("rw_sb", [P, KD, NE])
        rb_sb = sb("rb_sb", [P, NE])
        ssq = sb("ssq", [P, 8])
        rstd = sb("rstd", [P, 8])
        mx = sb("mx", [P, 2, 4])
        nmx = sb("nmx", [P, 2, 4])
        sm = sb("sm", [P, 2, 4])
        rsm = sb("rsm", [P, 2, 4])
        dec = sb("dec", [P, 2, 8])
        gwt = sb("gwt", [P, 2, TT])
        row_of = sb("row_of", [P, 2, TT], I32)
        slot_tok = sb("slot_tok", [SLOTS, NBLK], I32)
        tok_now = sb("tok_now", [SLOTS, 2], I32)
        wneg = sb("wneg", [P, 3, 32])
        pairs = sb("pairs", [P, 2], I32)
        pairs_f = sb("pairs_f", [P, 1])
        one_c = sb("one_c", [P, 1])
        pad0 = sb("pad0", [L, RPB_PAD])
        ctmp = sb("ctmp", [P, KD])
        qscale = sb("qscale", [P, 1])
        lo = sb("lo", [P, 4])
        tok8 = sb("tok8", [P, 8])

        flat = ring[:, :, :].rearrange("p s n -> p (s n)")
        win_w = [flat[:, i * 2048:(i + 1) * 2048].rearrange("p (k n) -> p k n", k=KD) for i in range(2)]
        ada_w = [v[:, a:a + 2048].rearrange("p (k n) -> p k n", k=KD)
                 for v, a in ((flat, 4096), (flat, 6144), (pool_b, 0), (pool_b, 2048))]
        bias_row = [brow[:, 0, :], brow[:, 1, :], pool_b[:, 4608:4864], pool_b[:, 4864:5120]]
        Z = 8192

        def z(n):
            nonlocal Z
            Z += n
            return flat[:, Z - n:Z]
        eq, ek2, qz_l, kz_l = z(1024), z(1024), z(2048), z(1024)
        wlf = ek2[:, 0:256].rearrange("p (k n) -> p k n", k=KD)
        qnz = flat[:, 8192:8192 + 4096].rearrange("p (d r t) -> p d r t", d=4, r=2)
        la = z(2048).rearrange("p (c n) -> p c n", c=TT)
        amat = la.rearrange("p c n -> p (c n)").rearrange("p (c h i) -> p c h i", c=TT, h=4)
        ekx = z(1024).rearrange("p (u n) -> p u n", u=2)
        bT = z(2048).rearrange("p (r n) -> p r n", r=2)
        khat = z(2048).rearrange("p (c n) -> p c n", c=TT)
        zeros_y = flat[:, 6 * 4096 - 2048:6 * 4096 - 1024]
        q_lev = [qz_l, khat.rearrange("p c n -> p (c n)")]
        k_lev = [kz_l, ek2]
        sg_exp = q_lev[1].rearrange("p (h n) -> p h n", h=4)
        gtab = flat[:, Z - 2048 - 8 * 265:Z - 2048].rearrange("p (h m) -> p h m", h=8)
        bm = khat.rearrange("p c n -> p (c n)")[:, 0:1536].rearrange("p (u s n) -> p u s n", u=2, s=3)
        v_tm = z(2048).rearrange("p (c n) -> p c n", c=TT)
        sg = z(2048).rearrange("p (h n) -> p h n", h=4)
        assert Z == 6 * 4096
        cat = hT
        qz = pool_a[:, 0:2048].rearrange("p (r n) -> p r n", r=2)
        kT = pool_a[:, 2048:3072]
        qd = pool_a[:, 3072:5120].rearrange("p (r n) -> p r n", r=2)
        st = pool_a[:, 5120:6656].rearrange("p (r c n) -> p r c n", r=2, c=3)
        P_sb = pool_a[:, 0:3072].rearrange("p (u c n) -> p u c n", u=3, c=4)
        PT_sb = pool_a[:, 4096:6144].rearrange("p (u c n) -> p u c n", u=2, c=4)
        log_T = pool_a[:, 1024:1152]
        xg = pool_a[0:SLOTS, 0:2048].rearrange("p (u n) -> p u n", u=2)
        hgT = pool_a[:, 2048:3072].rearrange("p (u k s) -> p u k s", u=2, k=KD)
        sil = pool_a[:, 3072:4096].rearrange("p (u n) -> p u n", u=2)
        gTs = pool_a[:, 4096:4608].rearrange("p (u n) -> p u n", u=2)
        y_sb = pool_a[:, 4608:5632].rearrange("p (u n) -> p u n", u=2)
        kn = pool_b[:, 0:2048].rearrange("p (d t) -> p d t", d=4)
        vn = pool_b[:, 2048:5632].rearrange("p (n f) -> p n f", n=7)
        sq = pool_c[:, 0:1024].rearrange("p (u n) -> p u n", u=2)
        rt = pool_c[:, 1024:2048].rearrange("p (u n) -> p u n", u=2)
        lfx = pool_c[0:33, 0:512]
        xn = [[pool_c[:, a * D:(a + 1) * D] for a in (0, 1, 0, 1)],
              [pool_a[:, 2 * D:3 * D], pool_a[:, 3 * D:4 * D], pool_c[:, D:2 * D], pool_c[:, 0:D]]]
        yg = [v.rearrange("p (j n) -> p j n", j=2)
              for v in (hT[:, 0:4, :].rearrange("p k t -> p (k t)"), hT[:, 4:8, :].rearrange("p k t -> p (k t)"),
                        pool_a[:, 2048:4096], pool_a[:, 4096:6144])]
        w13 = [[ring[:, 3 * u + i, :].rearrange("p (k n) -> p k n", k=KD) for i in range(2)] for u in range(2)]
        w2s = [ring[:, 3 * u + 2, :].rearrange("p (h q n) -> p h q n", h=2, q=2) for u in range(2)]

        def rt_at(a, n, dt=F32):
            v = pool_b[:, a:a + n]
            return v if dt == F32 else v.bitcast(dt)
        R = {name: rt_at(i * 128, 128) for i, name in enumerate(
            ("score", "sel", "oh1", "oh2", "tmp", "sel2", "first", "lin", "pick1", "pick2", "mask",
             "rank", "dst", "ge", "t2", "t3"))}
        small = [rt_at(2048 + i * 32, 32) for i in range(24)]
        oslot = rt_at(2816, 8 * 64).rearrange("p (j n) -> p j n", j=8)
        oblk = rt_at(3328, 8 * NBLK).rearrange("p (j n) -> p j n", j=8)
        wide = rt_at(3712, MAXOV * NE).rearrange("p (b e) -> p b e", b=MAXOV)
        blk_exp = rt_at(4224, NBLK, I32)
        blk_real = rt_at(4272, NBLK, I32)
        iota8 = sb("iota8", [P, NE])
        iota4 = sb("iota4", [P, NG])
        iota_e = sb("iota_e", [P, NE])
        iota_s = sb("iota_s", [P, 64])
        io_p, io_f, xor, xsh = (pool_c[:, i * P:(i + 1) * P].bitcast(I32) for i in range(4))
        xfl = pool_c[:, 512:640]
        io_8, io_t, io_e = (pool_c[:, a:b].bitcast(I32) for a, b in ((640, 648), (648, 656), (656, 688)))

        bank = [ctx.enter_context(nc.psum_tensor(f"bank{i}", [P, 512], F32)) for i in range(8)]

        rpb_pad = nc.dram_tensor("rpb_padded", [L, 8 * RPB_W + 2 * RPB_PAD], F32).ap()
        xn_dram = nc.dram_tensor("xn_rows", [T, D], F32).ap()
        y_dram = nc.dram_tensor("y_rows", [NBLK * SLOTS, D], F32).ap()

        tile_ready = sig("tile_ready", len(plan))
        act_took = sig("act_took", seen["a"])
        dve_took = sig("dve_took", seen["d"])
        dve_step = sig("dve_step", DVE_STEPS)
        act_step = sig("act_step", ACT_STEPS)
        consts_p, consts_v = sig("consts_p", 0), sig("consts_v", 0)
        rpb_copied = sig("rpb_copied", 0)
        c_in = sig("c_in", 0)
        x_in, par_in = sig("x_in", 0), sig("par_in", 0)
        c_act = sig("c_act", 0)
        x_new = sig("x_new", TT, TT)
        mod0 = sig("mod0", 0)
        mod_ready = sig("mod_ready", 0)
        win_in = [sig(f"win_in{i}", 16 * WIN_PIECES // 2) for i in range(2)]
        lf_in, gatew_in, gtab_in = sig("lf_in", 16), sig("gatew_in", 48), sig("gtab_in", 16 * 8)
        ada_in = [sig(f"ada_in{i}", 32 * (8 if i < 2 else 4), 32 * 2) for i in range(4)]
        bias_zero = sig("bias_zero", 1)
        ada_used = sig("ada_used", ADA_PIECES, 8)
        wo_in = [sig(f"wo_in{i}", 32) for i in range(2)]
        rstd_done = sig("rstd_done", 8)
        xn_done = sig("xn_done", 8)
        xn_stored = [sig(f"xn_stored{i}", 32) for i in range(2)]
        zeroed_q = sig("zeroed_q", 1)
        zeroed_l = sig("zeroed_l", 1)
        zeroed_n = sig("zeroed_n", 1)
        ln_done = sig("ln_done", 4)
        gexp_done, gate_done = sig("gexp_done", 1), sig("gate_done", 1)
        sg_done = sig("sg_done", 1)
        la_done = sig("la_done", 4)
        dec_done = sig("dec_done", 1)
        ekx_done, khat_done = sig("ekx_done", 4), sig("khat_done", 4)
        st_done = sig("st_done", 1)
        diff_q, diff_k = sig("diff_q", 7), sig("diff_k", 7)
        exp_q, exp_k = sig("exp_q", 7), sig("exp_k", 7)
        lev_q, lev_k = sig("lev_q", 7), sig("lev_k", 7)
        sq_done, rt_done = sig("sq_done", 12), sig("rt_done", 12)
        cat_g = sig("cat_g", 1)
        bm_done = sig("bm_done", 8)
        smax_done, sexp_done = sig("smax_done", 8), sig("sexp_done", 8)
        prob_done = sig("prob_done", 8)
        on_done = sig("on_done", 4)
        cat_n = sig("cat_n", 4)
        x_mid = sig("x_mid", TT)
        mask_done, over_in, slot1h = sig("mask_done", 1), sig("over_in", 1), sig("slot1h", 1)
        slots_set = sig("slots_set", 1)
        routed = sig("routed", 1)
        blk = {n: sig(n, 0) for n in ("xg_T", "hg_done", "up_ready", "up_exp", "g_done", "gT_ready",
                                      "gTs_done", "y_ready", "y_evac")}
        dve_blk = sig("dve_blk", 0)
        w_blk = [[sig(f"{n}_in{u}", 0) for n in ("w1", "w3", "w2")] for u in range(2)]
        gathered = [sig(f"gathered{u}", 0) for u in range(2)]
        tok_set = sig("tok_set", 0)
        y_stored = [sig(f"y_stored{u}", 0) for u in range(2)]
        yrows_in = [sig(f"yrows_in{tt}", 32) for tt in range(TT)]
        out_done = sig("out_done", 0)
        y_zeros, y_zeroed = sig("y_zeros", 0), sig("y_zeroed", 0)
        cstep, pstep = sig("cstep", 0), sig("pstep", 0)
        route_exp = sig("route_exp", 1)

        def ready(eng, l, key):
            eng.wait_ge(tile_ready.s, tile_ready.at(l, index[key] + 1))
            return bank[index[key] % RING]

        passed = {id(e): sig(n, 0) for e, n in ((nc.sync, "passed_sp"), (nc.tensor, "passed_pe"),
                                                (nc.scalar, "passed_act"), (nc.vector, "passed_dve"),
                                                (nc.gpsimd, "passed_pool"))}
        block = ctx.enter_context(nc.Block())

        def pass_on(eng):
            eng.sem_inc(passed[id(eng)].s, 1)

        def blocks(G, n):
            return G + (2 + n)

        def free_bank(pe, l, key):
            n = index[key]
            if n >= RING:
                who, count = taken[plan[n - RING][0]]
                took = act_took if who == "a" else dve_took
                pe.wait_ge(took.s, took.at(l, count))
            return bank[n % RING]

        def reg_counts(eng):
            pass_on(eng)
            return (eng.value_load(pairs[0:1, 0:1], min_val=0, max_val=L * NBLK // 2),
                    eng.value_load(pairs[0:1, 1:2], min_val=NE // 2 - 1, max_val=NBLK // 2 - 1))

        def ap_of(v, off, dims):
            return bass.AP(tensor=v.tensor, offset=v.offset + off, ap=[v.ap[0]] + dims)

        def rep(v, n):
            return bass.AP(tensor=v.tensor, offset=v.offset, ap=list(v.ap) + [[0, n]])

        def again(v, n):
            return bass.AP(tensor=v.tensor, offset=v.offset, ap=[v.ap[0], [0, n]] + list(v.ap[1:]))

        ada_cols = [2048 + 256 * m for m in range(16)] + [256 * m for m in range(8)]
        win_cols = [0, 256, C_V, C_V + 256, C_G, C_G + 256, C_KN, C_KN + 256, C_VN, C_VN + 256, C_QN, C_QN + 256]
        last_of_piece = [("q", 1), ("k", 1), ("v", 0, 3), ("v", 1, 3), ("g", 1), ("g", 3), ("kn", 1), ("kn", 3),
                         ("vf", 1), ("vf", 3), ("qn", 1), ("qn", 3)]
        w_ada_v = A["w_ada"].rearrange("l (p k) n -> l p k n", k=KD)
        w_in_v = A["w_in"].rearrange("l (p k) n -> l p k n", k=KD)
        w_out_v = A["w_out"].rearrange("l (k p) n -> l p k n", p=P)
        w1_v = A["w1"].rearrange("l e (p k) n -> (l e) p (k n)", k=KD)
        w3_v = A["w3"].rearrange("l e (p k) n -> (l e) p (k n)", k=KD)
        w2_v = A["w2"].rearrange("l e (h p q) n -> (l e) p h (q n)", h=2, q=2)
        y_blk = y_dram.rearrange("(b s) (h n) -> b h s n", s=SLOTS, h=2)

        @block.sync
        def _(sp):
            def ada_piece(slot, layer, col):
                sp.dma_start(ada_w[slot], w_ada_v[layer][:, :, col:col + 256]).then_inc(ada_in[slot].s, 16)
                sp.dma_start(bias_row[slot][0:1, :], A["b_ada"].rearrange("l (a n) -> l a n", a=1)[layer][:, col:col + 256]
                             ).then_inc(ada_in[slot].s, 16)

            def load_w1(u, e):
                sp.dma_start(ring[:, 3 * u, :], w1_v[e]).then_inc(w_blk[u][0].s, 16)

            def load_w3(u, e):
                sp.dma_start(ring[:, 3 * u + 1, :], w3_v[e]).then_inc(w_blk[u][1].s, 16)

            def load_w2(u, e):
                sp.dma_start(ring[:, 3 * u + 2, :].rearrange("p (h n) -> p h n", h=2), w2_v[e]
                             ).then_inc(w_blk[u][2].s, 16)

            sp.dma_start(c_sb[:, :], A["c"][0].rearrange("(p k) -> p k", k=KD)).then_inc(c_in.s, 16)
            sp.dma_start(x_sb[:, :, :], A["x"][0].rearrange("(t p) d -> p t d", p=P)).then_inc(x_in.s, 16)
            sp.wait_ge(consts_v.s, 1)
            sp.wait_ge(bias_zero.s, 1)
            for m in range(8):
                if m >= 4:
                    sp.wait_ge(ada_used.s, m - 3)
                ada_piece(m % 4, 0, 256 * m)

            with sp.Fori(0, L) as l:
                def win_piece(m):
                    if m >= 2:
                        sp.wait_ge(tile_ready.s, tile_ready.at(l, index[last_of_piece[m - 2]] + 1))
                    sp.dma_start(win_w[m % 2], w_in_v[l][:, :, win_cols[m]:win_cols[m] + 256]
                                 ).then_inc(win_in[m % 2].s, 16)

                def ada(m):
                    if m == 2:
                        sp.wait_ge(bias_zero.s, bias_zero.at(l, 1))
                    sp.wait_ge(ada_used.s, ada_used.at(l, m - 3 if 2 <= m < 18 else m - 1))
                    pass_on(sp)
                    ada_piece(m % 4 if m < 16 else m % 2, l if m < 16 else (1 - l), ada_cols[m])

                win_piece(0)
                sp.dma_start(wlf[:, :, :], w_in_v[l][:, :, C_LF:C_LF + 32]).then_inc(lf_in.s, 16)
                win_piece(1)
                for m in range(4):
                    ada(m)
                sp.wait_ge(y_zeros.s, 1)
                pass_on(sp)
                with sp.If(l < 1):
                    sp.dma_start(y_dram[NE * SLOTS:].rearrange("(p a) d -> p a d", p=P),
                                 again(zeros_y, MAXOV * SLOTS // P)).then_inc(y_zeroed.s, 16)
                for m in range(4, 8):
                    ada(m)
                win_piece(2)
                ada(8), ada(9)
                win_piece(3)
                for m in range(10, 14):
                    ada(m)
                win_piece(4)
                for m in range(14, 18):
                    ada(m)
                win_piece(5)
                win_piece(6), win_piece(7)
                ada(18), win_piece(8)
                ada(19), ada(20), win_piece(9)
                ada(21), ada(22), win_piece(10)
                ada(23), win_piece(11)
                sp.wait_ge(tile_ready.s, tile_ready.at(l, index[("qn", 3)] + 1))
                load_w1(0, l * NE)

                def wo_piece(m):
                    sp.dma_start(ada_w[m % 2], w_out_v[l][:, :, m * 256:(m + 1) * 256]).then_inc(wo_in[m % 2].s, 16)
                for m in range(2):
                    sp.wait_ge(ada_used.s, ada_used.at(l, ADA_PIECES - 1 + m))
                    wo_piece(m)
                sp.wait_ge(cat_n.s, cat_n.at(l, 4))
                load_w2(0, l * NE)
                load_w1(1, l * NE + 1), load_w3(1, l * NE + 1), load_w2(1, l * NE + 1)
                for m in range(2, 4):
                    sp.wait_ge(tile_ready.s, tile_ready.at(l, index[("y", m - 2, TT - 1)] + 1))
                    wo_piece(m)
                sp.wait_ge(tile_ready.s, tile_ready.at(l, index[("y", 3, TT - 1)] + 1))
                load_w3(0, l * NE)
                sp.wait_ge(routed.s, routed.at(l, 1))
                pairs0, more = reg_counts(sp)
                with sp.Fori(0, more) as i:
                    for u in range(2):
                        G = pairs0 * 2 + i * 2 + (2 + u)
                        e = l * NE + sp.value_load(blk_exp[0:1, bass.ds(i * 2 + (2 + u), 1)], min_val=0,
                                                   max_val=NE - 1)
                        real = sp.value_load(blk_real[0:1, bass.ds(i * 2 + (2 + u), 1)], min_val=0, max_val=1)
                        sp.wait_ge(blk["up_ready"].s, blocks(G, -1))
                        pass_on(sp)
                        with sp.If(real > 0):
                            load_w1(u, e)
                            load_w3(u, e)
                        with sp.If(real < 1):
                            sp.sem_inc(w_blk[u][0].s, 16)
                            sp.sem_inc(w_blk[u][1].s, 16)
                        sp.wait_ge(blk["y_ready"].s, blocks(G, -1))
                        pass_on(sp)
                        with sp.If(real > 0):
                            load_w2(u, e)
                        with sp.If(real < 1):
                            sp.sem_inc(w_blk[u][2].s, 16)
                sp.wait_ge(yrows_in[TT - 1].s, yrows_in[TT - 1].at(l, 32))
                pass_on(sp)
            for tt in range(TT):
                sp.wait_ge(x_new.s, L * TT + tt + 1)
                sp.dma_start(A["out"][0][tt * P:(tt + 1) * P, :], x_sb[:, tt, :]).then_inc(out_done.s, 16)
            sp.wait_ge(out_done.s, 16 * TT)

        @block.tensor
        def _(pe):
            def mm(out, lhsT, rhs, start, stop):
                return nc.tensor.matmul(out, lhsT, rhs, start=start, stop=stop, skip_group_check=True)

            def sum_chunk(out, cols):
                for k in range(KD):
                    last = mm(out[:, k:k + 1], acc[:, :].rearrange("p (n k) -> p k n", k=KD)[:, k, :],
                              ones[:, 0:1], True, True)
                return last

            pe.wait_ge(consts_p.s, 1)
            pe.wait_ge(consts_v.s, 2)
            for n in ("xg_T", "up_ready", "gT_ready", "y_ready"):
                pe.sem_inc(blk[n].s, 2)
            for n in range(2):
                pe.wait_ge(ada_used.s, 4 * (n + 1))
                sum_chunk(bank[7][:, n * 8:n * 8 + 8], n).then_inc(mod0.s, 1)

            with pe.Fori(0, L) as l:
                def norm_transposes(which, tt):
                    pe.wait_ge(xn_done.s, xn_done.at(l, 4 * (which - 1) + tt + 1))
                    for h in range(2):
                        out = free_bank(pe, l, ("x", which, tt, h))
                        for k in range(4):
                            src = xn[which - 1][tt].rearrange("p (n k) -> p k n", k=KD)[:, 4 * h + k, :]
                            last = nc.tensor.transpose(out[:, k * P:(k + 1) * P], src, ident[:, :])
                        last.then_inc(tile_ready.s, 1)

                def hT_ready(which):
                    pe.wait_ge(act_took.s, act_took.at(l, taken[("x", which, TT - 1, 0)][1]))
                    pe.wait_ge(dve_took.s, dve_took.at(l, taken[("x", which, TT - 1, 1)][1]))

                def piece(m):
                    pe.wait_ge(win_in[m % 2].s, win_in[m % 2].at(l, 16 * (m // 2 + 1)))
                    return win_w[m % 2]

                def feature_tile(key, w, col):
                    out = free_bank(pe, l, key)
                    for k in range(KD):
                        last = mm(out[:, :], w[:, k, col:col + P], hT[:, k, :], k == 0, k == KD - 1)
                    last.then_inc(tile_ready.s, 1)

                def token_tile(key, w, tokens):
                    out = free_bank(pe, l, key)
                    for k in range(KD):
                        last = mm(out[:, 0:256], tokens(k), w[:, k, :], k == 0, k == KD - 1)
                    last.then_inc(tile_ready.s, 1)

                def ada_tile(n):
                    out = free_bank(pe, l, ("ada", n))
                    pe.wait_ge(ada_used.s, ada_used.at(l, 4 * (n + 1)))
                    if n in (0, 3):
                        mm(out[:, :], ones[:, :], acc[:, 0:512], True, True).then_inc(tile_ready.s, 1)
                        out = free_bank(pe, l, ("ada", n, 1))
                        mm(out[:, :], ones[:, :], acc[:, 512:1024], True, True).then_inc(tile_ready.s, 1)
                    else:
                        sum_chunk(out, n).then_inc(tile_ready.s, 1)

                for tt in range(TT):
                    norm_transposes(1, tt)
                hT_ready(1)
                w = piece(0)
                for d in range(2):
                    feature_tile(("q", d), w, d * P)
                ada_tile(0)
                w = piece(1)
                for d in range(2):
                    feature_tile(("k", d), w, d * P)
                ada_tile(1)
                out = free_bank(pe, l, ("lf",))
                pe.wait_ge(lf_in.s, lf_in.at(l, 16))
                for k in range(KD):
                    last = mm(out[0:32, :], wlf[:, k, :], hT[:, k, :], k == 0, k == KD - 1)
                last.then_inc(tile_ready.s, 1)
                w = piece(2)
                for c in range(3):
                    token_tile(("v", 0, c), w, lambda k: hT[:, k, c * P:(c + 1) * P])
                ada_tile(2)
                for c in range(3, 4):
                    token_tile(("v", 0, c), w, lambda k: hT[:, k, c * P:(c + 1) * P])
                pe.wait_ge(act_took.s, act_took.at(l, taken[("lf",)][1]))
                pe.wait_ge(gatew_in.s, gatew_in.at(l, 48))
                for c in range(TT):
                    out = free_bank(pe, l, ("z", c))
                    mm(out[:, :], lfx[:, c * P:(c + 1) * P], gatew[:, :], True, True).then_inc(tile_ready.s, 1)
                w = piece(3)
                for c in range(2):
                    token_tile(("v", 1, c), w, lambda k: hT[:, k, c * P:(c + 1) * P])
                pe.wait_ge(la_done.s, la_done.at(l, 4))
                for r in range(2):
                    for d in range(2):
                        out = free_bank(pe, l, ("b", r, d))
                        for c in range(TT):
                            f = r * 256 + d * P
                            last = mm(out[:, c * P:(c + 1) * P], la[:, c, f:f + P], (upto, since)[r][:, :], True, True)
                        last.then_inc(tile_ready.s, 1)
                for c in range(2, 4):
                    token_tile(("v", 1, c), w, lambda k: hT[:, k, c * P:(c + 1) * P])
                for c in range(TT):
                    out = free_bank(pe, l, ("kx", c))
                    mm(out[:, 0:256], after[:, :], la[:, c, 0:256], True, True)
                    mm(out[:, 256:512], before[:, :], la[:, c, 256:512], True, True).then_inc(tile_ready.s, 1)
                    out = free_bank(pe, l, ("kt", c))
                    for d in range(2):
                        last = nc.tensor.transpose(out[:, d * P:(d + 1) * P],
                                                   kT[:, d * T + c * P:d * T + (c + 1) * P], ident[:, :])
                    last.then_inc(tile_ready.s, 1)
                ada_tile(3)
                for h in range(2):
                    feature_tile(("g", h), piece(4), h * P)
                for r, c in [(0, 0), (0, 1), (0, 2), (1, 3), (1, 2), (1, 1)]:
                    out = free_bank(pe, l, ("U", r, c))
                    pe.wait_ge(khat_done.s, khat_done.at(l, c + 1))
                    for h in range(4):
                        half = 64 * (h % 2)
                        last = mm(out[half:half + 64, (h // 2) * P:(h // 2 + 1) * P],
                                  khat[:, c, r * 256 + h * 64:r * 256 + h * 64 + 64],
                                  v_tm[:, c, h * P:(h + 1) * P], True, True)
                    last.then_inc(tile_ready.s, 1)

                def mean_tile(key, n, weights):
                    out = free_bank(pe, l, key)
                    pe.wait_ge(sq_done.s, sq_done.at(l, n + 1))
                    mm(out[:, :], weights[:, :], sq[:, n % 2, :], True, True).then_inc(tile_ready.s, 1)

                def level_tiles(lev, kv, qv, mean_of=None):
                    for c in range(TT):
                        out = free_bank(pe, l, ("P", lev, c))
                        for d in range(2):
                            at = d * T + c * P
                            last = mm(out[:, d * 256:(d + 1) * 256], kv[:, at:at + P], qv[:, :, at:at + P], True, True)
                        last.then_inc(tile_ready.s, 1)
                        if c == 0 and mean_of is not None:
                            mean_tile(("kms", mean_of), mean_of, mean64)

                pe.wait_ge(zeroed_q.s, zeroed_q.at(l, 1))
                level_tiles(7, kT, qz)
                for h in range(2, 4):
                    feature_tile(("g", h), piece(5), (h % 2) * P)
                done = index[("P", 7, TT - 1)] + 1
                for n, lev in enumerate(LEVELS):
                    pe.wait_ge(lev_q.s, lev_q.at(l, n + 1))
                    pe.wait_ge(lev_k.s, lev_k.at(l, n + 1))
                    level_tiles(lev, k_lev[n % 2], q_lev[n % 2].rearrange("p (r n) -> p r n", r=2),
                                n - 1 if 1 <= n <= 4 else None)
                    done = index[("P", lev, TT - 1)] + 1
                    while done < len(plan) and plan[done][0][0] in FILLERS:
                        key = plan[done][0]
                        if key[0] == "kn":
                            feature_tile(key, piece(6 + key[1] // 2), (key[1] % 2) * P)
                        elif key[0] == "ada":
                            ada_tile(key[1])
                        elif key[0] == "vf":
                            feature_tile(key, piece(8 + key[1] // 2), (key[1] % 2) * P)
                        else:
                            out = free_bank(pe, l, key)
                            pe.wait_ge(act_took.s, act_took.at(l, taken[("vf", key[1])][1]))
                            for n7 in range(4 * key[2], min(4 * key[2] + 4, 7)):
                                last = nc.tensor.transpose(out[:, (n7 % 4) * P:(n7 % 4 + 1) * P],
                                                           ekx[:, key[1] % 2, n7 * 64:n7 * 64 + P], ident[:, :])
                            last.then_inc(tile_ready.s, 1)
                        done += 1
                for i, ms in ((0, None), (1, 0), (2, 1), (3, 2), (None, 3)):
                    if i is not None:
                        feature_tile(("qn", i), piece(10 + i // 2), (i % 2) * P)
                    if ms is not None:
                        mean_tile(("qms", ms), 4 + ms, mean64)
                ada_tile(5)

                pe.wait_ge(dve_took.s, dve_took.at(l, taken[("P", 0, TT - 1)][1]))
                pe.wait_ge(st_done.s, st_done.at(l, 1))
                for i, ms in ((0, None), (1, 0), (2, 1), (3, 2), (None, 3)):
                    if i is not None:
                        out = free_bank(pe, l, ("o", i))
                        half, d = 64 * (i % 2), i // 2
                        for c in range(TT):
                            o = out[:, c * P:(c + 1) * P]
                            at = d * T + c * P
                            last = mm(o, v_tm[:, c, i * P:(i + 1) * P], amat[:, c, i, :], True, False)
                            for r in range(2):
                                if (c > 0, c < TT - 1)[r]:
                                    last = mm(o, st[half:half + 64, r, c - 1 + r, d * P:(d + 1) * P],
                                              qd[half:half + 64, r, at:at + P], False, r == 1 or c == TT - 1)
                        last.then_inc(tile_ready.s, 1)
                    if ms is not None:
                        mean_tile(("oms", ms), 8 + ms, ones)

                for h in range(11):
                    if h < 8:
                        d, r = h // 2, h % 2
                        if r == 0:
                            pe.wait_ge(dve_took.s, dve_took.at(l, taken[("qn", d)][1]))
                        for i in range(2):
                            out = free_bank(pe, l, ("S", h, i))
                            for cb in (2 * i, 2 * i + 1):
                                q0 = T - P * (cb + 1)
                                last = mm(out[:, (cb % 2) * 256:(cb % 2 + 1) * 256], qnz[:, d, r, q0:q0 + P],
                                          kn[:, d, KEY_AT[cb] * 64:KEY_AT[cb] * 64 + 256], True, True)
                            last.then_inc(tile_ready.s, 1)
                    if 2 <= h < 10:
                        g = h - 2
                        pe.wait_ge(prob_done.s, prob_done.at(l, g + 1))
                        for i in range(2):
                            out = free_bank(pe, l, ("PT", g, i))
                            for cb in (2 * i, 2 * i + 1):
                                for half in range(2):
                                    last = nc.tensor.transpose(
                                        out[:, (cb % 2) * 256 + half * P:(cb % 2) * 256 + (half + 1) * P],
                                        P_sb[:, g % 3, cb, half * P:(half + 1) * P], ident[:, :])
                            last.then_inc(tile_ready.s, 1)
                    if h >= 3:
                        g = h - 3
                        d, r = g // 2, g % 2
                        pe.wait_ge(act_took.s, act_took.at(l, taken[("PT", g, 1)][1]))
                        if r == 0 and d >= 2:
                            pe.wait_ge(cat_n.s, cat_n.at(l, d - 1))
                        for cb in range(4):
                            q0 = T - P * (cb + 1)
                            for half in range(2):
                                last = mm(bank[6 + d % 2][64 * r:64 * r + 64, q0:q0 + P],
                                          vn[:, KEY_AT[cb] + 2 * half, g * 64:(g + 1) * 64],
                                          PT_sb[:, g % 2, cb, half * P:(half + 1) * P], half == 0, half == 1)
                        if r == 1:
                            last.then_inc(on_done.s, 1)

                pe.wait_ge(cat_g.s, cat_g.at(l, 1))
                pe.wait_ge(cat_n.s, cat_n.at(l, 4))
                for m in range(4):
                    pe.wait_ge(wo_in[m % 2].s, wo_in[m % 2].at(l, 16 * (m // 2 + 1)))
                    for kind, tt in LAST_Y if m == 3 else [("y", t) for t in range(TT)]:
                        if kind == "y":
                            token_tile(("y", m, tt), ada_w[m % 2], lambda k: cat[:, k, tt * P:(tt + 1) * P])
                        else:
                            norm_transposes(2, tt)
                hT_ready(2)
                out = free_bank(pe, l, ("log_T",))
                for k in range(KD):
                    for tt in range(TT):
                        last = mm(out[tt * NE:(tt + 1) * NE, 0:P], rw_sb[:, k, :], hT[:, k, tt * P:(tt + 1) * P],
                                  k == 0, k == KD - 1)
                last.then_inc(tile_ready.s, 1)
                out = free_bank(pe, l, ("logits",))
                pe.wait_ge(act_took.s, act_took.at(l, taken[("log_T",)][1]))
                nc.tensor.transpose(out[:, 0:P], log_T, ident[:, :]).then_inc(tile_ready.s, 1)

                out = free_bank(pe, l, ("rank",))
                pe.wait_ge(mask_done.s, mask_done.at(l, 1))
                mask = R["mask"]
                for tt in range(TT):
                    o = out[:, tt * NE:(tt + 1) * NE]
                    mm(o, before[:, :], mask[:, tt * NE:(tt + 1) * NE], True, tt == 0)
                    for t2 in range(tt):
                        mm(o, ones[:, :], mask[:, t2 * NE:(t2 + 1) * NE], False, t2 == tt - 1)
                for tt in range(TT):
                    mm(out[:, 128:128 + NE], ones[:, :], mask[:, tt * NE:(tt + 1) * NE], tt == 0, tt == TT - 1)
                for tt in range(TT):
                    last = mm(out[0:NE, 160:161], mask[:, tt * NE:(tt + 1) * NE], ones[:, 0:1], tt == 0, tt == TT - 1)
                last.then_inc(tile_ready.s, 1)
                out = free_bank(pe, l, ("over",))
                pe.wait_ge(over_in.s, over_in.at(l, 1))
                nov = R["t3"][0:NE, :]
                mm(out[:, 0:NE], nov, before[0:NE, 0:NE], True, True)
                mm(out[:, NE:NE + 1], nov, ones[0:NE, 0:1], True, True).then_inc(tile_ready.s, 1)
                out = free_bank(pe, l, ("slot",))
                pe.wait_ge(slot1h.s, slot1h.at(l, 1))
                for j in range(8):
                    last = mm(out[0:SLOTS, 0:NBLK], oslot[:, j, :], oblk[:, j, :], j == 0, j == 7)
                last.then_inc(tile_ready.s, 1)

                pe.wait_ge(routed.s, routed.at(l, 1))
                pairs0, more = reg_counts(pe)

                def turn(u, G, pair):
                    pe.wait_ge(gathered[u].s, pair * 16 + 16)
                    pe.wait_ge(blk["hg_done"].s, blocks(G, -1))
                    pass_on(pe)
                    for k in range(KD):
                        src = xg[:, u, :].rearrange("p (n k) -> p k n", k=KD)[:, k, :]
                        last = nc.tensor.transpose(bank[u][:, k * SLOTS:(k + 1) * SLOTS], src,
                                                   ident[0:SLOTS, 0:SLOTS])
                    last.then_inc(blk["xg_T"].s, 1)

                def up(u, G, pair):
                    pe.wait_ge(blk["hg_done"].s, blocks(G, 1))
                    pe.wait_ge(blk["g_done"].s, blocks(G, -1))
                    for mat in range(2):
                        pe.wait_ge(w_blk[u][mat].s, pair * 16 + 16)
                        for k in range(KD):
                            for half in range(2):
                                last = mm(bank[2 + u][64 * half:64 * half + 64, mat * 256:(mat + 1) * 256],
                                          hgT[:, u, k, :], w13[u][mat][:, k, half * 256:(half + 1) * 256],
                                          k == 0, k == KD - 1)
                    last.then_inc(blk["up_ready"].s, 1)

                def turn_g(u, G):
                    pe.wait_ge(blk["g_done"].s, blocks(G, 1))
                    pe.wait_ge(blk["gTs_done"].s, blocks(G, -1))
                    for q in range(2):
                        src = sil[:, u, 256:512].rearrange("p (n q) -> p q n", q=2)[:, q, :]
                        last = nc.tensor.transpose(bank[4 + u][:, q * P:(q + 1) * P], src, ident[:, :])
                    last.then_inc(blk["gT_ready"].s, 1)

                def down(u, G, pair):
                    pe.wait_ge(blk["gTs_done"].s, blocks(G, 1))
                    pe.wait_ge(blk["y_evac"].s, blocks(G, -1))
                    pe.wait_ge(w_blk[u][2].s, pair * 16 + 16)
                    for n in range(4):
                        hh, q = n // 2, n % 2
                        for nh in range(2):
                            last = mm(bank[6 + u][64 * nh:64 * nh + 64, :],
                                      gTs[:, u, q * P + hh * 64:q * P + hh * 64 + 64],
                                      w2s[u][:, hh, q, nh * 512:(nh + 1) * 512], n == 0, n == 3)
                    last.then_inc(blk["y_ready"].s, 1)

                G0 = pairs0 * 2
                turn(0, G0, pairs0)
                up(0, G0, pairs0)
                turn(1, G0 + 1, pairs0)
                with pe.Fori(0, more) as i:
                    G, pair = G0 + i * 2, pairs0 + i
                    up(1, G + 1, pair)
                    turn_g(0, G)
                    turn(0, G + 2, pair + 1)
                    down(0, G, pair)
                    up(0, G + 2, pair + 1)
                    turn_g(1, G + 1)
                    turn(1, G + 3, pair + 1)
                    down(1, G + 1, pair)
                G, pair = G0 + more * 2, pairs0 + more
                up(1, G + 1, pair)
                turn_g(0, G)
                down(0, G, pair)
                turn_g(1, G + 1)
                down(1, G + 1, pair)

        @block.scalar
        def _(act):
            steps = [0]

            def link(l, ins):
                steps[0] += 1
                ins.then_inc(act_step.s, 1)
                act.wait_ge(act_step.s, act_step.at(l, steps[0]))

            F = nc.scalar.activation
            nc.scalar.preload_act_table_set("natural_log_exp_and_others")
            act.wait_ge(consts_p.s, 1)
            for n in ("gTs_done", "y_evac", "up_exp"):
                act.sem_inc(blk[n].s, 2)
            for u in range(2):
                act.sem_inc(y_stored[u].s, 32)
            act.wait_ge(c_in.s, 16)
            F(ctmp[:, :], c_sb[:, :], ACT.Exp, scale=-1.0).then_inc(c_act.s, 1)
            for l0 in range(L):
                def vec(v, n):
                    return v.rearrange("(p k) -> p k", k=n)
                act.dma_start(par_all[:, l0, 0:8], vec(A["ffn_norm"][l0], KD)).then_inc(par_in.s, 16)
                act.dma_start(par_all[:, l0, 8:16], vec(A["attn_norm"][1 - l0], KD)).then_inc(par_in.s, 16)
                act.dma_start(par_all[:, l0, 16:17], vec(A["gla_out_norm"][l0], 1)).then_inc(par_in.s, 16)
                for half in range(2):
                    rows = slice(64 * half, 64 * half + 64)
                    act.dma_start(par_all[rows, l0, 17:18], vec(A["na_q_norm"][l0], 1)).then_inc(par_in.s, 16)
                    act.dma_start(par_all[rows, l0, 18:19], vec(A["na_k_norm"][l0], 1)).then_inc(par_in.s, 16)
            act.dma_start(anorm0[:, :], A["attn_norm"][0].rearrange("(p k) -> p k", k=KD)).then_inc(par_in.s, 16)
            act.dma_start(rw_sb[:, :, :], A["router_w"].rearrange("(p k) n -> p k n", k=KD)).then_inc(par_in.s, 16)
            act.dma_start(rb_sb[:, :], bass.AP(tensor=A["router_b"].tensor, offset=0, ap=[[0, P], [1, NE]])
                          ).then_inc(par_in.s, 16)
            act.dma_start(rpb_pad[:, RPB_PAD:RPB_PAD + 8 * RPB_W], A["na_rpb"].rearrange("l h a b -> l (h a b)")
                          ).then_inc(rpb_copied.s, 16)
            act.wait_ge(consts_v.s, 2)
            act.dma_start(rpb_pad[:, 0:RPB_PAD], pad0[:, :]).then_inc(rpb_copied.s, 16)
            act.dma_start(rpb_pad[:, RPB_PAD + 8 * RPB_W:], pad0[:, :]).then_inc(rpb_copied.s, 16)
            act.wait_ge(rpb_copied.s, 48)
            act.wait_ge(par_in.s, 16 * 17)

            with act.Fori(0, L) as l:
                steps[0] = 0

                def gates_load():
                    act.dma_start(gatew[0:16, 0:256], A["gla_gate_w"].rearrange("l r a n -> (l r) a n")[l * 2]
                                  ).then_inc(gatew_in.s, 16)
                    act.dma_start(gatew[16:32, 256:512], A["gla_gate_w"].rearrange("l r a n -> (l r) a n")[l * 2 + 1]
                                  ).then_inc(gatew_in.s, 16)
                    act.dma_start(gatew[32:33, :], A["gla_gate_b"].rearrange("l (a r) n -> l a (r n)", a=1)[l]
                                  ).then_inc(gatew_in.s, 16)

                def tile(key):
                    return ready(act, l, key)

                def shift(which, tt):
                    a_, b_ = (A1, B1) if which == 1 else (A2, B2)
                    b = tile(("x", which, tt, 0))
                    for k in range(4):
                        last = F(hT[:, k, tt * P:(tt + 1) * P], b[:, k * P:(k + 1) * P], ACT.Identity,
                                 bias=b_[:, k:k + 1], scale=a_[:, k:k + 1])
                    last.then_inc(act_took.s, 1)

                def store_and_shift(tt):
                    act.wait_ge(xn_done.s, xn_done.at(l, 4 + tt + 1))
                    act.dma_start(xn_dram[tt * P:(tt + 1) * P, :], xn[1][tt]).then_inc(xn_stored[tt % 2].s, 16)
                    shift(2, tt)

                def norm(which):
                    c0 = 4 * (which - 1)
                    src = x_new if which == 1 else x_mid
                    for tt in range(TT):
                        act.wait_ge(src.s, l * TT + tt + 1)
                        link(l, F(flat[:, 8192:9216] if which == 1 else pool_a[:, 0:1024], x_sb[:, tt, :], ACT.Square,
                                  accum_out=ssq[:, c0 + tt:c0 + tt + 1]))
                        r1 = rstd[:, c0 + tt:c0 + tt + 1]
                        link(l, F(r1, ssq[:, c0 + tt:c0 + tt + 1], ACT.Ln, bias=eps_c[:, 0:1], scale=1.0 / D))
                        F(r1, r1, ACT.Exp, scale=-0.5).then_inc(rstd_done.s, 1)
                        if which == 2:
                            if tt >= 1:
                                store_and_shift(tt - 1)
                    if which == 2:
                        store_and_shift(TT - 1)

                norm(1)
                gates_load()
                act.wait_ge(mod_ready.s, 1)
                for tt in range(TT):
                    shift(1, tt)
                for d in range(2):
                    b = tile(("q", d))
                    for half in range(2):
                        rows = slice(64 * half, 64 * half + 64)
                        last = F(qz[rows, half, d * T:(d + 1) * T], b[rows, :], ACT.Copy, scale=0.125)
                    last.then_inc(act_took.s, 1)
                for d in range(2):
                    b = tile(("k", d))
                    F(kT[:, d * T:(d + 1) * T], b[:, :], ACT.Copy).then_inc(act_took.s, 1)
                b = tile(("lf",))
                act.wait_ge(dve_took.s, dve_took.at(l, taken[("ada", 0)][1]))
                F(lfx[0:32, :], b[0:32, :], ACT.Copy).then_inc(act_took.s, 1)
                def take_v(m, c0, c1):
                    for c in range(c0, c1):
                        b = tile(("v", m, c))
                        F(v_tm[:, c, m * 256:(m + 1) * 256], b[:, 0:256], ACT.Copy).then_inc(act_took.s, 1)

                def take_gate(h):
                    b = tile(("g", h))
                    F(sg[:, h, :], b[:, :], ACT.Copy).then_inc(act_took.s, 1)

                act.wait_ge(y_zeroed.s, 16)
                take_v(0, 0, TT)
                for c in range(TT):
                    b = tile(("z", c))
                    t1 = rt[:, c % 2, :]
                    if c >= 2:
                        act.wait_ge(la_done.s, la_done.at(l, c - 1))
                    link(l, F(t1, b[:, :], ACT.Abs))
                    link(l, F(t1, t1, ACT.Exp, scale=-1.0))
                    F(t1, t1, ACT.Ln, bias=one_c[:, 0:1]).then_inc(ln_done.s, 1)
                take_v(1, 0, 2)
                for r in range(2):
                    for d in range(2):
                        b = tile(("b", r, d))
                        F(bT[:, r, d * T:(d + 1) * T], b[:, :], ACT.Copy).then_inc(act_took.s, 1)
                act.wait_ge(act_took.s, act_took.at(l, taken[("b", 1, 1)][1]))
                take_v(1, 2, TT)
                for c in range(TT):
                    b = tile(("kx", c))
                    if c >= 2:
                        act.wait_ge(khat_done.s, khat_done.at(l, c - 1))
                    F(ekx[:, c % 2, :], b[:, :], ACT.Exp, scale=TAU_INV).then_inc(act_took.s, 1)
                for r in range(2):
                    F(qd[:, r, :], bT[:, r, :], ACT.Exp, scale=TAU_INV)
                    ends = bT[:, r, :].rearrange("p (n i) -> p n i", i=P)[:, :, P - 1 if r == 0 else 0]
                    last = F(dec[:, r, :], ends, ACT.Exp, scale=TAU_INV)
                last.then_inc(dec_done.s, 1)
                def level_exp(n):
                    act.wait_ge(diff_q.s, diff_q.at(l, n + 1))
                    F(eq, eq, ACT.Exp, scale=TAU_INV).then_inc(exp_q.s, 1)
                    act.wait_ge(diff_k.s, diff_k.at(l, n + 1))
                    F(k_lev[n % 2], k_lev[n % 2], ACT.Exp, scale=TAU_INV).then_inc(exp_k.s, 1)

                take_gate(0), take_gate(1)
                level_exp(0)
                for c in range(TT):
                    b = tile(("P", 7, c))
                    F(amat[:, c, :, :].rearrange("p h i -> p (h i)"), b[:, :], ACT.Copy).then_inc(act_took.s, 1)
                take_gate(2), take_gate(3)

                def squares(key, n):
                    b = tile(key)
                    if n >= 2:
                        ms = {"kn": "kms", "qn": "qms", "o": "oms"}
                        prev = [(a, i) for a in ("kn", "qn", "o") for i in range(4)][n - 2]
                        act.wait_ge(tile_ready.s, tile_ready.at(l, index[(ms[prev[0]], prev[1])] + 1))
                    F(sq[:, n % 2, :], b[:, :], ACT.Square).then_inc(sq_done.s, 1)

                def scales(key, n):
                    b = tile(key)
                    if n >= 2:
                        prev = [(a, i) for a in ("kn", "qn", "o") for i in range(4)][n - 2]
                        act.wait_ge(dve_took.s, dve_took.at(l, taken[prev][1]))
                    F(rt[:, n % 2, :], b[:, :], ACT.Ln, bias=eps_c[:, 0:1],
                      scale=1.0 if n < 8 else 1.0 / 128).then_inc(act_took.s, 1)
                    act.wait_ge(act_took.s, act_took.at(l, taken[key][1]))
                    F(rt[:, n % 2, :], rt[:, n % 2, :], ACT.Exp, scale=-0.5).then_inc(rt_done.s, 1)

                level_exp(1)
                for n, lev in enumerate(LEVELS):
                    if n < 5:
                        level_exp(n + 2)
                    if n == 6:
                        act.wait_ge(tile_ready.s, tile_ready.at(l, index[("P", LEVELS[5], TT - 1)] + 1))
                        F(sg_exp, sg[:, :, :], ACT.Exp, scale=-1.0).then_inc(gexp_done.s, 1)
                    at = index[("P", lev, TT - 1)] + 1
                    while plan[at][0][0] in FILLERS:
                        key = plan[at][0]
                        at += 1
                        if key[0] == "kn":
                            squares(key, key[1])
                        elif key[0] != "ada":
                            b = tile(key)
                            f = key[1]
                            if key[0] == "vf":
                                if f >= 2:
                                    act.wait_ge(tile_ready.s, tile_ready.at(l, index[("vt", f - 2, 1)] + 1))
                                F(ekx[:, f % 2, :].rearrange("p (c r) -> p r c", r=ROWS),
                                  b[:, :].rearrange("p (r c) -> p r c", c=COLS), ACT.Copy).then_inc(act_took.s, 1)
                            else:
                                n0, n1 = 4 * key[2], min(4 * key[2] + 4, 7)
                                F(vn[:, n0:n1, f * P:(f + 1) * P],
                                  b[:, 0:(n1 - n0) * P].rearrange("p (n f) -> p n f", f=P), ACT.Copy
                                  ).then_inc(act_took.s, 1)
                    if n < 4:
                        scales(("kms", n), n)
                act.wait_ge(st_done.s, st_done.at(l, 1))
                act.wait_ge(tile_ready.s, tile_ready.at(l, index[("vt", 3, 1)] + 1))
                for h in range(8):
                    src = bass.AP(tensor=rpb_pad.tensor, offset=rpb_pad[l][h * RPB_W:h * RPB_W + 1].offset,
                                  ap=[[1, 16], [31, 8], [1, 265]])
                    act.dma_start(gtab[:, h, :], src).then_inc(gtab_in.s, 16)

                for pre, n0 in (("qn", 4), ("o", 8)):
                    ms = pre[0] + "ms"
                    squares((pre, 0), n0), squares((pre, 1), n0 + 1)
                    for i in range(4):
                        scales((ms, i), n0 + i)
                        if i < 2:
                            squares((pre, i + 2), n0 + i + 2)
                for h in range(11):
                    if h < 8:
                        act.wait_ge(smax_done.s, smax_done.at(l, h + 1))
                        for cb in range(4):
                            last = F(P_sb[:, h % 3, cb, :], P_sb[:, h % 3, cb, :], ACT.Exp,
                                     bias=nmx[:, h % 2, cb:cb + 1], accum_out=sm[:, h % 2, cb:cb + 1])
                        last.then_inc(sexp_done.s, 1)
                    if 2 <= h < 10:
                        g = h - 2
                        for i in range(2):
                            b = tile(("PT", g, i))
                            F(PT_sb[:, g % 2, 2 * i:2 * i + 2, :].rearrange("p c n -> p (c n)"), b[:, :], ACT.Copy
                              ).then_inc(act_took.s, 1)
                    if h >= 4 and h % 2 == 0:
                        d = (h - 4) // 2
                        act.wait_ge(on_done.s, on_done.at(l, d + 1))
                        src = ap_of(bank[6 + d % 2][:, :], T - 1, [[-1, ROWS], [-ROWS, COLS]])
                        F(cat[:, 4 + d, :].rearrange("p (r c) -> p r c", c=COLS), src, ACT.Copy).then_inc(cat_n.s, 1)

                norm(2)
                b = tile(("log_T",))
                F(log_T, b[:, 0:P], ACT.Copy).then_inc(act_took.s, 1)
                b = tile(("logits",))
                F(R["score"], b[:, 0:128], ACT.Exp, scale=-1.0).then_inc(route_exp.s, 1)

                act.wait_ge(routed.s, routed.at(l, 1))
                pairs0, more = reg_counts(act)
                G0 = pairs0 * 2

                def up_exp(u, G):
                    act.wait_ge(blk["up_ready"].s, blocks(G, 1))
                    act.wait_ge(blk["gT_ready"].s, blocks(G, -1))
                    F(sil[:, u, 0:256], bank[2 + u][:, 0:256], ACT.Exp, scale=-1.0).then_inc(blk["up_exp"].s, 1)

                def take(u, G, row):
                    act.wait_ge(blk["gT_ready"].s, blocks(G, 1))
                    F(gTs[:, u, :], bank[4 + u][:, 0:256], ACT.Copy).then_inc(blk["gTs_done"].s, 1)
                    act.wait_ge(blk["y_evac"].s, blocks(G, 1))
                    for nh in range(2):
                        act.dma_start(y_blk[row][nh], y_sb[64 * nh:64 * nh + 64, u, :]).then_inc(y_stored[u].s, 16)

                up_exp(0, G0)
                with act.Fori(0, more) as i:
                    G, pair = G0 + i * 2, pairs0 + i
                    up_exp(1, G + 1)
                    take(0, G, i * 2)
                    up_exp(0, G + 2)
                    take(1, G + 1, i * 2 + 1)
                G, pair = G0 + more * 2, pairs0 + more
                up_exp(1, G + 1)
                take(0, G, more * 2)
                take(1, G + 1, more * 2 + 1)
            assert steps[0] == ACT_STEPS, steps

        @block.vector
        def _(dve):
            V = nc.vector
            steps = [0]

            def link(l, ins):
                steps[0] += 1
                ins.then_inc(dve_step.s, 1)
                dve.wait_ge(dve_step.s, dve_step.at(l, steps[0]))

            n0 = [0]

            def link0(ins):
                n0[0] += 1
                ins.then_inc(cstep.s, 1)
                dve.wait_ge(cstep.s, n0[0])
            link0(V.memset(brow[:, :, :].rearrange("p u n -> p (u n)"), 0.0))
            V.memset(pad0[:, :], 0.0).then_inc(consts_v.s, 1)
            V.memset(ones[:, :], 1.0)
            link0(V.memset(mean64[:, :], 0.0))
            V.memset(mean64[0:64, 0:64], 1.0 / 64)
            V.memset(mean64[64:128, 64:128], 1.0 / 64)
            V.memset(eps_c[:, :], EPS)
            V.memset(one_c[:, :], 1.0)
            V.memset(gatew[:, :], 0.0)
            V.memset(pairs[:, :], 0)
            V.memset(pairs_f[:, :], 0.0).then_inc(consts_v.s, 1)
            dve.wait_ge(consts_p.s, 1)
            link0(V.tensor_tensor(xor[:, :], io_p[:, :], io_f[:, :], ALU.bitwise_xor))
            for s_ in range(7):
                link0(V.tensor_scalar(xsh[:, :], xor[:, :], s_, None, ALU.arith_shift_right))
                link0(V.tensor_copy(xfl[:, :], xsh[:, :]))
                link0(V.tensor_scalar(lvl[:, s_, :], xfl[:, :], 1.0, None, ALU.is_equal))
            link0(V.tensor_scalar(xsh[:, 0:1], io_p[:, 0:1], 3, None, ALU.arith_shift_right))
            link0(V.tensor_copy(lo[:, 3:4], xsh[:, 0:1]))
            link0(V.tensor_scalar(lo[:, 1:2], lo[:, 3:4], -1.0, 15.0, ALU.mult, ALU.add))
            link0(V.tensor_scalar(lo[:, 0:1], lo[:, 1:2], -8.0, 0.0, ALU.add, ALU.max))
            link0(V.tensor_scalar(lo[:, 2:3], lo[:, 1:2], 8.0, 16.0, ALU.add, ALU.min))
            for m in range(3):
                link0(V.tensor_scalar(xfl[:, 0:32], iota_s[:, 0:32], lo[:, m:m + 1], None, ALU.subtract))
                link0(V.tensor_scalar(xfl[:, 32:64], xfl[:, 0:32], 0.0, None, ALU.is_ge))
                link0(V.tensor_scalar(xfl[:, 64:96], xfl[:, 0:32], 15.5, None, ALU.is_lt))
                link0(V.tensor_tensor(xfl[:, 96:128], xfl[:, 32:64], xfl[:, 64:96], ALU.mult))
                link0(V.tensor_scalar(wneg[:, m, :], xfl[:, 96:128], -1.0, -NEG, ALU.add, ALU.mult))
            dve.wait_ge(c_act.s, 1)
            link0(V.tensor_scalar(ctmp[:, :], ctmp[:, :], 1.0, None, ALU.add))
            link0(V.reciprocal(ctmp[:, :], ctmp[:, :]))
            link0(V.tensor_tensor(ctmp[:, :], ctmp[:, :], c_sb[:, :], ALU.mult))
            for n in ("hg_done", "g_done"):
                dve.sem_inc(blk[n].s, 2)

            def ada_part(slot, quarter, k):
                out = acc[:, quarter * 256:(quarter + 1) * 256]
                return V.scalar_tensor_tensor(out=out, in0=ada_w[slot][:, k, :], scalar=ctmp[:, k:k + 1],
                                              in1=bias_row[slot] if k == 0 else out, op0=ALU.mult, op1=ALU.add)

            def ada_pieces(pieces, step):
                for k in range(KD):
                    for i, (slot, quarter) in enumerate(pieces):
                        ins = ada_part(slot, quarter, k)
                        if k == KD - 1:
                            ins.then_inc(ada_used.s, 1)
                        else:
                            step(ins, 0 if k == KD - 2 and i == len(pieces) - 1 else len(pieces) - 1)

            def step0(ins, back):
                n0[0] += 1
                ins.then_inc(cstep.s, 1)
                dve.wait_ge(cstep.s, n0[0] - back)

            for m in range(0, 8, 2):
                if m == 4:
                    dve.wait_ge(mod0.s, 1)
                for i in range(2):
                    dve.wait_ge(ada_in[(m + i) % 4].s, 32 * (m // 4 + 1))
                ada_pieces([((m + i) % 4, (m + i) % 4) for i in range(2)], step0)
            dve.wait_ge(mod0.s, 2)
            dve.wait_ge(par_in.s, 16 * 17)
            V.tensor_copy(B1[:, :], bank[7][:, 0:8])
            V.scalar_tensor_tensor(out=A1[:, :], in0=bank[7][:, 8:16], scalar=1.0, in1=anorm0[:, :],
                                   op0=ALU.add, op1=ALU.mult).then_inc(mod_ready.s, 1)
            dve.wait_ge(x_in.s, 16)
            dve.sem_inc(x_new.s, TT)

            with dve.Fori(0, L) as l:
                steps[0] = 0

                def step(ins):
                    link(l, ins)

                def tile(key):
                    return ready(dve, l, key)

                def scaled(which, tt):
                    c0 = 4 * (which - 1) + tt
                    dve.wait_ge(rstd_done.s, rstd_done.at(l, c0 + 1))
                    if which == 1 and tt >= 2:
                        dve.wait_ge(tile_ready.s, tile_ready.at(l, index[("x", which, tt - 2, 1)] + 1))
                    V.tensor_scalar(xn[which - 1][tt], x_sb[:, tt, :], rstd[:, c0:c0 + 1], None,
                                    ALU.mult).then_inc(xn_done.s, 1)

                def shift_tile(which, tt):
                    a_, b_ = (A1, B1) if which == 1 else (A2, B2)
                    b = tile(("x", which, tt, 1))
                    for k in range(4):
                        last = V.tensor_scalar(hT[:, 4 + k, tt * P:(tt + 1) * P], b[:, k * P:(k + 1) * P],
                                               a_[:, 4 + k:5 + k], b_[:, 4 + k:5 + k], ALU.mult, ALU.add)
                    last.then_inc(dve_took.s, 1)

                def ada_step(ins, back):
                    steps[0] += 1
                    ins.then_inc(dve_step.s, 1)
                    dve.wait_ge(dve_step.s, dve_step.at(l, steps[0] - back))

                def ada_sum(*ms):
                    for m in ms:
                        use = m // 4 if m < 16 else 4 + (m - 16) // 2
                        loaded = ada_in[m % 4 if m < 16 else m % 2]
                        dve.wait_ge(loaded.s, loaded.at(l, 32 * (use + 1)))
                    ada_pieces([(m % 4 if m < 16 else m % 2, m % 4) for m in ms], ada_step)

                def ada_chunk(n):
                    ada_sum(4 * n, 4 * n + 1)
                    ada_sum(4 * n + 2, 4 * n + 3)

                for tt in range(TT):
                    scaled(1, tt)
                    if tt >= 1:
                        shift_tile(1, tt - 1)
                shift_tile(1, TT - 1)
                step(V.tensor_copy(par[:, :], par_all[:, bass.ds(l, 1), :].rearrange("p a n -> p (a n)")))
                dve.wait_ge(tile_ready.s, tile_ready.at(l, index[("x", 1, TT - 1, 1)] + 1))
                V.memset(lfx[32:33, :], 1.0)
                ada_chunk(0)
                b = tile(("ada", 0))
                V.tensor_copy(g1_bc[:, 0:512], b[:, :]).then_inc(dve_took.s, 1)
                V.tensor_copy(g1_bc[:, 512:1024], ready(dve, l, ("ada", 0, 1))[:, :]).then_inc(dve_took.s, 1)
                ada_chunk(1)
                b = tile(("ada", 1))
                V.tensor_copy(B2[:, :], b[:, 0:8]).then_inc(dve_took.s, 1)
                ada_chunk(2)
                b = tile(("ada", 2))
                V.scalar_tensor_tensor(out=A2[:, :], in0=b[:, 0:8], scalar=1.0, in1=par[:, 0:8], op0=ALU.add,
                                       op1=ALU.mult).then_inc(dve_took.s, 1)
                ada_sum(12, 13)
                for c in range(TT):
                    b = tile(("z", c))
                    dve.wait_ge(ln_done.s, ln_done.at(l, c + 1))
                    V.scalar_tensor_tensor(out=la[:, c, :], in0=b[:, :], scalar=0.0, in1=rt[:, c % 2, :],
                                           op0=ALU.min, op1=ALU.subtract).then_inc(dve_took.s, 1)
                    dve.wait_ge(dve_took.s, dve_took.at(l, taken[("z", c)][1]))
                    dve.sem_inc(la_done.s, 1)
                ada_sum(14, 15)

                def level_diff(n):
                    hh = 1 << LEVELS[n]
                    e = eq.rearrange("p (n a h) -> p n a h", a=2, h=hh)
                    f, g = (bT[:, r, :].rearrange("p (n a h) -> p n a h", a=2, h=hh) for r in range(2))
                    V.tensor_tensor(e[:, :, 1, :], f[:, :, 1, :], rep(f[:, :, 0, hh - 1], hh), ALU.subtract)
                    V.tensor_tensor(e[:, :, 0, :], g[:, :, 0, :], rep(g[:, :, 1, 0], hh), ALU.subtract
                                    ).then_inc(diff_q.s, 1)

                dve.wait_ge(act_took.s, act_took.at(l, taken[("b", 1, 1)][1]))
                level_diff(0)
                for c in range(TT):
                    b = tile(("kt", c))
                    dve.wait_ge(act_took.s, act_took.at(l, taken[("kx", c)][1]))
                    V.tensor_tensor(khat[:, c, :].rearrange("p (r n) -> p r n", r=2),
                                    ekx[:, c % 2, :].rearrange("p (r n) -> p r n", r=2), again(b[:, 0:256], 2),
                                    ALU.mult).then_inc(dve_took.s, 1)
                    dve.wait_ge(dve_took.s, dve_took.at(l, taken[("kt", c)][1]))
                    dve.sem_inc(khat_done.s, 1)
                for i in range(2):
                    b = ready(dve, l, ("ada", 3, i) if i else ("ada", 3))
                    V.tensor_copy(g2_bc[:, i * 512:(i + 1) * 512], b[:, :]).then_inc(dve_took.s, 1)
                dve.wait_ge(dec_done.s, dec_done.at(l, 1))
                for r, c in [(0, 0), (0, 1), (0, 2), (1, 3), (1, 2), (1, 1)]:
                    b = tile(("U", r, c))
                    to = c if r == 0 else c - 1
                    if c in (0, 3):
                        V.tensor_copy(st[:, r, to, :], b[:, 0:256]).then_inc(dve_took.s, 1)
                    else:
                        prev = to - 1 if r == 0 else to + 1
                        for d in range(2):
                            last = V.scalar_tensor_tensor(out=st[:, r, to, d * P:(d + 1) * P],
                                                          in0=st[:, r, prev, d * P:(d + 1) * P],
                                                          scalar=dec[:, r, d * 4 + c:d * 4 + c + 1],
                                                          in1=b[:, d * P:(d + 1) * P], op0=ALU.mult, op1=ALU.add)
                        last.then_inc(dve_took.s, 1)
                    dve.wait_ge(dve_took.s, dve_took.at(l, taken[("U", r, c)][1]))
                for half in range(2):
                    rows = slice(64 * half, 64 * half + 64)
                    last = V.tensor_tensor(qd[rows, :, :], qd[rows, :, :], again(qz[rows, half, :], 2), ALU.mult)
                last.then_inc(st_done.s, 1)

                def level_q(n):
                    dve.wait_ge(exp_q.s, exp_q.at(l, n + 1))
                    if n >= 2:
                        dve.wait_ge(tile_ready.s, tile_ready.at(l, index[("P", LEVELS[n - 2], TT - 1)] + 1))
                    else:
                        dve.wait_ge((zeroed_q, zeroed_l)[n].s, (zeroed_q, zeroed_l)[n].at(l, 1))
                    for half in range(2):
                        rows = slice(64 * half, 64 * half + 64)
                        last = V.tensor_tensor(q_lev[n % 2][rows, half * 1024:(half + 1) * 1024], eq[rows, :],
                                               qz[rows, half, :], ALU.mult)
                    last.then_inc(lev_q.s, 1)
                    dve.wait_ge(lev_q.s, lev_q.at(l, n + 1))
                    if n < 6:
                        level_diff(n + 1)

                def key_tile(i):
                    b = tile(("kn", i))
                    dve.wait_ge(rt_done.s, rt_done.at(l, i + 1))
                    V.scalar_tensor_tensor(
                        out=kn[:, i, :].rearrange("p (c r) -> p r c", r=ROWS),
                        in0=b[:, :].rearrange("p (r c) -> p r c", c=COLS), scalar=par[:, 18:19],
                        in1=rt[:, i % 2, :].rearrange("p (r c) -> p r c", c=COLS), op0=ALU.mult, op1=ALU.mult
                    ).then_inc(dve_took.s, 1)

                level_q(0)
                for n, lev in enumerate(LEVELS):
                    if n < 6:
                        level_q(n + 1)
                    for c in range(TT):
                        b = tile(("P", lev, c))
                        if n == 0:
                            dve.wait_ge(act_took.s, act_took.at(l, taken[("P", 7, c)][1]))
                        pass_on(dve)
                        V.copy_predicated(out=amat[:, c, :, :], mask=again(lvl[:, lev, :], 4),
                                          data=b[:, :].rearrange("p (h i) -> p h i", h=4)).then_inc(dve_took.s, 1)
                        if c == 0 and 1 <= n <= 4:
                            key_tile(n - 1)
                    dve.wait_ge(dve_took.s, dve_took.at(l, taken[("P", lev, TT - 1)][1]))
                    at = index[("P", lev, TT - 1)] + 1
                    while plan[at][0][0] in FILLERS:
                        key = plan[at][0]
                        at += 1
                        if key[0] == "ada":
                            b = tile(key)
                            V.tensor_copy(B1[:, :], b[:, 0:8]).then_inc(dve_took.s, 1)
                    ada_sum(16 + n)
                ada_sum(23)

                def query_tile(i):
                    b = tile(("qn", i))
                    dve.wait_ge(rt_done.s, rt_done.at(l, 4 + i + 1))
                    for half in range(2):
                        rows = slice(64 * half, 64 * half + 64)
                        last = V.scalar_tensor_tensor(
                            out=ap_of(qnz[rows, i, half, :], T - 1, [[-1, ROWS], [-ROWS, COLS]]),
                            in0=b[rows, :].rearrange("p (r c) -> p r c", c=COLS), scalar=qscale[rows, 0:1],
                            in1=rt[rows, i % 2, :].rearrange("p (r c) -> p r c", c=COLS), op0=ALU.mult, op1=ALU.mult)
                    last.then_inc(dve_took.s, 1)

                step(V.tensor_scalar(qscale[:, :], par[:, 17:18], 0.125, None, ALU.mult))
                dve.wait_ge(zeroed_n.s, zeroed_n.at(l, 1))
                for i in range(4):
                    query_tile(i)
                    if i == 0:
                        dve.wait_ge(gexp_done.s, gexp_done.at(l, 1))
                    step(V.tensor_scalar(sg_exp[:, i, :], sg_exp[:, i, :], 1.0, None, ALU.add))
                    step(V.reciprocal(sg_exp[:, i, :], sg_exp[:, i, :]))
                    last = V.tensor_tensor(sg[:, i, :], sg[:, i, :], sg_exp[:, i, :], ALU.mult)
                last.then_inc(gate_done.s, 1)
                b = tile(("ada", 5))
                V.scalar_tensor_tensor(out=A1[:, :], in0=b[:, 0:8], scalar=1.0, in1=par[:, 8:16], op0=ALU.add,
                                       op1=ALU.mult).then_inc(dve_took.s, 1)
                for i in range(4):
                    b = tile(("o", i))
                    dve.wait_ge(rt_done.s, rt_done.at(l, 8 + i + 1))
                    V.scalar_tensor_tensor(out=cat[:, i, :], in0=b[:, :], scalar=par[:, 16:17], in1=rt[:, i % 2, :],
                                           op0=ALU.mult, op1=ALU.mult).then_inc(dve_took.s, 1)
                    dve.wait_ge(dve_took.s, dve_took.at(l, taken[("o", i)][1]))
                    last = V.tensor_tensor(cat[:, i, :], cat[:, i, :], sg[:, i, :], ALU.mult)
                last.then_inc(cat_g.s, 1)

                for h in range(9):
                    if h < 8:
                        dve.wait_ge(bm_done.s, bm_done.at(l, h + 1))
                        for cb in range(4):
                            if cb % 2 == 0:
                                b = tile(("S", h, cb // 2))
                                pass_on(dve)
                            last = V.tensor_tensor_reduce(
                                out=P_sb[:, h % 3, cb, :], in0=b[:, (cb % 2) * 256:(cb % 2 + 1) * 256],
                                in1=bm[:, h % 2, MASK_OF[cb], :], scale=1.0, scalar=3.0 * NEG,
                                op0=ALU.add, op1=ALU.max, accum_out=mx[:, h % 2, cb:cb + 1])
                            if cb % 2:
                                last.then_inc(dve_took.s, 1)
                        dve.wait_ge(dve_took.s, dve_took.at(l, taken[("S", h, 1)][1]))
                        V.tensor_scalar(nmx[:, h % 2, :], mx[:, h % 2, :], -1.0, None, ALU.mult
                                        ).then_inc(smax_done.s, 1)
                    if h >= 1:
                        g = h - 1
                        dve.wait_ge(sexp_done.s, sexp_done.at(l, g + 1))
                        step(V.reciprocal(rsm[:, g % 2, :], sm[:, g % 2, :]))
                        V.tensor_tensor(P_sb[:, g % 3, :, :], P_sb[:, g % 3, :, :], rep(rsm[:, g % 2, :], 256), ALU.mult
                                        ).then_inc(prob_done.s, 1)

                def add_y(m, tt):
                    b = tile(("y", m, tt))
                    cols = slice(m * 256, (m + 1) * 256)
                    tmp = pool_c[:, (tt % 2) * 256:(tt % 2 + 1) * 256]
                    V.tensor_tensor(tmp, b[:, 0:256], g1_bc[:, cols], ALU.mult).then_inc(dve_took.s, 1)
                    dve.wait_ge(dve_took.s, dve_took.at(l, taken[("y", m, tt)][1]))
                    last = V.tensor_tensor(x_sb[:, tt, cols], x_sb[:, tt, cols], tmp, ALU.add)
                    if m == 3:
                        last.then_inc(x_mid.s, 1)

                for m in range(3):
                    for tt in range(TT):
                        add_y(m, tt)
                add_y(3, 0), add_y(3, 1), add_y(3, 2)
                scaled(2, 0)
                shift_tile(2, 0)
                add_y(3, 3)
                scaled(2, 1), scaled(2, 2)
                shift_tile(2, 1)
                scaled(2, 3)
                shift_tile(2, 2), shift_tile(2, 3)

                def v4(a):
                    return a.rearrange("p (t g e) -> p (t g) e", g=NG, e=EG)
                score, sel, oh1, oh2, tmp, sel2 = (R[n] for n in ("score", "sel", "oh1", "oh2", "tmp", "sel2"))
                pick1, pick2, mask, rank, dst, ge, t2, t3 = (
                    R[n] for n in ("pick1", "pick2", "mask", "rank", "dst", "ge", "t2", "t3"))
                m1, m2, gs, mf, gh, q4 = (small[i][:, 0:16] for i in range(6))
                gm = small[6][:, 0:4]
                b = tile(("logits",))
                dve.wait_ge(route_exp.s, route_exp.at(l, 1))
                V.tensor_scalar(score, score, 1.0, None, ALU.add).then_inc(dve_took.s, 1)
                dve.wait_ge(dve_took.s, dve_took.at(l, taken[("logits",)][1]))
                step(V.reciprocal(score, score))
                step(V.tensor_tensor(sel.rearrange("p (t e) -> p t e", e=NE), score.rearrange("p (t e) -> p t e", e=NE),
                                     again(rb_sb[:, :], TT), ALU.add))

                def first_of(vals, best, n, order, out, scratch):
                    step(V.tensor_tensor(scratch, vals, rep(best, n), ALU.is_equal))
                    step(V.tensor_tensor(scratch, scratch, order, ALU.mult))
                    step(V.tensor_reduce(mf[:, 0:best.shape[1]], scratch, AX, ALU.max))
                    step(V.tensor_tensor(out, scratch, rep(mf[:, 0:best.shape[1]], n), ALU.is_equal))

                order8 = again(iota8[:, 0:EG], TT * NG)
                step(V.tensor_reduce(m1, v4(sel), AX, ALU.max))
                first_of(v4(sel), m1, EG, order8, v4(oh1), v4(tmp))
                step(V.scalar_tensor_tensor(out=sel2, in0=oh1, scalar=NEG, in1=sel, op0=ALU.mult, op1=ALU.add))
                step(V.tensor_reduce(m2, v4(sel2), AX, ALU.max))
                first_of(v4(sel2), m2, EG, order8, v4(oh2), v4(tmp))
                step(V.tensor_tensor(gs, m1, m2, ALU.add))
                gs_v = gs.rearrange("p (t g) -> p t g", g=NG)
                step(V.tensor_reduce(gm, gs_v, AX, ALU.max))
                first_of(gs_v, gm, NG, again(iota4[:, :], TT), gh.rearrange("p (t g) -> p t g", g=NG),
                         q4.rearrange("p (t g) -> p t g", g=NG))
                step(V.tensor_tensor(v4(pick1), v4(oh1), rep(gh, EG), ALU.mult))
                step(V.tensor_tensor(v4(pick2), v4(oh2), rep(gh, EG), ALU.mult))
                V.tensor_tensor(mask, pick1, pick2, ALU.add).then_inc(mask_done.s, 1)
                V.tensor_copy(pairs[:, 0:1], pairs_f[:, 0:1])
                def te(a):
                    return a.rearrange("p (t e) -> p t e", e=NE)
                for j, pk in enumerate((pick1, pick2)):
                    step(V.tensor_tensor(tmp, pk, score, ALU.mult))
                    step(V.tensor_reduce(gwt[:, j, :], te(tmp), AX, ALU.add))
                wsum = small[7][:, 0:4]
                step(V.tensor_tensor(wsum, gwt[:, 0, :], gwt[:, 1, :], ALU.add))
                step(V.reciprocal(wsum, wsum))
                step(V.tensor_tensor(gwt[:, :, :], gwt[:, :, :], again(wsum, 2), ALU.mult))
                b = tile(("rank",))
                step(V.tensor_copy(rank, b[:, 0:128]))
                cntT, cnt = small[8], small[9]
                step(V.tensor_copy(cnt, b[:, 128:160]))
                V.tensor_copy(cntT[0:NE, 0:1], b[0:NE, 160:161]).then_inc(dve_took.s, 1)
                dve.wait_ge(dve_took.s, dve_took.at(l, taken[("rank",)][1]))
                thr = small[10]
                step(V.tensor_scalar(thr[:, 0:7], iota_s[:, 1:8], 64.0, None, ALU.mult))
                novT, c7 = small[11], small[12]
                step(V.tensor_tensor(c7[0:NE, 0:7], rep(cntT[0:NE, 0], 7), thr[0:NE, 0:7], ALU.is_gt))
                step(V.tensor_reduce(novT[0:NE, 0:1], c7[0:NE, 0:7], AX, ALU.add))
                V.tensor_scalar(t3[0:NE, :], ones[0:NE, :], novT[0:NE, 0:1], None, ALU.mult).then_inc(over_in.s, 1)
                cmp7 = wide.rearrange("p b e -> p (b e)")[:, 0:NE * 7].rearrange("p (e m) -> p e m", m=7)
                step(V.tensor_tensor(cmp7, rep(cnt, 7), again(thr[:, 0:7], NE), ALU.is_gt))
                nov = small[13]
                step(V.tensor_reduce(nov, cmp7, AX, ALU.add))
                b = tile(("over",))
                before_e, total = small[14], small[15]
                step(V.tensor_copy(before_e, b[:, 0:NE]))
                V.tensor_copy(total[:, 0:1], b[:, NE:NE + 1]).then_inc(dve_took.s, 1)
                dve.wait_ge(dve_took.s, dve_took.at(l, taken[("over",)][1]))
                shift_e = small[18]
                step(V.tensor_scalar(shift_e, before_e, float(NE - 1), 64.0, ALU.add, ALU.mult))
                step(V.tensor_tensor(shift_e, shift_e, iota_e[:, :], ALU.subtract))
                step(V.tensor_scalar(ge, rank, float(SLOTS), None, ALU.is_ge))
                step(V.tensor_tensor(te(ge), te(ge), again(shift_e, TT), ALU.mult))
                step(V.tensor_tensor(dst, rank, ge, ALU.add))
                step(V.tensor_tensor(te(dst), te(dst), again(iota_e[:, :], TT), ALU.add))
                rowf = small[19][:, 0:8]
                for j, pk in enumerate((pick1, pick2)):
                    step(V.tensor_tensor(tmp, pk, dst, ALU.mult))
                    step(V.tensor_reduce(rowf[:, j * 4:(j + 1) * 4], te(tmp), AX, ALU.add))
                row_v = row_of[:, :, :].rearrange("p j t -> p (j t)")
                step(V.tensor_copy(row_v, rowf))
                ia, fa = (small[20][:, 0:8].bitcast(I32), small[21][:, 0:8])
                ib, fb = (small[22][:, 0:8].bitcast(I32), small[23][:, 0:8])
                step(V.tensor_scalar(ia, row_v, 6, None, ALU.arith_shift_right))
                step(V.tensor_scalar(ib, row_v, SLOTS - 1, None, ALU.bitwise_and))
                step(V.tensor_copy(fa, ia))
                step(V.tensor_copy(fb, ib))
                step(V.tensor_tensor(oslot, again(iota_s[:, :], 8), rep(fb, SLOTS), ALU.is_equal))
                step(V.tensor_tensor(oblk, again(iota_s[:, 0:NBLK], 8), rep(fa, NBLK), ALU.is_equal))
                V.tensor_tensor(oblk, oblk, rep(tok8[:, :], NBLK), ALU.mult).then_inc(slot1h.s, 1)
                b = tile(("slot",))
                V.tensor_copy(slot_tok[:, :], b[0:SLOTS, 0:NBLK]).then_inc(dve_took.s, 1)
                dve.wait_ge(dve_took.s, dve_took.at(l, taken[("slot",)][1]))
                dve.sem_inc(slots_set.s, 1)
                upto_e, ex = small[16], small[17]
                step(V.tensor_tensor(upto_e, before_e, nov, ALU.add))
                step(V.tensor_tensor(wide, again(upto_e, MAXOV), rep(iota_s[:, 0:MAXOV], NE), ALU.is_le))
                step(V.tensor_reduce(ex[:, 0:MAXOV], wide, AX, ALU.add))
                V.tensor_copy(blk_real[:, 0:NE], ones[:, 0:NE])
                V.tensor_scalar(blk_real[:, NE:NBLK], ex[:, 0:MAXOV], float(NE), None, ALU.is_lt)
                step(V.tensor_scalar(ex[:, 0:MAXOV], ex[:, 0:MAXOV], float(NE - 1), None, ALU.min))
                V.tensor_copy(blk_exp[:, 0:NE], iota_s[:, 0:NE])
                step(V.tensor_copy(blk_exp[:, NE:NBLK], ex[:, 0:MAXOV]))
                half_i, half_f = small[20][:, 0:1].bitcast(I32), small[21][:, 0:1]
                step(V.tensor_scalar(total[:, 1:2], total[:, 0:1], 1.0, None, ALU.add))
                step(V.tensor_copy(half_i, total[:, 1:2]))
                step(V.tensor_scalar(half_i, half_i, 1, None, ALU.arith_shift_right))
                step(V.tensor_copy(half_f, half_i))
                step(V.tensor_scalar(pairs[:, 1:2], half_f, float(NE // 2 - 1), None, ALU.add))
                step(V.scalar_tensor_tensor(out=pairs_f[:, 0:1], in0=half_f, scalar=float(NE // 2),
                                            in1=pairs_f[:, 0:1], op0=ALU.add, op1=ALU.add))
                dve.sem_inc(routed.s, 1)
                pairs0, more = reg_counts(dve)
                G0 = pairs0 * 2

                def own(ins, G, n):
                    ins.then_inc(dve_blk.s, 1)
                    dve.wait_ge(dve_blk.s, G * 4 + n)

                def modulate(u, G):
                    b = bank[u][:, :].rearrange("p (k s) -> p k s", k=KD)
                    dve.wait_ge(blk["xg_T"].s, blocks(G, 1))
                    dve.wait_ge(blk["up_ready"].s, blocks(G, -1))
                    own(V.tensor_tensor(hgT[:, u, :, :], b, rep(A2[:, :], SLOTS), ALU.mult), G, 1)
                    V.tensor_tensor(hgT[:, u, :, :], hgT[:, u, :, :], rep(B2[:, :], SLOTS), ALU.add
                                    ).then_inc(blk["hg_done"].s, 1)

                def silu(u, G):
                    dve.wait_ge(blk["up_exp"].s, blocks(G, 1))
                    e1 = sil[:, u, 0:256]
                    own(V.tensor_scalar(e1, e1, 1.0, None, ALU.add), G, 2)
                    own(V.reciprocal(e1, e1), G, 3)
                    own(V.tensor_tensor(e1, bank[2 + u][:, 0:256], e1, ALU.mult), G, 4)
                    V.tensor_tensor(sil[:, u, 256:512], e1, bank[2 + u][:, 256:512], ALU.mult
                                    ).then_inc(blk["g_done"].s, 1)

                def gate_y(u, G, pair):
                    dve.wait_ge(blk["y_ready"].s, blocks(G, 1))
                    dve.wait_ge(y_stored[u].s, pair * 32 + 32)
                    for nh in range(2):
                        rows = slice(64 * nh, 64 * nh + 64)
                        last = V.tensor_tensor(y_sb[rows, u, :], bank[6 + u][rows, :],
                                               g2_bc[rows, nh * 512:(nh + 1) * 512], ALU.mult)
                    last.then_inc(blk["y_evac"].s, 1)

                modulate(0, G0)
                silu(0, G0)
                modulate(1, G0 + 1)
                with dve.Fori(0, more) as i:
                    G, pair = G0 + i * 2, pairs0 + i
                    silu(1, G + 1)
                    modulate(0, G + 2)
                    gate_y(0, G, pair)
                    silu(0, G + 2)
                    modulate(1, G + 3)
                    gate_y(1, G + 1, pair)
                G, pair = G0 + more * 2, pairs0 + more
                silu(1, G + 1)
                gate_y(0, G, pair)
                gate_y(1, G + 1, pair)

                for tt in range(TT):
                    dve.wait_ge(yrows_in[tt].s, yrows_in[tt].at(l, 32))
                    x = x_sb[:, tt, :]
                    step(V.scalar_tensor_tensor(out=x, in0=yg[tt][:, 0, :], scalar=gwt[:, 0, tt:tt + 1], in1=x,
                                                op0=ALU.mult, op1=ALU.add))
                    V.scalar_tensor_tensor(out=x, in0=yg[tt][:, 1, :], scalar=gwt[:, 1, tt:tt + 1], in1=x,
                                           op0=ALU.mult, op1=ALU.add).then_inc(x_new.s, 1)
            assert steps[0] == DVE_STEPS, steps

        @block.gpsimd
        def _(pool):
            G_ = nc.gpsimd
            n0 = [0]

            def link0(ins):
                n0[0] += 1
                ins.then_inc(pstep.s, 1)
                pool.wait_ge(pstep.s, n0[0])

            G_.memset(pool_b[:, 4608:5120], 0.0).then_inc(bias_zero.s, 1)
            G_.memset(zeros_y, 0.0).then_inc(y_zeros.s, 1)
            for t_ in (ident, upto, since, after, before):
                last = G_.memset(t_[:, :], 0.0 if t_ is ident else 1.0)
            link0(last)
            for t_, op, fill, cm, st_, base in ((ident, ALU.not_equal, 1.0, 1, -1, 0),
                                                (upto, ALU.is_ge, 0.0, -1, 1, 0),
                                                (since, ALU.is_ge, 0.0, 1, -1, 0),
                                                (after, ALU.is_gt, 0.0, 1, -1, 0),
                                                (before, ALU.is_gt, 0.0, -1, 1, 0)):
                last = G_.affine_select(out=t_[:, :], in_=t_[:, :], compare_op=op, fill=fill, base=base,
                                        pattern=[[st_, P]], channel_multiplier=cm)
            link0(last)
            G_.iota(io_p[:, :], pattern=[[0, P]], base=0, channel_multiplier=1)
            G_.iota(io_f[:, :], pattern=[[1, P]], base=0, channel_multiplier=0)
            G_.iota(io_8[:, :], pattern=[[-1, EG]], base=EG, channel_multiplier=0)
            link0(G_.iota(io_t[:, :], pattern=[[0, 2], [P, TT]], base=0, channel_multiplier=1))
            link0(G_.iota(io_e[:, :], pattern=[[SLOTS, NE]], base=0, channel_multiplier=0))
            G_.tensor_copy(iota_s[:, :], io_f[:, 0:64])
            G_.tensor_copy(iota8[:, 0:EG], io_8[:, :])
            G_.tensor_copy(iota4[:, :], io_8[:, 4:8])
            G_.tensor_copy(tok8[:, :], io_t[:, :])
            link0(G_.tensor_copy(iota_e[:, :], io_e[:, :]))
            pool.sem_inc(consts_p.s, 1)

            with pool.Fori(0, L) as l:
                pool.wait_ge(x_new.s, l * TT + TT)
                pass_on(pool)
                for half in range(2):
                    rows = slice(64 * (1 - half), 64 * (1 - half) + 64)
                    G_.memset(qz[rows, half, :], 0.0)
                    last = G_.memset(qz_l[rows, half * 1024:(half + 1) * 1024], 0.0)
                last.then_inc(zeroed_q.s, 1)
                pool.wait_ge(zeroed_q.s, zeroed_q.at(l, 1))
                pool.wait_ge(y_zeroed.s, 16)
                pool.wait_ge(act_took.s, act_took.at(l, taken[("b", 1, 1)][1]))
                for n, lev in enumerate(LEVELS):
                    if n >= 2:
                        pool.wait_ge(tile_ready.s, tile_ready.at(l, index[("P", LEVELS[n - 2], TT - 1)] + 1))
                    hh = 1 << lev
                    e = k_lev[n % 2].rearrange("p (n a h) -> p n a h", a=2, h=hh)
                    f, g = (bT[:, r, :].rearrange("p (n a h) -> p n a h", a=2, h=hh) for r in range(2))
                    G_.tensor_tensor(e[:, :, 0, :], rep(f[:, :, 0, hh - 1], hh), f[:, :, 0, :], ALU.subtract)
                    G_.tensor_tensor(e[:, :, 1, :], rep(g[:, :, 1, 0], hh), g[:, :, 1, :], ALU.subtract
                                     ).then_inc(diff_k.s, 1)
                    pool.wait_ge(exp_k.s, exp_k.at(l, n + 1))
                    if n == 0:
                        pool.wait_ge(tile_ready.s, tile_ready.at(l, index[("U", 1, 1)] + 1))
                        pass_on(pool)
                        for half in range(2):
                            rows = slice(64 * (1 - half), 64 * (1 - half) + 64)
                            last = G_.memset(q_lev[1][rows, half * 1024:(half + 1) * 1024], 0.0)
                        last.then_inc(zeroed_l.s, 1)
                        pool.wait_ge(zeroed_l.s, zeroed_l.at(l, 1))
                    G_.tensor_tensor(k_lev[n % 2], k_lev[n % 2], kT, ALU.mult).then_inc(lev_k.s, 1)
                pool.wait_ge(tile_ready.s, tile_ready.at(l, index[("P", 0, TT - 1)] + 1))
                pass_on(pool)
                for half in range(2):
                    rows = slice(64 * (1 - half), 64 * (1 - half) + 64)
                    last = G_.memset(qnz[rows, :, half, :], 0.0)
                last.then_inc(zeroed_n.s, 1)
                pool.wait_ge(zeroed_n.s, zeroed_n.at(l, 1))
                pool.wait_ge(gtab_in.s, gtab_in.at(l, 16 * 8))
                pool.wait_ge(gate_done.s, gate_done.at(l, 1))
                for h in range(8):
                    if h >= 2:
                        pool.wait_ge(smax_done.s, smax_done.at(l, h - 1))
                    for m in range(3):
                        src = ap_of(gtab[:, h, :], RPB_PAD - 8 * m, [[1, 32], [31, ROWS]])
                        last = G_.tensor_tensor(bm[:, h % 2, m, :].rearrange("p (c r) -> p c r", r=ROWS), src,
                                                rep(wneg[:, m, :], ROWS), ALU.add)
                    last.then_inc(bm_done.s, 1)

                pool.wait_ge(bm_done.s, bm_done.at(l, 8))
                pool.wait_ge(slots_set.s, slots_set.at(l, 1))
                for i in range(2):
                    pool.wait_ge(xn_stored[i].s, xn_stored[i].at(l, 32))
                pass_on(pool)
                pairs0 = pool.value_load(pairs[0:1, 0:1], min_val=0, max_val=L * NBLK // 2)
                G0 = pairs0 * 2

                def gather(u, G, row):
                    pool.wait_ge(blk["xg_T"].s, blocks(G, -1))
                    pass_on(pool)
                    G_.tensor_copy(tok_now[:, u:u + 1], slot_tok[:, bass.ds(row, 1)]).then_inc(tok_set.s, 1)
                    pool.wait_ge(tok_set.s, G + 1)
                    pass_on(pool)
                    G_.indirect_dma_start(xg[:, u, :], None, xn_dram, bass.IndirectOffsetOnAxis(tok_now[:, u:u + 1], 0)
                                          ).then_inc(gathered[u].s, 16)

                for u in range(2):
                    gather(u, G0 + u, u)
                pool.wait_ge(routed.s, routed.at(l, 1))
                pass_on(pool)
                more = pool.value_load(pairs[0:1, 1:2], min_val=NE // 2 - 1, max_val=NBLK // 2 - 1)
                G_.memset(pool_b[:, 4608:5120], 0.0).then_inc(bias_zero.s, 1)
                with pool.Fori(0, more) as i:
                    for u in range(2):
                        gather(u, G0 + i * 2 + (2 + u), i * 2 + (2 + u))
                for u in range(2):
                    pool.wait_ge(y_stored[u].s, pairs0 * 32 + more * 32 + 64)
                pass_on(pool)
                for tt in range(TT):
                    for j in range(2):
                        G_.indirect_dma_start(yg[tt][:, j, :], None, y_dram,
                                              bass.IndirectOffsetOnAxis(row_of[:, j, tt:tt + 1], 0)
                                              ).then_inc(yrows_in[tt].s, 16)

_INS = ["x", "c", "w_ada", "b_ada", "attn_norm", "ffn_norm", "w_in", "gla_gate_w", "gla_gate_b", "gla_out_norm",
        "na_q_norm", "na_k_norm", "na_rpb", "w_out", "router_w", "router_b", "w1", "w3", "w2"]

def kernel(**inputs):
    import numpy as np
    import concourse.bacc as bacc
    from concourse.bass_utils import run_bass_kernel_spmd

    nc = bacc.Bacc("TRN2", target_bir_lowering=False, num_devices=1)
    arrays, aps = {}, {}
    for name in _INS:
        a = np.ascontiguousarray(inputs[name])
        arrays[name] = a
        aps[name] = nc.dram_tensor(name, a.shape, mybir.dt.from_np(a.dtype), kind="ExternalInput").ap()
    aps["out"] = nc.dram_tensor("out", (1, T, D), F32, kind="ExternalOutput").ap()
    build(nc, aps)
    r = run_bass_kernel_spmd(nc, [arrays], core_ids=[0])
    return r.results[0]["out"]
```
